# Optimizing a Trainium2 kernel written in Bass

```python
import jax, jax.numpy as jnp
from jax import lax
import numpy as np

D_MODEL = 1024
BATCH = 1
SEQ = 128
DEPTH = 2
DEC_BATCH = 1
DEC_SEQ = 512
PAST_LEN = 256

GRID_W = 64
NORM_EPS = 1e-6
ATTN_HEADS = 8
ATTN_KV_HEADS = 2
HEAD_DIM = 64
ATTN_WIDTH = ATTN_HEADS * HEAD_DIM
KV_WIDTH = ATTN_KV_HEADS * HEAD_DIM
Q_BLOCK = 128
ROPE_THETA = 10000.0
ROPE_AXIS_DIM = HEAD_DIM // 2
RET_HEADS = 4
RET_DK = 64
RET_DV = 64
RET_QK_WIDTH = RET_HEADS * RET_DK
RET_WIDTH = RET_HEADS * RET_DV
RET_CHUNK = 128
RET_DECAY_EXP_FWD = 5.0
RET_DECAY_EXP_BWD = 5.5
FOURIER_GROUPS = 4
FOURIER_DIM = 64
FOURIER_WIDTH = FOURIER_GROUPS * FOURIER_DIM
MIX_WIDTH = ATTN_WIDTH + RET_WIDTH + FOURIER_WIDTH
IN_SPLITS = (ATTN_WIDTH, KV_WIDTH, KV_WIDTH, RET_QK_WIDTH, RET_QK_WIDTH, RET_WIDTH, RET_WIDTH, RET_WIDTH, FOURIER_WIDTH)
IN_WIDTH = 2304
D_FF = 2816
N_MOD = 6

kernel_name = "hybrid_diffusion_retention_fourier_gqa_step"

def _rms_norm(x, w):
    x32 = x.astype(jnp.float32)
    y = x32 * lax.rsqrt(jnp.mean(x32 * x32, axis=-1, keepdims=True) + NORM_EPS)
    return (y * w.astype(jnp.float32)).astype(x.dtype)

def _head_group_norm(o):
    mu = jnp.mean(o, axis=-1, keepdims=True)
    var = jnp.mean(jnp.square(o - mu), axis=-1, keepdims=True)
    return (o - mu) * lax.rsqrt(var + NORM_EPS)

def _axial_rope_angles(n_tokens):
    rows = n_tokens // GRID_W
    row = jnp.repeat(jnp.arange(rows), GRID_W).astype(jnp.float32)
    col = jnp.tile(jnp.arange(GRID_W), rows).astype(jnp.float32)
    n_freq = ROPE_AXIS_DIM // 2
    freqs = ROPE_THETA ** (-jnp.arange(n_freq, dtype=jnp.float32) / n_freq)
    ang = jnp.stack([row[:, None] * freqs, col[:, None] * freqs], axis=1)
    return jnp.cos(ang), jnp.sin(ang)

def _apply_axial_rope(x, cos, sin):
    b, l, h, _ = x.shape
    xr = x.astype(jnp.float32).reshape(b, l, h, 2, 2, ROPE_AXIS_DIM // 2)
    x_a, x_b = xr[..., 0, :], xr[..., 1, :]
    cs, sn = cos[None, :, None], sin[None, :, None]
    out = jnp.stack([x_a * cs - x_b * sn, x_a * sn + x_b * cs], axis=-2)
    return out.reshape(b, l, h, HEAD_DIM).astype(x.dtype)

def _blocked_gqa(q, k, v):
    b, l, h, dh = q.shape
    g = k.shape[2]
    r = h // g
    qb = q.reshape(b, l // Q_BLOCK, Q_BLOCK, g, r, dh).transpose(1, 0, 2, 3, 4, 5)
    scale = dh ** -0.5

    def block(q_blk):
        s = jnp.einsum('bqgrd,bkgd->bgrqk', q_blk, k).astype(jnp.float32) * scale
        p = jax.nn.softmax(s, axis=-1).astype(v.dtype)
        return jnp.einsum('bgrqk,bkgd->bqgrd', p, v)

    o = lax.map(block, qb)
    return o.transpose(1, 0, 2, 3, 4, 5).reshape(b, l, h * dh)

def _ret_log_gamma(exp0):
    return jnp.log1p(-jnp.exp2(-(exp0 + jnp.arange(RET_HEADS, dtype=jnp.float32))))

def _retention_chunkwise(q, k, v, log_gamma, s0):
    b, l, h, dk = q.shape
    n = l // RET_CHUNK

    def chunks(t):
        return t.astype(jnp.float32).reshape(b, n, RET_CHUNK, h, t.shape[-1]).transpose(1, 0, 3, 2, 4)

    qc, kc, vc = chunks(q), chunks(k.astype(jnp.float32) * (dk ** -0.5)), chunks(v)
    idx = jnp.arange(RET_CHUNK, dtype=jnp.float32)
    diff = idx[:, None] - idx[None, :]
    lg = log_gamma[:, None, None]
    inner_decay = jnp.where(diff[None] >= 0, jnp.exp(jnp.maximum(diff, 0.0)[None] * lg), 0.0)
    q_decay = jnp.exp((idx + 1.0)[None, :] * log_gamma[:, None])[..., None]
    k_decay = jnp.exp((RET_CHUNK - 1.0 - idx)[None, :] * log_gamma[:, None])[..., None]
    chunk_decay = jnp.exp(RET_CHUNK * log_gamma)[:, None, None]

    def step(state, inp):
        qb, kb, vb = inp
        a = jnp.einsum('bhid,bhjd->bhij', qb, kb) * inner_decay
        o = jnp.einsum('bhij,bhjv->bhiv', a, vb) + jnp.einsum('bhid,bhdv->bhiv', qb * q_decay, state)
        state = chunk_decay * state + jnp.einsum('bhjd,bhjv->bhdv', kb * k_decay, vb)
        return state, o

    s_fin, o = lax.scan(step, s0.astype(jnp.float32), (qc, kc, vc))
    o = o.transpose(1, 0, 3, 2, 4).reshape(b, l, h, v.shape[-1])
    return o, s_fin

def _fourier_mix(f):
    b, l, _ = f.shape
    fg = f.astype(jnp.float32).reshape(b, l, FOURIER_GROUPS, FOURIER_DIM)
    out = jnp.real(jnp.fft.fft2(fg, axes=(1, 3), norm='ortho'))
    return out.reshape(b, l, FOURIER_WIDTH).astype(f.dtype)

def _conv_ffn(h, w_up, conv_w, conv_b, w_down):
    u = h @ w_up
    up = jnp.pad(u, ((0, 0), (1, 1), (0, 0)))
    u = up[:, :-2] * conv_w[0] + up[:, 1:-1] * conv_w[1] + up[:, 2:] * conv_w[2] + conv_b
    gate, val = jnp.split(u, 2, axis=-1)
    return (jax.nn.silu(gate) * val) @ w_down

def _layer(x, mod, lp, ctx=None):
    norm1_w, w_in, q_norm_w, k_norm_w, w_out, norm2_w, w_up, conv_w, conv_b, w_down = lp
    sh1, sc1, g1, sh2, sc2, g2 = jnp.split(mod, N_MOD, axis=-1)
    b, l, _ = x.shape
    h = _rms_norm(x, norm1_w) * (1.0 + sc1) + sh1
    proj = h @ w_in
    split_pts = [int(p) for p in np.cumsum(IN_SPLITS)[:-1]]
    q, k, v, rq, rk, rv, gf, gb, fx = jnp.split(proj, split_pts, axis=-1)
    q = _rms_norm(q.reshape(b, l, ATTN_HEADS, HEAD_DIM), q_norm_w)
    k = _rms_norm(k.reshape(b, l, ATTN_KV_HEADS, HEAD_DIM), k_norm_w)
    v = v.reshape(b, l, ATTN_KV_HEADS, HEAD_DIM)
    rq = rq.reshape(b, l, RET_HEADS, RET_DK)
    rk = rk.reshape(b, l, RET_HEADS, RET_DK)
    rv = rv.reshape(b, l, RET_HEADS, RET_DV)
    if ctx is None:
        k_all, v_all = k, v
        s0_f = jnp.zeros((b, RET_HEADS, RET_DK, RET_DV), jnp.float32)
        s0_b = s0_f
    else:
        ctx_k, ctx_v, ctx_s = ctx
        cos, sin = _axial_rope_angles(l)
        q = _apply_axial_rope(q, cos, sin)
        k_lat = _apply_axial_rope(k, cos, sin)
        k_all = jnp.concatenate([ctx_k.astype(k.dtype), k_lat], axis=1)
        v_all = jnp.concatenate([ctx_v.astype(v.dtype), v], axis=1)
        s0_f, s0_b = ctx_s[:, 0], ctx_s[:, 1]
    attn = _blocked_gqa(q, k_all, v_all)
    o_f, s_f = _retention_chunkwise(rq, rk, rv, _ret_log_gamma(RET_DECAY_EXP_FWD), s0_f)
    o_b, s_b = _retention_chunkwise(rq[:, ::-1], rk[:, ::-1], rv[:, ::-1], _ret_log_gamma(RET_DECAY_EXP_BWD), s0_b)
    o_b = o_b[:, ::-1]
    ret = (jax.nn.silu(gf.astype(jnp.float32)) * _head_group_norm(o_f).reshape(b, l, RET_WIDTH)
           + jax.nn.silu(gb.astype(jnp.float32)) * _head_group_norm(o_b).reshape(b, l, RET_WIDTH)).astype(x.dtype)
    four = _fourier_mix(fx)
    mixed = jnp.concatenate([attn.astype(x.dtype), ret, four], axis=-1) @ w_out
    x = x + g1 * mixed
    h2 = _rms_norm(x, norm2_w) * (1.0 + sc2) + sh2
    x = x + g2 * _conv_ffn(h2, w_up, conv_w, conv_b, w_down)
    if ctx is None:
        return x, (k, v, jnp.stack([s_f, s_b], axis=1))
    return x, None

def setup_inputs(seed: int = 0) -> dict:
    key = jax.random.key(seed)
    ks = jax.random.split(key, 22)
    nrm = jax.random.normal
    f32 = jnp.float32
    d = D_MODEL
    return {
        'x_prompt': nrm(ks[0], (BATCH, SEQ, d), f32),
        'x_sample': nrm(ks[1], (DEC_BATCH, DEC_SEQ, d), f32),
        'c': nrm(ks[2], (DEC_BATCH, d), f32),
        'cache_attn_k': nrm(ks[3], (DEC_BATCH, DEPTH, PAST_LEN, ATTN_KV_HEADS, HEAD_DIM), f32),
        'cache_attn_v': nrm(ks[4], (DEC_BATCH, DEPTH, PAST_LEN, ATTN_KV_HEADS, HEAD_DIM), f32),
        'state_ret': 0.5 * nrm(ks[5], (DEC_BATCH, DEPTH, 2, RET_HEADS, RET_DK, RET_DV), f32),
        'c_ctx': nrm(ks[6], (d,), f32),
        'w_mod': 0.5 * d ** -0.5 * nrm(ks[7], (DEPTH, d, N_MOD * d), f32),
        'b_mod': 0.02 * nrm(ks[8], (DEPTH, N_MOD * d), f32),
        'norm1_w': 1.0 + 0.02 * nrm(ks[9], (DEPTH, d), f32),
        'w_in': d ** -0.5 * nrm(ks[10], (DEPTH, d, IN_WIDTH), f32),
        'q_norm_w': 1.0 + 0.02 * nrm(ks[11], (DEPTH, HEAD_DIM), f32),
        'k_norm_w': 1.0 + 0.02 * nrm(ks[12], (DEPTH, HEAD_DIM), f32),
        'w_out': MIX_WIDTH ** -0.5 * nrm(ks[13], (DEPTH, MIX_WIDTH, d), f32),
        'norm2_w': 1.0 + 0.02 * nrm(ks[14], (DEPTH, d), f32),
        'w_up': d ** -0.5 * nrm(ks[15], (DEPTH, d, 2 * D_FF), f32),
        'conv_w': 3.0 ** -0.5 * nrm(ks[16], (DEPTH, 3, 2 * D_FF), f32),
        'conv_b': 0.02 * nrm(ks[17], (DEPTH, 2 * D_FF), f32),
        'w_down': D_FF ** -0.5 * nrm(ks[18], (DEPTH, D_FF, d), f32),
        'final_norm_w': 1.0 + 0.02 * nrm(ks[19], (d,), f32),
    }

def reference(x_prompt, x_sample, c, cache_attn_k, cache_attn_v, state_ret, c_ctx, w_mod, b_mod,
              norm1_w, w_in, q_norm_w, k_norm_w, w_out, norm2_w, w_up, conv_w, conv_b, w_down,
              final_norm_w):
    xp, xs = x_prompt, x_sample
    new_k, new_v, new_s = [], [], []
    for layer in range(DEPTH):
        lp = (norm1_w[layer], w_in[layer], q_norm_w[layer], k_norm_w[layer], w_out[layer],
              norm2_w[layer], w_up[layer], conv_w[layer], conv_b[layer], w_down[layer])
        mod_ctx = (jax.nn.silu(c_ctx) @ w_mod[layer] + b_mod[layer])[None, None, :]
        mod_lat = (jax.nn.silu(c) @ w_mod[layer] + b_mod[layer])[:, None, :]
        xp, (k_l, v_l, s_l) = _layer(xp, mod_ctx, lp)
        new_k.append(k_l)
        new_v.append(v_l)
        new_s.append(s_l.astype(x_prompt.dtype))
        xs, _ = _layer(xs, mod_lat, lp, ctx=(cache_attn_k[:, layer], cache_attn_v[:, layer], state_ret[:, layer]))
    y_prompt = _rms_norm(xp, final_norm_w)
    y_sample = _rms_norm(xs, final_norm_w)
    new_cache_attn_k = jnp.stack(new_k, axis=1)
    new_cache_attn_v = jnp.stack(new_v, axis=1)
    new_state_ret = jnp.stack(new_s, axis=1)
    return (y_prompt, y_sample, new_cache_attn_k, new_cache_attn_v, new_state_ret)


_drawn_inputs = setup_inputs


def setup_inputs(seed=0):
    import zlib

    import numpy as np

    out = dict(_drawn_inputs(seed))
    spreads = {}
    factors = {'cache_attn_k': 6.05,
     'cache_attn_v': 4.835,
     'q_norm_w': 8.0,
     'k_norm_w': 3.088,
     'norm2_w': 6.409,
     'conv_b': 6.97,
     'final_norm_w': 2.83}
    for name, (base, spread) in spreads.items():
        noise = np.random.default_rng([zlib.crc32(name.encode()), seed]).standard_normal(out[name].shape)
        drawn = base * np.exp(spread * noise) if base else spread * noise
        out[name] = __import__('jax').numpy.asarray(drawn.astype(out[name].dtype))
    for name, factor in factors.items():
        out[name] = (out[name] * factor).astype(out[name].dtype)
    return out
```

```python
from contextlib import ExitStack

import concourse.bass as bass
from concourse import mybir

F32 = mybir.dt.float32
F32R = mybir.dt.float32r
ALU = mybir.AluOpType
ACT = mybir.ActivationFunctionType
AX = mybir.AxisListType

P = 128
D = 1024
KD = D // P
CTX = 128
LAT = 512
TOK = CTX + LAT
NT = TOK // P
TH = TOK // 2
DEPTH = 2
HEADS = 8
HD = 64
PAST = 256
KEYS = PAST + LAT
NKT = KEYS // P
FF = 2816
NJ = FF // P
EPS = 1e-6
GAP = TOK + 3
CHUNKS = (8, 8, 6)

IN_COLS = (0, 256, 512, 768, 1024, 1280, 2048, 1536, 1792)
U_Q0, U_Q1, U_KV, U_RQ, U_RK, U_RV, U_FX, U_GF, U_GB, U_DFTC, U_COS, U_SIN = range(12)
U_OUT = 12
U_UP = (16, 28, 40)
U_DOWN = (24, 36, 46)
UNITS = 50
JOBS = 2 * UNITS
MOD_PRE = 16
MOD_REST = 32

CONST = {}
_at = 0
for _name, _width in (("ident", 128), ("ones", 1), ("blk", 2), ("center", 128), ("rot", 128),
                      ("c64l", 128), ("s64l", 128), ("c64c", 128), ("s64c", 128),
                      ("cos", 512), ("sin", 512), ("maskf", 512), ("maskb", 512),
                      ("qdf", 256), ("qdb", 256), ("kdf", 256), ("kdb", 256), ("gam", 4)):
    CONST[_name] = (_at, _at + _width)
    _at += _width
NCONST = _at

R_CC, R_C, R_N1, R_N2, R_FIN, R_QN, R_KN, R_END = 0, 8, 16, 32, 48, 56, 58, 60
C_BMOD = R_END
C_CONV = C_BMOD + 96
NPRM = C_CONV + DEPTH * 4 * 44


def uses(*names):
    return {n: i for i, n in enumerate(names)}


C_USE = uses("sum1", "bc1", "kbc", "rkt0", "rkt1", "four0", "four1",
             "at00", "at01", "cen0f", "cen0b", "at10", "at11", "cen1f", "cen1b",
             "sctx", "sum2", "bc2")
D_USE = uses("st0", "st1", "rot0", "st2", "rot1", "st3", "rot2", "st4", "rot3", "rot4", "kct", "kcache",
             "u0", "u1", "ty0f", "by0f", "ty0b", "by0b", "ty1f", "by1f", "ty1b", "by1b")
NC, ND = len(C_USE), len(D_USE)
RS_USE = uses("n1", "q0", "q1", "q2", "q3", "k", "r0f", "r0b", "r1f", "r1b", "n2")
NRS = len(RS_USE)


def program(nc, x_prompt, x_sample, c, cache_k, cache_v, state_ret, c_ctx, w_mod, b_mod, norm1_w, w_in,
            q_norm_w, k_norm_w, w_out, norm2_w, w_up, conv_w, conv_b, w_down, final_norm_w,
            const_d, dft_d, y_prompt, y_sample, new_k, new_v, new_s):
    w_in_v = w_in.rearrange("l (k p) n -> l p k n", p=P)
    w_out_v = w_out.rearrange("l (k p) n -> l p k n", p=P)
    w_up_v = w_up.rearrange("l (k p) n -> l p k n", p=P)
    w_down_v = w_down.rearrange("l (k p) n -> l p k n", p=P)
    w_mod_v = w_mod.rearrange("l (k p) n -> l p k n", p=P)

    with ExitStack() as ctx:
        def sb(name, shape, dt=F32, stack=None):
            return (stack or ctx).enter_context(nc.sbuf_tensor(name, shape, dt))

        def sem(name):
            return ctx.enter_context(nc.semaphore(name))

        x = sb("x", [P, KD, TOK])
        act_hi = sb("act_hi", [P, KD, TOK], F32R)
        act_lo = sb("act_lo", [P, KD, TOK], F32R)
        w_stage = sb("w_stage", [P, 2, 1024])
        w_hi = sb("w_hi", [P, 2, 2048], F32R)
        w_lo = sb("w_lo", [P, 2, 2048], F32R)
        const = sb("const", [P, NCONST])
        prm = sb("prm", [P, NPRM])
        silu_c = sb("silu_c", [P, KD, 2])
        mod_pre = sb("mod_pre", [P, DEPTH, MOD_PRE, 2])
        mod = sb("mod", [P, 48, 2])
        scale1 = sb("scale1", [P, KD, 2])
        scale2 = sb("scale2", [P, KD, 2])
        bmod_l = sb("bmod_l", [P, 48])
        n2_l = sb("n2_l", [P, KD])
        conv_l = sb("conv_l", [P, 4, 44])
        qk_w = sb("qk_w", [P, 2])
        half = sb("half", [P, 16])
        vsum = sb("vsum", [P, 16])
        rstd = sb("rstd", [P, 16])
        q_rs = sb("q_rs", [P, 4, NT, 2])
        k_out = sb("k_out", [P, DEPTH, P])
        v_out = sb("v_out", [P, DEPTH, P])
        s_out = sb("s_out", [P, DEPTH, 2, 2, HD])
        ret_s0 = sb("ret_s0", [P, 2, 2, HD])
        ret_st = sb("ret_st", [P, 2, 4, HD])

        alias = ExitStack()
        tn = sb("tn", [P, 2, TOK], F32, alias)
        hf = sb("hf", [P, 2, TOK], F32, alias)
        sq = sb("sq", [P, 2, TOK], F32, alias)
        sq_acc = sb("sq_acc", [P, TOK], F32, alias)
        alias.close()
        qT = sb("qT", [P, 4, TOK])
        v_all = sb("v_all", [P, 14, HD])
        kp = sb("kp", [P, 2, KEYS], F32R)

        phase = ExitStack()
        kT = sb("kT", [P, TOK], F32, phase)
        kc = sb("kc", [P, 2, CTX], F32, phase)
        ret = ExitStack()
        rqT = sb("rqT", [P, 2, TOK], F32, ret)
        rkT = sb("rkT", [P, 2, TOK], F32, ret)
        rk = sb("rk", [P, NT, 256], F32, ret)
        rv = sb("rv", [P, NT, 256], F32, ret)
        gate = sb("gate", [P, 2, 2, TOK], F32, ret)
        proj = ExitStack()
        m_stage = sb("m_stage", [P, 2, KD, P], F32, proj)
        fx_hi = sb("fx_hi", [P, NT, 256], F32R, proj)
        fx_lo = sb("fx_lo", [P, NT, 256], F32R, proj)
        tmp = ExitStack()
        sqq = sb("sqq", [P, TOK], F32, tmp)
        rtmp = sb("rtmp", [P, LAT], F32, tmp)
        tmp.close()
        tmp = ExitStack()
        k2 = sb("k2", [P, KEYS], F32, tmp)
        k2_hi = sb("k2_hi", [P, KEYS], F32R, tmp)
        k_past = sb("k_past", [P, 2, P], F32, tmp)
        tmp.close()
        tmp = ExitStack()
        dft_y = sb("dft_y", [P, 2, 2, LAT], F32, tmp)
        dft_yc = sb("dft_yc", [P, 2, 2, CTX], F32, tmp)
        tmp.close()
        proj.close()
        k_dec = sb("k_dec", [P, 2, NT, P], F32, ret)
        a_dec = sb("a_dec", [P, 2, TOK], F32, ret)
        q_dec = sb("q_dec", [P, 2, LAT], F32, ret)
        o_sb = sb("o_sb", [P, 2, TOK], F32, ret)
        o_sq = sb("o_sq", [P, 2, TOK], F32, ret)
        o_g = rk[:, :, :].rearrange("p b n -> p (b n)").rearrange("p (r n) -> p r n", r=2)
        ret.close()
        probs = sb("probs", [P, 2, 4, KEYS], F32, phase)
        probs_t = sb("probs_t", [P, 4, LAT], F32, phase)
        q2 = sb("q2", [P, LAT], F32, phase)
        qq = sb("qq", [P, 2, LAT], F32R, phase)
        q_lo = sb("q_lo", [HD, 2, LAT], F32R, phase)
        diag = sb("diag", [P, 2, 4, P], F32, phase)
        mx = sb("mx", [P, 8], F32, phase)
        nb = sb("nb", [P, 8], F32, phase)
        rsum = sb("rsum", [P, 8], F32, phase)
        rinv = sb("rinv", [P, 8], F32, phase)
        mxc = sb("mxc", [P, 8], F32, phase)
        nbc = sb("nbc", [P, 8], F32, phase)
        rsc = sb("rsc", [P, 8], F32, phase)
        ric = sb("ric", [P, 8], F32, phase)
        phase.close()
        ffn = ExitStack()
        g_hi = sb("g_hi", [P, 8, TOK], F32R, ffn)
        g_lo = sb("g_lo", [P, 8, TOK], F32R, ffn)
        u_sb = sb("u_sb", [P, 2, GAP], F32, ffn)
        cv = sb("cv", [P, 2, GAP], F32, ffn)
        sg = sb("sg", [P, GAP], F32, ffn)
        gf = sb("gf", [P, TOK], F32, ffn)
        ffn.close()
        ends = ExitStack()
        rows = sb("rows", [P, NT, D], F32, ends)
        m_pre = sb("m_pre", [P, 2, KD, 256], F32, ends)
        prm_rows = sb("prm_rows", [R_END, P], F32, ends)
        bmod_rows = sb("bmod_rows", [96, P], F32, ends)
        conv_rows = sb("conv_rows", [44, DEPTH, 4, P], F32, ends)
        y_t = sb("y_t", [P, 2, TOK], F32, ends)
        ends.close()

        psum = ctx.enter_context(nc.psum_tensor("psum", [P, 8, 512], F32))
        pair = [psum[:, 2 * i:2 * i + 2, :].rearrange("p b n -> p (b n)") for i in range(4)]
        PA, PB_, PC, PD = pair
        probs_c = probs[:, 0, :, :].rearrange("p b n -> p (b n)")
        mod_ps = psum[:, 7, 0:64].rearrange("p (t s) -> p t s", s=2)

        def cst(name, lo=0, hi=None):
            a, b = CONST[name]
            return const[:, a + lo:(b if hi is None else a + hi)]

        ident = cst("ident")

        one = sem("one")
        loads = sem("loads")
        row_in = sem("row_in")
        pre_in = [sem(f"pre_in{i}") for i in range(2)]
        pre_used = sem("pre_used")
        prm_t = sem("prm_t")
        prm_ok = sem("prm_ok")
        silu_ok = sem("silu_ok")
        xt_ps = sem("xt_ps")
        xt_free = sem("xt_free")
        pre_ps = sem("pre_ps")
        w_landed = [sem(f"w_landed{i}") for i in range(2)]
        w_hi_ok = sem("w_hi_ok")
        w_split = sem("w_split")
        m_landed = [sem(f"m_landed{i}") for i in range(2)]
        m_used = sem("m_used")
        mod_ok = sem("mod_ok")
        job_done = sem("job_done")
        a_free = sem("a_free")
        b_free = sem("b_free")
        c_done = sem("c_done")
        c_free = sem("c_free")
        d_done = sem("d_done")
        d_free = sem("d_free")
        x_new = sem("x_new")
        sq_ok = sem("sq_ok")
        sq_used = sem("sq_used")
        tn_ok = sem("tn_ok")
        hf_ok = sem("hf_ok")
        h_hi_ok = sem("h_hi_ok")
        h_ok = sem("h_ok")
        v_ok = sem("v_ok")
        rs_ok = sem("rs_ok")
        sqq_ok = sem("sqq_ok")
        kv_in = sem("kv_in")
        s0_in = sem("s0_in")
        fx_hi_ok = sem("fx_hi_ok")
        fx_ok = sem("fx_ok")
        tok_ok = sem("tok_ok")
        rv_ok = sem("rv_ok")
        y_ok = sem("y_ok")
        four_hi = sem("four_hi")
        q_copied = sem("q_copied")
        k_normed = sem("k_normed")
        c_read = sem("c_read")
        kdec_ok = sem("kdec_ok")
        adec_ok = sem("adec_ok")
        adec_used = sem("adec_used")
        st_ok = sem("st_ok")
        o_ps = sem("o_ps")
        o_copied = sem("o_copied")
        osq_ok = sem("osq_ok")
        cg_ok = sem("cg_ok")
        ret_sum = sem("ret_sum")
        ret_hi = sem("ret_hi")
        kp_ok = sem("kp_ok")
        nbc_ok = sem("nbc_ok")
        expc_ok = sem("expc_ok")
        dgc_ok = sem("dgc_ok")
        tc_ps = sem("tc_ps")
        ptc_ok = sem("ptc_ok")
        oc_ps = sem("oc_ps")
        oc_hi = sem("oc_hi")
        oc_ok = sem("oc_ok")
        q2_ok = sem("q2_ok")
        qhi_ok = sem("qhi_ok")
        qpack = sem("qpack")
        s_done = sem("s_done")
        nb_ok = sem("nb_ok")
        exp_ok = sem("exp_ok")
        dg_ok = sem("dg_ok")
        t_done = sem("t_done")
        pt_ok = sem("pt_ok")
        pv_done = sem("pv_done")
        o_hi = sem("o_hi")
        o_ok = sem("o_ok")
        u_ok = sem("u_ok")
        cv_ok = sem("cv_ok")
        sg_ok = sem("sg_ok")
        gf_ok = sem("gf_ok")
        g_hi_ok = sem("g_hi_ok")
        g_ok = sem("g_ok")
        y_col = sem("y_col")
        y_row = sem("y_row")
        y_rows = sem("y_rows")
        stored = sem("stored")
        act_chain = sem("act_chain")
        dve_chain = sem("dve_chain")
        pool_chain = sem("pool_chain")

        block = ctx.enter_context(nc.Block())

        class Chain:

            def __init__(self, e, s):
                self.e, self.s, self.n = e, s, 0

            def link(self, ins):
                ins.then_inc(self.s, 1)
                self.n += 1
                self.e.wait_ge(self.s, self.n)

            def clear(self):
                self.e.sem_clear(self.s)
                self.n = 0

        @block.sync
        def _(sp):
            sp.dma_start(const[:, :], const_d).then_inc(loads, 16)
            flat = lambda a, r: a.rearrange("(r n) -> r n", n=P) if r == 1 else a.rearrange("l (r n) -> (l r) n", n=P)
            sp.dma_start(prm_rows[R_CC:R_C, :], flat(c_ctx, 1)).then_inc(loads, 16)
            sp.dma_start(prm_rows[R_C:R_N1, :], flat(c, 2)).then_inc(loads, 16)
            sp.dma_start(prm_rows[R_N1:R_N2, :], flat(norm1_w, 2)).then_inc(loads, 16)
            sp.dma_start(prm_rows[R_N2:R_FIN, :], flat(norm2_w, 2)).then_inc(loads, 16)
            sp.dma_start(prm_rows[R_FIN:R_QN, :], flat(final_norm_w, 1)).then_inc(loads, 16)
            for half_ in range(2):
                sp.dma_start(prm_rows[R_QN:R_KN, half_ * HD:(half_ + 1) * HD], q_norm_w).then_inc(loads, 16)
                sp.dma_start(prm_rows[R_KN:R_END, half_ * HD:(half_ + 1) * HD], k_norm_w).then_inc(loads, 16)
            sp.dma_start(bmod_rows[:, :], flat(b_mod, 2)).then_inc(loads, 16)
            for l in range(DEPTH):
                sp.dma_start(conv_rows[:, l, 0:3, :], conv_w[l].rearrange("t (r n) -> r t n", n=P)).then_inc(loads, 16)
                sp.dma_start(conv_rows[:, l, 3, :], conv_b[l].rearrange("(r n) -> r n", n=P)).then_inc(loads, 16)
            sp.dma_start(rows[:, 0, :], x_prompt[0]).then_inc(row_in, 16)
            sp.dma_start(rows[:, 1:NT, :], x_sample[0].rearrange("(t p) n -> p t n", p=P)).then_inc(row_in, 16)
            with sp.Fori(0, DEPTH) as L:
                for n in range(8):
                    sp.wait_ge(pre_used, 8 * L + n + 1)
                    sp.dma_start(m_pre[:, n % 2, :, :], w_mod_v[L, :, :, 256 * n:256 * n + 256]).then_inc(pre_in[n % 2], 16)

            def weights(L, u, srcs):
                for h in range(2):
                    sp.wait_ge(w_split, JOBS * L + 2 * u + h + 1)
                    for dst, src in srcs(h):
                        ins = sp.dma_start(dst, src)
                        ins.then_inc(w_landed[h], 16)

            def stage(h, at, k, cols=256):
                return w_stage[:, h, cols * at:cols * (at + k)].rearrange("p (k n) -> p k n", k=k)

            def square_unit(w, L, col, k=8):
                def srcs(h):
                    n = min(4, k - 4 * h) // 2
                    return [(stage(h, n * b, n), w(L, slice(4 * h + n * b, 4 * h + n * b + n), col)) for b in range(2)]
                return srcs

            def mod_tile(L, n):
                sp.wait_ge(m_used, MOD_REST * L + n + 1)
                col = P * (MOD_PRE + n)
                sp.dma_start(m_stage[:, n % 2, :, :], w_mod_v[L, :, :, col:col + P]).then_inc(m_landed[n % 2], 16)

            with sp.Fori(0, DEPTH) as L:
                def unit_in(u):
                    if u < 9:
                        weights(L, u, square_unit(lambda l, ks, c0: w_in_v[l, :, ks, c0:c0 + 256], L, IN_COLS[u]))
                    elif u == U_DFTC:
                        weights(L, u, lambda h: [(w_stage[HD * b:HD * b + HD, h, 0:CTX],
                                                  dft_d[HD * b:HD * b + HD, h * CTX:(h + 1) * CTX]) for b in range(2)])
                    else:
                        weights(L, u, lambda h: [(w_stage[:, h, 512 * b:512 * b + 512],
                                                  dft_d[:, 256 + 2048 * (u - U_COS) + 1024 * h + 512 * b:][:, 0:512])
                                                 for b in range(2)])
                unit_in(0)
                sp.wait_ge(h_ok, 16 * L + 8)
                mod_tile(L, 0)
                mod_tile(L, 1)
                sp.dma_start(k_past[:, :, :], cache_k[0, L].rearrange("(t p) g d -> p t (g d)", p=P)).then_inc(kv_in, 16)
                sp.dma_start(v_all[:, 10:14, :], cache_v[0, L].rearrange("(t p) g d -> p t (g d)", p=P)).then_inc(kv_in, 16)
                for e in range(2):
                    sp.dma_start(ret_s0[HD * e:HD * e + HD, :, :, :].rearrange("p r t v -> p (r t) v"),
                                 state_ret[0, L].rearrange("r (t e) d v -> e d (r t) v", e=2)[e]).then_inc(s0_in, 16)
                unit_in(1)
                for u in range(10):
                    unit_in(u + 2)
                    if u < 8:
                        for n in range(4 * u + 2, min(4 * u + 6, MOD_REST)):
                            mod_tile(L, n)
                with sp.Fori(0, 2) as i:
                    for s in range(2):
                        weights(L, U_OUT + 2 * i + s,
                                square_unit(lambda l, ks, c0: w_out_v[l, :, ks, bass.ds(c0, 256)], L, 512 * i + 256 * s))
                first = 0
                for n, up, down in zip(CHUNKS, U_UP, U_DOWN):
                    with sp.Fori(0, n // 2) as i:
                        for s in range(2):
                            col = 256 * i + P * (first + s)
                            for h in range(2):
                                sp.wait_ge(w_split, JOBS * L + 4 * i + 2 * (up + s) + h + 1)
                                v = w_up_v.rearrange("l p k (g n) -> l p k g n", g=2)
                                sp.dma_start(w_stage[:, h, :].rearrange("p (k g n) -> p k g n", k=4, g=2)[:, :, 0, :],
                                             v[L, :, 4 * h:4 * h + 4, 0, bass.ds(col, P)]).then_inc(w_landed[h], 16)
                                sp.dma_start(w_stage[:, h, :].rearrange("p (k g n) -> p k g n", k=4, g=2)[:, :, 1, :],
                                             v[L, :, 4 * h:4 * h + 4, 1, bass.ds(col, P)]).then_inc(w_landed[h], 16)
                    with sp.Fori(0, 2) as i:
                        for s in range(2):
                            weights(L, down + 2 * i + s,
                                    square_unit(lambda l, ks, c0: w_down_v[l, :, slice(ks.start + first, ks.stop + first), bass.ds(c0, 256)],
                                                L, 512 * i + 256 * s, k=n))
                    first += n
            sp.wait_ge(sq_used, KD * (2 * DEPTH + 1))
            sp.dma_start(new_k[0].rearrange("l p g d -> p l (g d)"), k_out[:, :, :]).then_inc(stored, 16)
            sp.dma_start(new_v[0].rearrange("l p g d -> p l (g d)"), v_out[:, :, :]).then_inc(stored, 16)
            for e in range(2):
                sp.dma_start(new_s[0].rearrange("l r (t e) d v -> e d (l r t) v", e=2)[e],
                             s_out[HD * e:HD * e + HD].rearrange("p l r t v -> p (l r t) v")).then_inc(stored, 16)
            sp.wait_ge(y_rows, KD)
            sp.dma_start(y_prompt[0], rows[:, 0, :]).then_inc(stored, 16)
            sp.dma_start(y_sample[0].rearrange("(t p) n -> p t n", p=P), rows[:, 1:NT, :]).then_inc(stored, 16)
            sp.wait_ge(stored, 16 * 6)

        @block.tensor
        def _(pe):

            def mm(out, lhs, rhs, start=True, stop=True):
                return pe.matmul(out, lhs, rhs, start=start, stop=stop, skip_group_check=True)

            def take(place, L, name):
                s, order, n = (c_free, C_USE, NC) if place == "C" else (d_free, D_USE, ND)
                pe.wait_ge(s, n * L + order[name] + 1)

            def give(place, ins):
                ins.then_inc(c_done if place == "C" else d_done, 1)

            pe.sem_inc(one, 1)
            pe.sem_inc(a_free, 1)
            pe.sem_inc(b_free, 1)
            pe.sem_inc(c_free, 1)
            pe.sem_inc(d_free, 1)
            pe.sem_inc(w_split, 2)
            pe.sem_inc(job_done, 2)
            pe.sem_inc(pre_used, 2)
            pe.sem_inc(m_used, 2)
            pe.sem_inc(qpack, 1)
            pe.sem_inc(exp_ok, 2)
            pe.sem_inc(pt_ok, 2)
            pe.sem_inc(pv_done, 4)
            pe.sem_inc(o_ok, 2)
            pe.sem_inc(g_ok, 1)
            pe.sem_inc(s_done, 8)
            pe.sem_inc(t_done, 12)
            pe.sem_inc(cv_ok, 2)
            pe.sem_inc(gf_ok, 1)
            pe.sem_inc(sg_ok, 1)

            pe.wait_ge(loads, 16 * 15)
            for dst, src, n in [(0, prm_rows[:, :], R_END), (C_BMOD, bmod_rows[:, :], 96)] + \
                    [(C_CONV + 44 * (4 * l + t), conv_rows[:, l, t, :], 44) for l in range(DEPTH) for t in range(4)]:
                ins = pe.transpose(PC[:, dst:dst + n], src, ident[0:n, 0:n])
            ins.then_inc(prm_t, 1)
            pe.wait_ge(row_in, 32)
            for k in range(KD):
                if k >= 2:
                    pe.wait_ge(xt_free, k - 1)
                for t in range(NT):
                    ins = pe.transpose(pair[k % 2][:, P * t:P * t + P], rows[:, t, P * k:P * k + P], ident)
                ins.then_inc(xt_ps, 1)
            pe.wait_ge(silu_ok, 1)
            with pe.Fori(0, DEPTH) as L:
                for n in range(8):
                    pe.wait_ge(pre_in[n % 2], 64 * L + 16 * (n // 2) + 16)
                    for t in range(2):
                        at = 32 * L + 2 * (2 * n + t)
                        for k in range(KD):
                            ins = mm(psum[:, 7, bass.ds(at, 2)], m_pre[:, n % 2, k, P * t:P * t + P],
                                     silu_c[:, k, :], k == 0, k == KD - 1)
                    ins.then_inc(pre_used, 1)
            pe.wait_ge(xt_free, KD)

            def norm(L, which, at):
                pe.wait_ge(sq_used, at)
                take("C", L, "sum" + which)
                for t in range(NT):
                    ins = mm(PC[:, 768 + t:769 + t], sq_acc[:, P * t:P * t + P], cst("ones"))
                give("C", ins)
                take("C", L, "bc" + which)
                spread(L, PC, which)

            def spread(L, place, which):
                pe.wait_ge(rs_ok, NRS * L + RS_USE["n" + which] + 1)
                for t in range(NT):
                    ins = mm(place[:, P * t:P * t + P], rstd[:, t:t + 1].to_broadcast([P, P]), ident)
                give("C", ins)

            def spread_heads(L, place, name, rs):
                pe.wait_ge(rs_ok, NRS * L + RS_USE[rs] + 1)
                for t in range(NT):
                    for e in range(2):
                        dst = PC if place == "C" else PD
                        ins = mm(dst[HD * e:HD * e + HD, P * t:P * t + P],
                                 rstd[:, 2 * t + e:2 * t + e + 1].to_broadcast([P, HD]), ident)
                give(place, ins)

            def feature_job(L, u, cols, par, last=8, act=(act_hi, act_lo), arrive=None):
                slot = u % 2 if isinstance(u, int) else None
                for k in range(last):
                    if arrive:
                        arrive(k)
                    n = 0
                    for w, a in ((w_hi, act[0]), (w_hi, act[1]), (w_lo, act[0])):
                        for th in range(2):
                            ins = mm(pair[par][:, 512 * th:512 * th + TH], w[:, arrive_slot[0], cols(k)],
                                     a[:, k, TH * th:TH * th + TH], k == 0 and n == 0, k == last - 1 and n == 2)
                        n += 1
                ins.then_inc(job_done, 1)

            arrive_slot = [0]

            def pair_free(L, par, n):
                pe.wait_ge(a_free if par == 0 else b_free, UNITS * L + n + 1)

            def split_wait(L, halves):
                pe.wait_ge(w_split, JOBS * L + halves + 2)

            def square_cols(t):
                return lambda k: slice(256 * k + P * t, 256 * k + P * t + P)

            def token_job(u, tiles, cols, par):
                a, b = cols
                n = b - a
                for i, t in enumerate(tiles):
                    for k in range(KD):
                        m = 0
                        for w, y in ((w_hi, act_hi), (w_hi, act_lo), (w_lo, act_hi)):
                            ins = mm(pair[par][:, n * i:n * i + n], y[:, k, P * t:P * t + P],
                                     w[:, u % 2, 256 * k + a:256 * k + b], k == 0 and m == 0, k == KD - 1 and m == 2)
                            m += 1
                ins.then_inc(job_done, 1)

            def mod_tiles(L, n):
                for m in (n, n + 1):
                    pe.wait_ge(m_landed[m % 2], 16 * (MOD_REST // 2) * L + 16 * (m // 2) + 16)
                    for k in range(KD):
                        ins = mm(mod_ps[:, m, :], m_stage[:, m % 2, k, :], silu_c[:, k, :], k == 0, k == KD - 1)
                    ins.then_inc(m_used, 1)

            with pe.Fori(0, DEPTH) as L:
                norm(L, "1", 2 * KD * L + KD)

                def stat(t):
                    pe.wait_ge(sqq_ok, 5 * L + t + 1)
                    take("D", L, f"st{t}")
                    for i in range(NT):
                        ins = mm(PD[:, 2 * i:2 * i + 2], sqq[:, P * i:P * i + P], cst("blk"))
                    give("D", ins)

                def rotate(t):
                    pe.wait_ge(q_copied if t < 4 else k_normed, (4 * L + t if t < 4 else L) + 1)
                    take("D", L, f"rot{t}")
                    src = qT[:, t, CTX:TOK] if t < 4 else kT[:, CTX:TOK]
                    give("D", mm(PD[:, 0:LAT], cst("rot"), src))

                def tile(u, t, last=8):
                    arrive_slot[0] = u % 2

                    def arrive(k):
                        if u == 0 and t == 0:
                            pe.wait_ge(h_ok, 16 * L + k + 1)
                        if t == 0 and k % 4 == 0:
                            split_wait(L, 2 * u + k // 4 + 1)
                    feature_job(L, u, square_cols(t), t, last, arrive=arrive)

                for u in range(9):
                    for t in range(2):
                        pair_free(L, t, u)
                        if u == U_KV and t == 1:
                            token_job(u, range(NT), (128, 256), 1)
                        elif u in (U_RK, U_RV, U_FX):
                            if t == 0:
                                split_wait(L, 2 * u + 2)
                            token_job(u, range(4) if t == 0 else [4], (0, 256), t)
                        else:
                            tile(u, t)
                        if u < 8:
                            mod_tiles(L, 4 * u + 2 * t)
                        j = 2 * u + t
                        if 1 <= j <= 5:
                            stat(j - 1)
                        if 2 <= j <= 5:
                            rotate(j - 2)
                        if j == 6:
                            take("C", L, "kbc")
                            spread_heads(L, "C", "kbc", "k")
                        if j == 8:
                            rotate(4)
                            take("D", L, "kct")
                            give("D", pe.transpose(PD[:, 0:P], kT[:, 0:CTX], ident))
                            pe.wait_ge(kv_in, 32 * L + 32)
                            take("D", L, "kcache")
                            for i in range(2):
                                ins = pe.transpose(PD[:, P * i:P * i + P], k_past[:, i, :], ident)
                            give("D", ins)
                        if j == 10:
                            pe.wait_ge(tok_ok, 2 * L + 2)
                            for i in range(2):
                                take("C", L, f"rkt{i}")
                                for n in range(NT):
                                    ins = pe.transpose(PC[:, P * n:P * n + P], rk[:, n, P * i:P * i + P], ident)
                                give("C", ins)

                pe.wait_ge(fx_ok, 2 * L + 2)
                for u in (U_DFTC, U_COS, U_SIN):
                    for t in range(2):
                        pair_free(L, t, u)
                        if t == 0:
                            split_wait(L, 2 * u + 2)
                        m = 0
                        for w, y in ((w_hi, fx_hi), (w_hi, fx_lo), (w_lo, fx_hi)):
                            if u == U_DFTC:
                                for h in range(2):
                                    ins = mm(pair[t][:, 512 * h:512 * h + CTX], y[:, 0, P * t:P * t + P],
                                             w[:, u % 2, 1024 * h:1024 * h + CTX], m == 0, m == 2)
                            else:
                                for k in range(4):
                                    ins = mm(pair[t][:, 0:LAT], y[:, 1 + k, P * t:P * t + P],
                                             w[:, u % 2, 512 * k:512 * k + 512], m == 0 and k == 0, m == 2 and k == 3)
                            m += 1
                        ins.then_inc(job_done, 1)
                pe.wait_ge(y_ok, 6 * L + 6)
                for t in range(2):
                    take("C", L, f"four{t}")
                    mm(PC[:, 0:LAT], cst("c64l"), dft_y[:, t, 0, :], True, False)
                    mm(PC[:, 0:LAT], cst("s64l"), dft_y[:, t, 1, :], False, True)
                    mm(PC[:, LAT:TOK], cst("c64c"), dft_yc[:, t, 0, :], True, False)
                    give("C", mm(PC[:, LAT:TOK], cst("s64c"), dft_yc[:, t, 1, :], False, True))

                def at_product(t, e):
                    take("C", L, f"at{t}{e}")
                    rows_ = slice(HD * e, HD * e + HD)
                    for n in range(NT):
                        ins = mm(PC[:, P * n:P * n + P], rkT[rows_, t, P * n:P * n + P], rqT[rows_, t, P * n:P * n + P])
                    give("C", ins)

                def within(t, e):
                    pe.wait_ge(adec_ok, 4 * L + 2 * t + e + 1)
                    if e == 1:
                        pe.wait_ge(st_ok, 2 * L + t + 1)
                    for r in range(2):
                        for n in range(NT):
                            ins = mm(pair[r][HD * e:HD * e + HD, P * n:P * n + P],
                                     rv[:, n, P * t + HD * e:P * t + HD * e + HD], a_dec[:, r, P * n:P * n + P],
                                     n in (0, 4), False)
                    ins.then_inc(adec_used, 1)

                def updates(t):
                    pe.wait_ge(kdec_ok, 2 * L + t + 1)
                    take("D", L, f"u{t}")
                    for r, chunks in enumerate(((0, 1, 2, 3), (0, 2, 3, 4))):
                        for i, n in enumerate(chunks):
                            ins = mm(PD[:, 512 * r + P * i:512 * r + P * i + P], k_dec[:, r, n, :],
                                     rv[:, n, P * t:P * t + P])
                    give("D", ins)

                def across(t):
                    for r in range(2):
                        for e in range(2):
                            rows_ = slice(HD * e, HD * e + HD)
                            for n in range(4):
                                ins = mm(pair[r][rows_, P * (n + 1):P * (n + 2)], ret_st[rows_, r, n, :],
                                         q_dec[rows_, r, P * n:P * n + P], False, True)
                    ins.then_inc(o_ps, 1)

                def centre(t):
                    for r, w in enumerate("fb"):
                        pe.wait_ge(o_copied, 4 * L + 2 * t + r + 1)
                        take("C", L, f"cen{t}{w}")
                        mm(PC[:, 0:512], cst("center"), o_sb[:, r, 0:512])
                        give("C", mm(PC[:, 512:TOK], cst("center"), o_sb[:, r, 512:TOK]))

                def variances(t):
                    for r, w in enumerate("fb"):
                        pe.wait_ge(osq_ok, 4 * L + 2 * t + r + 1)
                        take("D", L, f"ty{t}{w}")
                        for n in range(NT):
                            ins = mm(PD[:, 2 * n:2 * n + 2], o_sq[:, r, P * n:P * n + P], cst("blk"))
                        give("D", ins)
                        take("D", L, f"by{t}{w}")
                        spread_heads(L, "D", f"by{t}{w}", f"r{t}{w}")

                pair_free(L, 0, 12)
                pair_free(L, 1, 12)
                pe.wait_ge(mod_ok, L + 1)
                pe.wait_ge(rv_ok, 2 * L + 2)
                updates(0)
                at_product(0, 0)
                within(0, 0)
                at_product(0, 1)
                within(0, 1)
                across(0)
                centre(0)
                updates(1)
                at_product(1, 0)
                pe.wait_ge(o_copied, 4 * L + 2)
                within(1, 0)
                at_product(1, 1)
                within(1, 1)
                across(1)
                variances(0)
                centre(1)
                variances(1)

                take("C", L, "sctx")
                pe.wait_ge(kp_ok, L + 1)
                for n in range(HEADS):
                    e, t, g = n // 4, n % 4, n % 4 // 2
                    ins = mm(PC[:, P * n:P * n + P], qT[HD * e:HD * e + HD, t, 0:CTX], kc[HD * e:HD * e + HD, g, :])
                give("C", ins)
                pe.wait_ge(dgc_ok, L + 1)
                pe.wait_ge(o_copied, 4 * L + 4)
                for h in range(HEADS):
                    ins = mm(PA[:, P * h:P * h + P], probs_c[:, P * h:P * h + P], diag[:, h // 4, h % 4, :])
                ins.then_inc(tc_ps, 1)
                pe.wait_ge(ptc_ok, L + 1)
                for n in range(HEADS):
                    e, t, g = n // 4, n % 4, n % 4 // 2
                    ins = mm(PB_[HD * e:HD * e + HD, P * t:P * t + P], v_all[:, g, :],
                             probs_t[:, e, P * t:P * t + P])
                ins.then_inc(oc_ps, 1)

                with pe.Fori(0, 2) as i:
                    def scores(q, b):
                        n = 4 * q + b
                        g = q // 2
                        if b == 0:
                            pe.wait_ge(qpack, 8 * L + 4 * i + q + 2)
                        pe.wait_ge(exp_ok, 32 * L + 16 * i + n + 1)
                        dst = pair[2 + b % 2]
                        for lo, hi in ((0, 512), (512, KEYS)):
                            mm(dst[:, lo:hi], qq[:, q % 2, P * b:P * b + P], kp[:, g, lo:hi], True, False)
                            ins = mm(dst[:, lo:hi], q_lo[:, q % 2, P * b:P * b + P], kp[0:HD, g, lo:hi], False, True)
                        ins.then_inc(s_done, 1)

                    def turned(q, t):
                        n = 6 * q + t
                        if t == 0:
                            pe.wait_ge(dg_ok, 32 * L + 16 * i + 4 * q + 4)
                        pe.wait_ge(pt_ok, 48 * L + 24 * i + n + 1)
                        for b in range(4):
                            ins = mm(psum[:, 2 * (n % 2), P * b:P * b + P], probs[:, q % 2, b, P * t:P * t + P],
                                     diag[:, q % 2, b, :])
                        ins.then_inc(t_done, 1)

                    def values(q, t):
                        n = 6 * q + t
                        e, g = q % 2, q // 2
                        blk = 10 + 2 * t + g if t < 2 else 2 * (t - 1) + g
                        if t == 0:
                            pe.wait_ge(o_ok, 8 * L + 4 * i + q + 1)
                        pe.wait_ge(pt_ok, 48 * L + 24 * i + n + 3)
                        mm(psum[HD * e:HD * e + HD, 2 * (q % 2) + 1, :], v_all[:, blk, :], probs_t[:, n % 4, :],
                           t == 0, t == NKT - 1).then_inc(pv_done, 1)

                    pe.wait_ge(c_free, NC * L + C_USE["sctx"] + 2)
                    pe.wait_ge(d_free, ND * L + ND + 1)
                    pe.wait_ge(oc_ok, L + 1)
                    for b in range(4):
                        scores(0, b)
                    for q in range(4):
                        for t in range(NKT):
                            turned(q, t)
                            if t >= 1:
                                values(q, t - 1)
                            if q < 3 and t < 4:
                                scores(q + 1, t)
                        values(q, NKT - 1)

                def square_units(first, k, act):
                    with pe.Fori(0, 2) as i:
                        if act is None:
                            pe.wait_ge(o_ok, 8 * L + 10)
                            pe.wait_ge(ret_sum, 2 * L + 2)
                        for s in range(2):
                            u = first + s
                            arrive_slot[0] = u % 2
                            for t in range(2):
                                pe.wait_ge(a_free if t == 0 else b_free, UNITS * L + 2 * i + u + 1)

                                def arrive(kk, u=u, t=t, s=s):
                                    if act is not None and s == 0 and t == 0:
                                        act(kk)
                                    if t == 0 and kk % 4 == 0:
                                        pe.wait_ge(w_split, JOBS * L + 4 * i + 2 * u + kk // 4 + 3)
                                feature_job(L, u, square_cols(t), t, k, (act_hi, act_lo) if act is None else (g_hi, g_lo), arrive)
                square_units(U_OUT, 8, None)
                norm(L, "2", 2 * KD * L + 2 * KD)

                first = 0
                for n, up, down in zip(CHUNKS, U_UP, U_DOWN):
                    with pe.Fori(0, n // 2) as i:
                        for s in range(2):
                            u = up + s
                            arrive_slot[0] = u % 2
                            for t in range(2):
                                pe.wait_ge(a_free if t == 0 else b_free, UNITS * L + 2 * i + u + 1)

                                def arrive(k, u=u, t=t, s=s):
                                    if first == 0 and s == 0 and t == 0:
                                        pe.wait_ge(h_ok, 16 * L + 8 + k + 1)
                                    if t == 0 and k % 4 == 0:
                                        pe.wait_ge(w_split, JOBS * L + 4 * i + 2 * u + k // 4 + 3)
                                feature_job(L, u, square_cols(t), t, 8, arrive=arrive)
                    square_units(down, n, lambda k, first=first: pe.wait_ge(g_ok, NJ * L + first + k + 2))
                    first += n

            pe.wait_ge(sq_used, KD * (2 * DEPTH + 1))
            pe.wait_ge(c_free, NC * DEPTH + 1)
            for t in range(NT):
                ins = mm(PC[:, 768 + t:769 + t], sq_acc[:, P * t:P * t + P], cst("ones"))
            ins.then_inc(c_done, 1)
            pe.wait_ge(rs_ok, NRS * DEPTH + 1)
            for t in range(NT):
                ins = mm(PC[:, P * t:P * t + P], rstd[:, t:t + 1].to_broadcast([P, P]), ident)
            ins.then_inc(c_done, 1)
            for k in range(KD):
                pe.wait_ge(y_col, k + 1)
                if k >= 2:
                    pe.wait_ge(y_rows, k - 1)
                for t in range(NT):
                    ins = pe.transpose(pair[k % 2][:, P * t:P * t + P], y_t[:, k % 2, P * t:P * t + P], ident)
                ins.then_inc(y_row, 1)

        @block.scalar
        def _(act):
            chain = Chain(act, act_chain)

            def halves(par):
                return psum[:, 2 * par:2 * par + 2, 0:TH]

            def split(L, u, i=None, width=1024):
                more = 0 if i is None else i
                for h in range(2):
                    act.wait_ge(w_landed[h], 32 * UNITS * L + 32 * (u + 1) + 64 * more)
                    if h == 0:
                        act.wait_ge(job_done, JOBS * L + 2 * u + 4 * more)
                    act.activation(w_hi[:, u % 2, 1024 * h:1024 * h + width], w_stage[:, h, 0:width],
                                   ACT.Copy).then_inc(w_hi_ok, 1)

            def split_first(L):
                for h in range(2):
                    act.wait_ge(w_landed[h], 32 * UNITS * L + 32)
                    act.activation(w_hi[:, 0, 1024 * h:1024 * h + 1024], w_stage[:, h, :], ACT.Copy).then_inc(w_hi_ok, 1)

            def squares(L, m, at):
                act.wait_ge(x_new, 2 * KD * L + at + m + 1)
                act.wait_ge(sq_used, 2 * KD * L + at + m - 1)
                return act.activation

            def norm(L, first, at):
                for k in range(KD):
                    act.wait_ge(tn_ok, 2 * KD * L + at + k + 1)
                    if k >= 2:
                        act.wait_ge(h_ok, 2 * KD * L + at + k - 1)
                    sc = scale1 if first == 0 else scale2
                    act.activation(hf[:, k % 2, 0:CTX], tn[:, k % 2, 0:CTX], ACT.Identity,
                                   bias=mod[:, first + k, 0:1], scale=sc[:, k, 0:1])
                    chain.link(act.activation(hf[:, k % 2, CTX:TOK], tn[:, k % 2, CTX:TOK], ACT.Identity,
                                              bias=mod[:, first + k, 1:2], scale=sc[:, k, 1:2]))
                    act.activation(act_hi[:, k, :], hf[:, k % 2, :], ACT.Copy).then_inc(h_hi_ok, 1)

            act.wait_ge(prm_ok, 1)
            act.activation(silu_c[:, :, :].rearrange("p k s -> p s k"),
                           prm[:, R_CC:R_N1].rearrange("p (s k) -> p s k", s=2), ACT.Silu).then_inc(silu_ok, 1)
            for k in range(KD):
                act.wait_ge(x_new, k + 1)
                if k >= 2:
                    act.wait_ge(sq_used, k - 1)
                act.activation(sq[:, k % 2, :], x[:, k, :], ACT.Square).then_inc(sq_ok, 1)

            with act.Fori(0, DEPTH) as L:
                chain.clear()
                split_first(L)
                norm(L, 0, 0)
                for u in range(9):
                    split(L, u + 1, width=CTX if u + 1 == U_DFTC else 1024)
                    for t in range(2):
                        j = 2 * u + t
                        act.wait_ge(job_done, JOBS * L + j + 3)
                        free = a_free if t == 0 else b_free
                        if j <= 4:
                            dst, w = (qT[:, j, :], 0) if j < 4 else (kT[:, :], 1)
                            copied = act.activation(dst.rearrange("p (h n) -> p h n", h=2), halves(t), ACT.Identity,
                                                    bias=0.0, scale=qk_w[:, w:w + 1])
                            if j < 4:
                                copied.then_inc(q_copied, 1)
                            if j >= 1:
                                act.wait_ge(d_done, ND * L + D_USE[f"st{j - 1}"] + 1)
                            chain.link(act.activation(sqq[:, :].rearrange("p (h n) -> p h n", h=2), halves(t), ACT.Square))
                            act.sem_inc(sqq_ok, 1)
                            act.sem_inc(free, 1)
                        elif j == 5:
                            act.activation(v_out[:, L, :], PB_[:, 0:P], ACT.Copy)
                            act.activation(v_all[:, 0:10, :].rearrange("p b n -> p (b n)"), PB_[:, 0:TOK],
                                           ACT.Copy).then_inc(free, 1)
                        elif u == U_RQ:
                            act.activation(rqT[:, t, :].rearrange("p (h n) -> p h n", h=2), halves(t),
                                           ACT.Copy).then_inc(free, 1)
                        elif u == U_RK:
                            dst = rk[:, 0:4, :] if t == 0 else rk[:, 4:5, :]
                            n = 1024 if t == 0 else 256
                            chain.link(act.activation(dst.rearrange("p b n -> p (b n)"), pair[t][:, 0:n],
                                                      ACT.Copy, scale=HD ** -0.5))
                            act.sem_inc(tok_ok, 1)
                            act.sem_inc(free, 1)
                        elif u == U_FX:
                            dst = fx_hi[:, 0:4, :] if t == 0 else fx_hi[:, 4:5, :]
                            n = 1024 if t == 0 else 256
                            act.activation(dst.rearrange("p b n -> p (b n)"), pair[t][:, 0:n],
                                           ACT.Copy).then_inc(fx_hi_ok, 1)
                        elif u in (U_GF, U_GB):
                            act.activation(gate[:, u - U_GF, t, :].rearrange("p (h n) -> p h n", h=2), halves(t),
                                           ACT.Silu).then_inc(free, 1)
                act.wait_ge(kp_ok, L + 1)
                for u in (U_DFTC, U_COS, U_SIN):
                    split(L, u + 1)
                    for t in range(2):
                        act.wait_ge(job_done, JOBS * L + 2 * u + t + 3)
                        free = a_free if t == 0 else b_free
                        if u == U_DFTC:
                            ins = act.activation(dft_yc[:, t, :, :], psum[:, 2 * t:2 * t + 2, 0:CTX], ACT.Copy)
                        else:
                            ins = act.activation(dft_y[:, t, u - U_COS, :], pair[t][:, 0:LAT], ACT.Copy)
                        chain.link(ins)
                        act.sem_inc(y_ok, 1)
                        act.sem_inc(free, 1)
                for t in range(2):
                    act.wait_ge(c_done, NC * L + C_USE[f"four{t}"] + 1)
                    act.activation(act_hi[:, 6 + t, CTX:TOK], PC[:, 0:LAT], ACT.Copy)
                    act.activation(act_hi[:, 6 + t, 0:CTX], PC[:, LAT:TOK], ACT.Copy).then_inc(four_hi, 1)

                def copies(t):
                    act.wait_ge(o_ps, 2 * L + t + 1)
                    for r in range(2):
                        act.activation(o_sb[:, r, :], pair[r][:, 0:TOK], ACT.Copy).then_inc(o_copied, 1)

                def osquares(t):
                    for r, w in enumerate("fb"):
                        act.wait_ge(c_done, NC * L + C_USE[f"cen{t}{w}"] + 1)
                        act.activation(o_sq[:, r, :], PC[:, 0:TOK], ACT.Square).then_inc(osq_ok, 1)

                def leading(t):
                    act.wait_ge(ret_hi, 2 * L + t + 1)
                    act.activation(act_hi[:, 4 + t, :], o_g[:, 0, :], ACT.Copy).then_inc(c_read, 1)

                copies(0)
                osquares(0)
                copies(1)
                leading(0)
                osquares(1)
                leading(1)

                act.wait_ge(ret_sum, 2 * L + 2)
                act.wait_ge(nbc_ok, L + 1)
                for h in range(HEADS):
                    ins = act.activation(probs_c[:, P * h:P * h + P], PC[:, P * h:P * h + P], ACT.Exp, bias=nbc[:, h:h + 1],
                                         scale=q_rs[:, h % 4, 0, h // 4:h // 4 + 1], accum_out=rsc[:, h:h + 1])
                ins.then_inc(expc_ok, 1)
                act.wait_ge(oc_ps, L + 1)
                act.activation(act_hi[:, 0:4, 0:CTX], PB_[:, 0:512].rearrange("p (t n) -> p t n", t=4),
                               ACT.Copy).then_inc(oc_hi, 1)

                with act.Fori(0, 2) as i:
                    chain.clear()

                    def prepare(q):
                        e, t = q % 2, i + 2 * (q // 2)
                        act.wait_ge(qpack, 8 * L + 4 * i + q + 1)
                        for half_ in range(2):
                            ins = act.activation(q2[HD * half_:HD * half_ + HD, :], qT[HD * e:HD * e + HD, t, CTX:TOK], ACT.Copy)
                        chain.link(ins)
                        act.wait_ge(s_done, 32 * L + 16 * i + 4 * q + 4)
                        act.activation(qq[:, q % 2, :], q2[:, :], ACT.Copy).then_inc(qhi_ok, 1)

                    def exps(q):
                        act.wait_ge(t_done, 48 * L + 24 * i + 6 * q + 6)
                        for b in range(4):
                            act.wait_ge(nb_ok, 32 * L + 16 * i + 4 * q + b + 1)
                            at = 4 * (q % 2) + b
                            act.activation(probs[:, q % 2, b, :], pair[2 + b % 2][:, 0:KEYS], ACT.Exp, bias=nb[:, at:at + 1],
                                           scale=q_rs[:, i + 2 * (q // 2), 1 + b, q % 2:q % 2 + 1],
                                           accum_out=rsum[:, at:at + 1]).then_inc(exp_ok, 1)

                    def output(q):
                        e, t = q % 2, i + 2 * (q // 2)
                        act.wait_ge(pv_done, 48 * L + 24 * i + 6 * q + 10)
                        act.activation(act_hi[HD * e:HD * e + HD, t, CTX:TOK],
                                       psum[HD * e:HD * e + HD, 2 * (q % 2) + 1, :], ACT.Copy).then_inc(o_hi, 1)

                    prepare(0)
                    exps(0)
                    prepare(1)
                    for q in range(1, 4):
                        exps(q)
                        if q < 3:
                            prepare(q + 1)
                        output(q - 1)
                    output(3)

                def square_units(first, at, last=False):
                    def two(i, more):
                        for s in range(2):
                            if not (last and isinstance(i, int) and i == 1 and s == 1):
                                split(L, first + s + 1 + (2 * i if isinstance(i, int) else 0), None if isinstance(i, int) else i)
                            if at is not None:
                                for t in range(2):
                                    m = 4 * i + 2 * s + t
                                    act.wait_ge(x_new, 2 * KD * L + at + m + 1)
                                    act.wait_ge(sq_used, 2 * KD * L + at + m - 1)
                                    act.activation(sq[:, t, :], x[:, m, :], ACT.Square).then_inc(sq_ok, 1)
                    if last:
                        two(0, None)
                        two(1, None)
                    else:
                        with act.Fori(0, 2) as i:
                            two(i, None)

                square_units(U_OUT, KD)
                chain.clear()
                norm(L, 24, KD)
                first = 0
                for n, up, down in zip(CHUNKS, U_UP, U_DOWN):
                    with act.Fori(0, n // 2) as i:
                        chain.clear()
                        for s in range(2):
                            split(L, up + s + 1, i)
                            for t in range(2):
                                act.wait_ge(job_done, JOBS * L + 2 * (up + s) + t + 3 + 4 * i)
                                act.wait_ge(cv_ok, 2 * NJ * L + 4 * i + 2 * (first + s) + t + 1)
                                act.activation(u_sb[:, t, 1:1 + CTX], pair[t][:, 0:CTX], ACT.Copy)
                                act.activation(u_sb[:, t, 2 + CTX:2 + TH], pair[t][:, CTX:TH], ACT.Copy)
                                ins = act.activation(u_sb[:, t, 2 + TH:2 + TOK], pair[t][:, 512:512 + TH], ACT.Copy)
                                chain.link(ins)
                                act.sem_inc(u_ok, 1)
                                act.sem_inc(a_free if t == 0 else b_free, 1)
                            act.wait_ge(cv_ok, 2 * NJ * L + 4 * i + 2 * (first + s) + 3)
                            act.wait_ge(gf_ok, NJ * L + 2 * i + first + s + 1)
                            act.activation(sg[:, 1:2 + TOK], cv[:, 0, 1:2 + TOK], ACT.Silu).then_inc(sg_ok, 1)
                            act.wait_ge(gf_ok, NJ * L + 2 * i + first + s + 2)
                            act.activation(g_hi[:, 2 * i + s, :], gf[:, :], ACT.Copy).then_inc(g_hi_ok, 1)
                    first += n
                    square_units(down, 2 * KD if first == NJ else None, last=first == NJ)

        @block.vector
        def _(dve):
            chain = Chain(dve, dve_chain)

            def tell(ins, *sems):
                chain.link(ins)
                for s in sems:
                    dve.sem_inc(s, 1)

            def split(L, u, i=None, width=1024):
                for h in range(2):
                    dve.wait_ge(w_hi_ok, JOBS * L + 2 * u + h + 1 + (0 if i is None else 4 * i))
                    cols = slice(1024 * h, 1024 * h + width)
                    dve.tensor_tensor(w_lo[:, u % 2, cols], w_stage[:, h, 0:width], w_hi[:, u % 2, cols].bitcast(F32),
                                      ALU.subtract).then_inc(w_split, 1)

            def add_squares(L, m, slot, at):
                dve.wait_ge(sq_ok, 2 * KD * L + at + m + 1)
                tell(dve.tensor_tensor(sq_acc[:, :], sq_acc[:, :], sq[:, slot, :], ALU.add), sq_used)

            def norm(L, which, at):
                dve.wait_ge(c_done, NC * L + C_USE["sum" + which] + 1)
                if which == "2":
                    dve.wait_ge(rs_ok, NRS * L + RS_USE["n2"])
                tell(dve.tensor_scalar(vsum[:, 0:NT], PC[:, 768:768 + NT], EPS, None, ALU.add), v_ok, c_free)
                dve.wait_ge(c_done, NC * L + C_USE["bc" + which] + 1)
                for k in range(KD + 1):
                    if k < KD:
                        if k >= 2:
                            dve.wait_ge(h_hi_ok, 2 * KD * L + at + k - 1)
                        ins = dve.tensor_tensor(tn[:, k % 2, :], x[:, k, :], PC[:, 0:TOK], ALU.mult)
                        if k == KD - 1:
                            tell(ins, tn_ok, c_free)
                        else:
                            ins.then_inc(tn_ok, 1)
                    if k >= 1:
                        dve.wait_ge(h_hi_ok, 2 * KD * L + at + k)
                        dve.tensor_tensor(act_lo[:, k - 1, :], hf[:, (k - 1) % 2, :], act_hi[:, k - 1, :].bitcast(F32),
                                          ALU.subtract).then_inc(h_ok, 1)

            dve.wait_ge(prm_t, 1)
            chain.link(dve.tensor_copy(prm[:, :], PC[:, 0:NPRM]))
            dve.sem_inc(prm_ok, 1)
            dve.memset(sq_acc[:, :], 0.0)
            for k in range(KD):
                dve.wait_ge(xt_ps, k + 1)
                tell(dve.tensor_copy(x[:, k, :], pair[k % 2][:, 0:TOK]), xt_free, x_new)
                if k >= 1:
                    dve.wait_ge(sq_ok, k)
                    tell(dve.tensor_tensor(sq_acc[:, :], sq_acc[:, :], sq[:, (k - 1) % 2, :], ALU.add), sq_used)
            dve.wait_ge(sq_ok, KD)
            tell(dve.tensor_tensor(sq_acc[:, :], sq_acc[:, :], sq[:, (KD - 1) % 2, :], ALU.add), sq_used)
            dve.wait_ge(pre_used, 8 * DEPTH + 2)
            for l in range(DEPTH):
                ins = dve.tensor_tensor(mod_pre[:, l, :, :], psum[:, 7, 32 * l:32 * l + 32].rearrange("p (t s) -> p t s", s=2),
                                        prm[:, C_BMOD + 48 * l:C_BMOD + 48 * l + MOD_PRE]
                                        .rearrange("p (t o) -> p t o", o=1).to_broadcast([P, MOD_PRE, 2]), ALU.add)
            chain.link(ins)

            with dve.Fori(0, DEPTH) as L:
                chain.clear()

                def by_group(v, n):
                    return v.rearrange("p (t o) -> p t o", o=1).to_broadcast([P, n, 2])

                dve.tensor_copy(mod[:, 0:MOD_PRE, :], mod_pre[:, L, :, :])
                dve.tensor_copy(bmod_l[:, :], prm[:, bass.ds(48 * L + C_BMOD, 48)])
                dve.tensor_copy(n2_l[:, :], prm[:, bass.ds(KD * L + R_N2, KD)])
                dve.tensor_copy(conv_l[:, :, :].rearrange("p a b -> p (a b)"), prm[:, bass.ds(176 * L + C_CONV, 176)])
                dve.tensor_copy(qk_w[:, 0:1], prm[:, bass.ds(L + R_QN, 1)])
                dve.tensor_copy(qk_w[:, 1:2], prm[:, bass.ds(L + R_KN, 1)])
                chain.link(dve.tensor_copy(vsum[:, 0:KD], prm[:, bass.ds(KD * L + R_N1, KD)]))
                chain.link(dve.scalar_tensor_tensor(scale1[:, :, :], mod[:, KD:2 * KD, :], 1.0, by_group(vsum[:, 0:KD], KD),
                                                    ALU.add, ALU.mult))
                split(L, 0)
                norm(L, "1", 0)

                def rope(t, src):
                    dve.wait_ge(d_done, ND * L + D_USE[f"rot{t}"] + 1)
                    chain.link(dve.tensor_tensor(src, src, cst("cos"), ALU.mult))
                    tell(dve.tensor_tensor(rtmp[:, :], PD[:, 0:LAT], cst("sin"), ALU.mult), d_free)
                    chain.link(dve.tensor_tensor(src, src, rtmp[:, :], ALU.add))

                def powers(t):
                    dve.wait_ge(d_done, ND * L + D_USE[f"st{t}"] + 1)
                    dve.wait_ge(rs_ok, NRS * L + RS_USE[f"q{t}" if t < 4 else "k"])
                    k = float(HD) if t < 4 else 1.0
                    tell(dve.tensor_scalar(vsum[:, 0:2 * NT], PD[:, 0:2 * NT], k, k * EPS, ALU.mult, ALU.add), v_ok, d_free)

                for u in range(9):
                    split(L, u + 1, width=CTX if u + 1 == U_DFTC else 1024)
                    for t in range(2):
                        j = 2 * u + t
                        if 1 <= j <= 5:
                            powers(j - 1)
                        if 2 <= j <= 5:
                            rope(j - 2, qT[:, j - 2, CTX:TOK])
                        if j == 6:
                            dve.wait_ge(c_done, NC * L + C_USE["kbc"] + 1)
                            tell(dve.tensor_tensor(kT[:, :], kT[:, :], PC[:, 0:TOK], ALU.mult), c_free, k_normed)
                        if j == 8:
                            for g in range(2):
                                for half_ in range(2):
                                    dve.tensor_copy(kc[HD * half_:HD * half_ + HD, g, :], kT[HD * g:HD * g + HD, 0:CTX])
                            rope(4, kT[:, CTX:TOK])
                            dve.wait_ge(d_done, ND * L + D_USE["kct"] + 1)
                            tell(dve.tensor_copy(k_out[:, L, :], PD[:, 0:P]), d_free)
                            dve.wait_ge(d_done, ND * L + D_USE["kcache"] + 1)
                            for g in range(2):
                                rows_ = slice(HD * g, HD * g + HD)
                                for half_ in range(2):
                                    to = slice(HD * half_, HD * half_ + HD)
                                    dve.tensor_copy(k2[to, 0:PAST], PD[rows_, 0:PAST])
                                    ins = dve.tensor_copy(k2[to, PAST:KEYS], kT[rows_, CTX:TOK])
                                tell(ins, *([d_free] if g else []))
                                dve.tensor_copy(kp[0:HD, g, :], k2[0:HD, :])
                                chain.link(dve.tensor_copy(k2_hi[:, :], k2[:, :]))
                                chain.link(dve.tensor_tensor(kp[HD:P, g, :], k2[HD:P, :], k2_hi[HD:P, :].bitcast(F32), ALU.subtract))
                            dve.sem_inc(kp_ok, 1)
                        if u == U_RV:
                            dve.wait_ge(job_done, JOBS * L + j + 3)
                            dst, n = (rv[:, 0:4, :], 1024) if t == 0 else (rv[:, 4:5, :], 256)
                            tell(dve.tensor_copy(dst.rearrange("p b n -> p (b n)"), pair[t][:, 0:n]), rv_ok,
                                 a_free if t == 0 else b_free)
                            dve.wait_ge(c_done, NC * L + C_USE[f"rkt{t}"] + 1)
                            dve.tensor_copy(rkT[:, t, :], PC[:, 0:TOK]).then_inc(c_free, 1)
                        if u == U_FX:
                            dve.wait_ge(fx_hi_ok, 2 * L + t + 1)
                            dst, src, n = (fx_lo[:, 0:4, :], fx_hi[:, 0:4, :], 1024) if t == 0 else (fx_lo[:, 4:5, :], fx_hi[:, 4:5, :], 256)
                            tell(dve.tensor_tensor(dst.rearrange("p b n -> p (b n)"), pair[t][:, 0:n],
                                                   src.rearrange("p b n -> p (b n)").bitcast(F32), ALU.subtract), fx_ok,
                                 a_free if t == 0 else b_free)
                dve.wait_ge(m_used, MOD_REST * (L + 1) + 2)
                tell(dve.tensor_tensor(mod[:, MOD_PRE:48, :], mod_ps, by_group(bmod_l[:, MOD_PRE:48], MOD_REST), ALU.add), mod_ok)
                chain.link(dve.scalar_tensor_tensor(scale2[:, :, :], mod[:, 32:40, :], 1.0, by_group(n2_l[:, :], KD), ALU.add, ALU.mult))
                for u in (U_DFTC, U_COS, U_SIN):
                    split(L, u + 1)
                for t in range(2):
                    dve.wait_ge(four_hi, 2 * L + t + 1)
                    dve.tensor_tensor(act_lo[:, 6 + t, CTX:TOK], PC[:, 0:LAT], act_hi[:, 6 + t, CTX:TOK].bitcast(F32), ALU.subtract)
                    dve.tensor_tensor(act_lo[:, 6 + t, 0:CTX], PC[:, LAT:TOK], act_hi[:, 6 + t, 0:CTX].bitcast(F32),
                                      ALU.subtract).then_inc(c_free, 1)

                def keys_decayed(t):
                    if t == 1:
                        dve.wait_ge(d_done, ND * L + D_USE["u0"] + 1)
                    for r, name in enumerate(("kdf", "kdb")):
                        w = cst(name, P * t, P * t + P).rearrange("p (o n) -> p o n", o=1).to_broadcast([P, NT, P])
                        ins = dve.tensor_tensor(k_dec[:, r, :, :], rk[:, :, P * t:P * t + P], w, ALU.mult)
                    tell(ins, kdec_ok)

                def queries_decayed(t):
                    if t == 1:
                        dve.wait_ge(o_ps, 2 * L + 1)
                    for r, name in enumerate(("qdf", "qdb")):
                        w = cst(name, P * t, P * t + P).rearrange("p (o n) -> p o n", o=1).to_broadcast([P, 4, P])
                        ins = dve.tensor_tensor(q_dec[:, r, :].rearrange("p (c n) -> p c n", c=4),
                                                rqT[:, t, CTX:TOK].rearrange("p (c n) -> p c n", c=4), w, ALU.mult)
                    chain.link(ins)

                def masked(t, e):
                    dve.wait_ge(c_done, NC * L + C_USE[f"at{t}{e}"] + 1)
                    if t or e:
                        dve.wait_ge(adec_used, 4 * L + 2 * t + e)
                    for r, name in enumerate(("maskf", "maskb")):
                        h = 2 * t + e
                        w = cst(name, P * h, P * h + P).rearrange("p (o n) -> p o n", o=1).to_broadcast([P, NT, P])
                        ins = dve.tensor_tensor(a_dec[:, r, :].rearrange("p (c n) -> p c n", c=NT),
                                                PC[:, 0:TOK].rearrange("p (c n) -> p c n", c=NT), w, ALU.mult)
                    tell(ins, adec_ok, c_free)

                def states(t):
                    dve.wait_ge(d_done, ND * L + D_USE[f"u{t}"] + 1)
                    if t == 1:
                        dve.wait_ge(o_ps, 2 * L + 1)
                    for r in range(2):
                        for e in range(2):
                            rows_ = slice(HD * e, HD * e + HD)
                            dve.tensor_copy(s_out[rows_, L, r, t, :], PD[rows_, 512 * r + HD * e:512 * r + HD * e + HD])
                    first = dve.tensor_copy(ret_st[:, 0, 0, :], ret_s0[:, 0, t, :])
                    chain.link(dve.tensor_copy(ret_st[:, 1, 3, :], ret_s0[:, 1, t, :]))
                    for n in range(3):
                        for r, to, frm, up in ((0, n + 1, n, n + 1), (1, 2 - n, 3 - n, 3 - n)):
                            for e in range(2):
                                rows_ = slice(HD * e, HD * e + HD)
                                at = 512 * r + P * up + HD * e
                                g = CONST["gam"][0] + 2 * r + t
                                ins = dve.scalar_tensor_tensor(ret_st[rows_, r, to, :], ret_st[rows_, r, frm, :],
                                                               const[rows_, g:g + 1], PD[rows_, at:at + HD], ALU.mult, ALU.add)
                        chain.link(ins)
                    dve.sem_inc(st_ok, 1)
                    dve.sem_inc(d_free, 1)

                def gated(t):
                    for r, w in enumerate("fb"):
                        dve.wait_ge(osq_ok, 4 * L + 2 * t + r + 1)
                        tell(dve.tensor_tensor(o_g[:, r, :], PC[:, 0:TOK], gate[:, r, t, :], ALU.mult), c_free)

                def normalised(t):
                    for r, w in enumerate("fb"):
                        dve.wait_ge(d_done, ND * L + D_USE[f"ty{t}{w}"] + 1)
                        dve.wait_ge(rs_ok, NRS * L + RS_USE[f"r{t}{w}"])
                        tell(dve.tensor_scalar(vsum[:, 0:2 * NT], PD[:, 0:2 * NT], EPS, None, ALU.add), v_ok, d_free)
                        dve.wait_ge(d_done, ND * L + D_USE[f"by{t}{w}"] + 1)
                        tell(dve.tensor_tensor(o_g[:, r, :], o_g[:, r, :], PD[:, 0:TOK], ALU.mult), d_free)
                    tell(dve.tensor_tensor(o_g[:, 0, :], o_g[:, 0, :], o_g[:, 1, :], ALU.add), ret_hi)
                    dve.wait_ge(c_read, 2 * L + t + 1)
                    tell(dve.tensor_tensor(act_lo[:, 4 + t, :], o_g[:, 0, :], act_hi[:, 4 + t, :].bitcast(F32), ALU.subtract), ret_sum)

                dve.wait_ge(s0_in, 32 * (L + 1))
                keys_decayed(0)
                queries_decayed(0)
                masked(0, 0)
                masked(0, 1)
                states(0)
                keys_decayed(1)
                gated(0)
                queries_decayed(1)
                masked(1, 0)
                masked(1, 1)
                states(1)
                normalised(0)
                gated(1)
                normalised(1)

                dve.wait_ge(c_done, NC * L + C_USE["sctx"] + 1)
                chain.link(dve.reduce_max(mxc[:, :], PC[:, 0:1024].rearrange("p (h n) -> p h n", h=HEADS), AX.X))
                dve.scalar_tensor_tensor(nbc[:, :].rearrange("p (e t) -> p e t", e=2), mxc[:, :].rearrange("p (e t) -> p e t", e=2),
                                         -1.0, q_rs[:, :, 0, :].rearrange("p t e -> p e t"), ALU.mult, ALU.mult).then_inc(nbc_ok, 1)
                dve.wait_ge(expc_ok, L + 1)
                dve.sem_inc(c_free, 1)
                chain.link(dve.reciprocal(ric[:, :], rsc[:, :]))
                for h in range(HEADS):
                    ins = dve.tensor_scalar(diag[:, h // 4, h % 4, :], ident, ric[:, h:h + 1], None, ALU.mult)
                ins.then_inc(dgc_ok, 1)
                dve.wait_ge(tc_ps, L + 1)
                dve.tensor_copy(probs_t[:, 0:2, :].rearrange("p b n -> p (b n)"), PA).then_inc(ptc_ok, 1)
                dve.wait_ge(oc_hi, L + 1)
                dve.tensor_tensor(act_lo[:, 0:4, 0:CTX], PB_[:, 0:512].rearrange("p (t n) -> p t n", t=4),
                                  act_hi[:, 0:4, 0:CTX].bitcast(F32), ALU.subtract).then_inc(oc_ok, 1)

                with dve.Fori(0, 2) as i:
                    chain.clear()

                    def rest(q):
                        dve.wait_ge(qhi_ok, 8 * L + 4 * i + q + 1)
                        dve.tensor_tensor(q_lo[:, q % 2, :], q2[0:HD, :], qq[0:HD, q % 2, :].bitcast(F32),
                                          ALU.subtract).then_inc(qpack, 1)

                    def maximum(q, b):
                        dve.wait_ge(s_done, 32 * L + 16 * i + 4 * q + b + 9)
                        at = 4 * (q % 2) + b
                        chain.link(dve.reduce_max(mx[:, at:at + 1], pair[2 + b % 2][:, 0:KEYS], AX.X))
                        dve.scalar_tensor_tensor(nb[:, at:at + 1], mx[:, at:at + 1], -1.0,
                                                 q_rs[:, i + 2 * (q // 2), 1 + b, q % 2:q % 2 + 1], ALU.mult, ALU.mult).then_inc(nb_ok, 1)

                    def diagonals(q):
                        dve.wait_ge(t_done, 48 * L + 24 * i + 6 * q + 6)
                        a = 4 * (q % 2)
                        dve.wait_ge(exp_ok, 32 * L + 16 * i + 4 * q + 6)
                        chain.link(dve.reciprocal(rinv[:, a:a + 4], rsum[:, a:a + 4]))
                        for b in range(4):
                            dve.tensor_scalar(diag[:, q % 2, b, :], ident, rinv[:, a + b:a + b + 1], None, ALU.mult).then_inc(dg_ok, 1)

                    def turned(q, t):
                        n = 6 * q + t
                        dve.wait_ge(t_done, 48 * L + 24 * i + n + 13)
                        dve.wait_ge(pv_done, 48 * L + 24 * i + n + 1)
                        dve.tensor_copy(probs_t[:, n % 4, :], psum[:, 2 * (n % 2), :]).then_inc(pt_ok, 1)

                    def output(q):
                        e, t = q % 2, i + 2 * (q // 2)
                        dve.wait_ge(o_hi, 8 * L + 4 * i + q + 1)
                        rows_ = slice(HD * e, HD * e + HD)
                        dve.tensor_tensor(act_lo[rows_, t, CTX:TOK], psum[rows_, 2 * (q % 2) + 1, :],
                                          act_hi[rows_, t, CTX:TOK].bitcast(F32), ALU.subtract).then_inc(o_ok, 1)

                    rest(0)
                    for b in range(4):
                        maximum(0, b)
                    for q in range(4):
                        diagonals(q)
                        if q < 3:
                            rest(q + 1)
                        for t in range(NKT):
                            turned(q, t)
                            if q < 3 and t < 4:
                                maximum(q + 1, t)
                            if q >= 1 and t == 2:
                                output(q - 1)
                    output(3)

                chain.clear()
                dve.memset(sq_acc[:, :], 0.0)
                for t in range(2):
                    for at in (0, CTX + 1, GAP - 1):
                        ins = dve.memset(u_sb[:, t, at:at + 1], 0.0)
                chain.link(ins)

                def square_units(first, gains, at, last=False):
                    def two(i):
                        static = isinstance(i, int)
                        for s in range(2):
                            if not (last and i == 1 and s == 1):
                                split(L, first + s + 1 + (2 * i if static else 0), None if static else i)
                            for t in range(2):
                                m = 4 * i + 2 * s + t
                                dve.wait_ge(job_done, JOBS * L + 2 * (first + s) + t + 3 + 4 * i)
                                for lo, hi, src in ((0, CTX, pair[t][:, 0:CTX]), (CTX, TH, pair[t][:, CTX:TH]),
                                                    (TH, TOK, pair[t][:, 512:512 + TH])):
                                    g = 0 if lo == 0 else 1
                                    ins = dve.scalar_tensor_tensor(x[:, m, lo:hi], src, mod[:, gains + m, g:g + 1],
                                                                   x[:, m, lo:hi], ALU.mult, ALU.add)
                                tell(ins, a_free if t == 0 else b_free, *([x_new] if at is not None else []))
                                if at is not None:
                                    add_squares(L, m, t, at)
                    if last:
                        two(0)
                        two(1)
                    else:
                        with dve.Fori(0, 2) as i:
                            chain.clear()
                            two(i)
                    chain.clear()

                square_units(U_OUT, 16, KD)
                norm(L, "2", KD)

                first = 0
                for n, up, down in zip(CHUNKS, U_UP, U_DOWN):
                    with dve.Fori(0, n // 2) as i:
                        chain.clear()
                        for s in range(2):
                            split(L, up + s + 1, i)
                            j = first + s
                            for t in range(2):
                                dve.wait_ge(u_ok, 2 * NJ * L + 4 * i + 2 * j + t + 1)
                                if t == 0:
                                    dve.wait_ge(sg_ok, NJ * L + 2 * i + j + 1)
                                tile = 2 * i + j + 22 * t
                                c1 = slice(1, 2 + TOK)
                                chain.link(dve.tensor_scalar(cv[:, t, c1], u_sb[:, t, c1], conv_l[:, 1, bass.ds(tile, 1)],
                                                             conv_l[:, 3, bass.ds(tile, 1)], ALU.mult, ALU.add))
                                chain.link(dve.scalar_tensor_tensor(cv[:, t, c1], u_sb[:, t, 0:1 + TOK], conv_l[:, 0, bass.ds(tile, 1)],
                                                                    cv[:, t, c1], ALU.mult, ALU.add))
                                tell(dve.scalar_tensor_tensor(cv[:, t, c1], u_sb[:, t, 2:3 + TOK], conv_l[:, 2, bass.ds(tile, 1)],
                                                              cv[:, t, c1], ALU.mult, ALU.add), cv_ok)
                            dve.wait_ge(sg_ok, NJ * L + 2 * i + j + 2)
                            dve.tensor_tensor(gf[:, 0:CTX], sg[:, 1:1 + CTX], cv[:, 1, 1:1 + CTX], ALU.mult)
                            dve.tensor_tensor(gf[:, CTX:TOK], sg[:, 2 + CTX:2 + TOK], cv[:, 1, 2 + CTX:2 + TOK], ALU.mult).then_inc(gf_ok, 1)
                            dve.wait_ge(g_hi_ok, NJ * L + 2 * i + j + 1)
                            dve.tensor_tensor(g_lo[:, 2 * i + s, :], gf[:, :], g_hi[:, 2 * i + s, :].bitcast(F32),
                                              ALU.subtract).then_inc(g_ok, 1)
                    first += n
                    chain.clear()
                    if first == NJ:
                        chain.link(dve.memset(sq_acc[:, :], 0.0))
                    square_units(down, 40, 2 * KD if first == NJ else None, last=first == NJ)

            chain.clear()
            dve.wait_ge(c_done, NC * DEPTH + 1)
            tell(dve.tensor_scalar(vsum[:, 0:NT], PC[:, 768:768 + NT], EPS, None, ALU.add), v_ok)
            dve.wait_ge(c_done, NC * DEPTH + 2)
            for k in range(KD + 1):
                if k < KD:
                    if k >= 2:
                        dve.wait_ge(y_row, k - 1)
                    dve.scalar_tensor_tensor(y_t[:, k % 2, :], x[:, k, :], prm[:, R_FIN + k:R_FIN + k + 1], PC[:, 0:TOK],
                                             ALU.mult, ALU.mult).then_inc(y_col, 1)
                if k >= 1:
                    dve.wait_ge(y_row, k)
                    dve.tensor_copy(rows[:, :, P * (k - 1):P * k], pair[(k - 1) % 2][:, 0:TOK].rearrange("p (t n) -> p t n", t=NT))\
                       .then_inc(y_rows, 1)

        @block.gpsimd
        def _(pool):
            pool.memset(half[:, :], -0.5).then_inc(pool_chain, 1)
            pool.wait_ge(pool_chain, 1)
            with pool.Fori(0, DEPTH) as L:
                for name, n in RS_USE.items():
                    pool.wait_ge(v_ok, NRS * L + n + 1)
                    w = NT if name in ("n1", "n2") else 2 * NT
                    if name[0] == "q":
                        dst = q_rs[:, int(name[1]), :, :].rearrange("p t e -> p (t e)")
                    else:
                        dst = rstd[:, 0:w]
                    pool.tensor_tensor(dst, vsum[:, 0:w], half[:, 0:w], ALU.pow).then_inc(rs_ok, 1)
            pool.wait_ge(v_ok, NRS * DEPTH + 1)
            pool.tensor_tensor(rstd[:, 0:NT], vsum[:, 0:NT], half[:, 0:NT], ALU.pow).then_inc(rs_ok, 1)


def constants(np):
    f32 = np.float32
    out = np.zeros((P, NCONST), np.float64)

    def put(name, v):
        a, b = CONST[name]
        out[:, a:b] = v

    i = np.arange(P)
    put("ident", np.eye(P))
    put("ones", np.full((P, 1), 1.0 / D))
    put("blk", (i[:, None] // HD == np.arange(2)[None]) / HD)
    same = (i[:, None] // HD == i[None] // HD)
    put("center", np.eye(P) - same / HD)
    rot = np.zeros((P, P))
    for m in range(P):
        base, r = m // 32 * 32, m % 32
        if r < 16:
            rot[base + r + 16, m] = -1.0
        else:
            rot[base + r - 16, m] = 1.0
    put("rot", rot)
    ang = 2 * np.pi * (np.outer(i % HD, i % HD) % HD) / HD
    for name, n in (("l", LAT), ("c", CTX)):
        put("c64" + name, same * np.cos(ang) / np.sqrt(n * HD))
        put("s64" + name, same * -np.sin(ang) / np.sqrt(n * HD))
    tok = np.arange(LAT)
    freqs = (f32(10000.0) ** (-np.arange(16, dtype=f32) / f32(16))).astype(f32)
    pos = np.stack([(tok // 64).astype(f32), (tok % 64).astype(f32)])
    d = i % HD
    a = (pos[d // 32] * freqs[d % 16][:, None]).astype(f32).astype(np.float64)
    put("cos", np.cos(a))
    put("sin", np.sin(a))
    j, q = i[:, None], i[None]
    for r, (w, base) in enumerate((("f", 5.0), ("b", 5.5))):
        lg = np.log1p(-np.exp2(-(f32(base) + np.arange(4, dtype=f32)))).astype(f32).astype(np.float64)
        dist = (q - j) if r == 0 else (j - q)
        put("mask" + w, np.concatenate([np.where(dist >= 0, np.exp(np.maximum(dist, 0) * lg[h]), 0.0) for h in range(4)], 1))
        place = i if r == 0 else P - 1 - i
        put("qd" + w, np.concatenate([np.exp((place + 1.0)[None] * lg[2 * t + i // HD][:, None]) for t in range(2)], 1))
        put("kd" + w, np.exp((P - 1.0 - place)[:, None] * lg[np.arange(256) // HD][None]))
        for t in range(2):
            out[:, CONST["gam"][0] + 2 * r + t] = np.exp(P * lg[2 * t + i // HD])
    dft = np.zeros((P, 256 + 4096), np.float64)
    a = 2 * np.pi * (np.outer(i, i) % CTX) / CTX
    dft[:, 0:128], dft[:, 128:256] = np.cos(a), np.sin(a)
    a = 2 * np.pi * (np.outer(tok, tok) % LAT) / LAT
    for n, v in enumerate((np.cos(a), np.sin(a))):
        dft[:, 256 + 2048 * n:256 + 2048 * (n + 1)] = v.reshape(4, P, LAT).transpose(1, 0, 2).reshape(P, 2048)
    return out.astype(f32), dft.astype(f32)


_INS = ["x_prompt", "x_sample", "c", "cache_attn_k", "cache_attn_v", "state_ret", "c_ctx", "w_mod", "b_mod", "norm1_w",
        "w_in", "q_norm_w", "k_norm_w", "w_out", "norm2_w", "w_up", "conv_w", "conv_b", "w_down", "final_norm_w"]
_OUTS = [(1, CTX, D), (1, LAT, D), (1, DEPTH, CTX, 2, HD), (1, DEPTH, CTX, 2, HD), (1, DEPTH, 2, 4, HD, HD)]


def kernel(**inputs):
    import numpy as _np
    import concourse.bacc as _bacc
    from concourse import mybir as _mybir
    from concourse.bass_utils import run_bass_kernel_spmd as _run

    nc = _bacc.Bacc("TRN2", target_bir_lowering=False, num_devices=1)
    arrays, args = {}, []
    const, dft = constants(_np)
    for name, a in [(n, inputs[n]) for n in _INS] + [("const", const), ("dft", dft)]:
        a = _np.ascontiguousarray(a)
        arrays[f"in_{name}_dram"] = a
        args.append(nc.dram_tensor(f"in_{name}_dram", a.shape, _mybir.dt.from_np(a.dtype), kind="ExternalInput").ap())
    for i, shape in enumerate(_OUTS):
        args.append(nc.dram_tensor(f"out_{i}_dram", shape, _mybir.dt.float32, kind="ExternalOutput").ap())
    program(nc, *args)
    r = _run(nc, [arrays], core_ids=[0])
    return tuple(r.results[0][f"out_{i}_dram"] for i in range(len(_OUTS)))
```

```python
from contextlib import ExitStack

import concourse.bass as bass
from concourse import mybir

F32 = mybir.dt.float32
F32R = mybir.dt.float32r
ALU = mybir.AluOpType
ACT = mybir.ActivationFunctionType
AX = mybir.AxisListType

P = 128
D = 1024
KD = D // P
CTX = 128
LAT = 512
TOK = CTX + LAT
NT = TOK // P
TH = TOK // 2
DEPTH = 2
HEADS = 8
HD = 64
PAST = 256
KEYS = PAST + LAT
NKT = KEYS // P
FF = 2816
NJ = FF // P
EPS = 1e-6
GAP = TOK + 3
CHUNKS = (8, 8, 6)

IN_COLS = (0, 256, 512, 768, 1024, 1280, 2048, 1536, 1792)
U_Q0, U_Q1, U_KV, U_RQ, U_RK, U_RV, U_FX, U_GF, U_GB, U_DFTC, U_COS, U_SIN = range(12)
U_OUT = 12
U_UP = (16, 28, 40)
U_DOWN = (24, 36, 46)
UNITS = 50
JOBS = 2 * UNITS
MOD_ROUNDS = 4
MT = KD * MOD_ROUNDS
V_SH1, V_SC1, V_G1, V_SH2, V_SC2, V_G2 = range(6)

CONST = {}
_at = 0
for _name, _width in (("ident", 128), ("ones", 1), ("blk", 2), ("center", 128), ("rot", 128),
                      ("c64l", 128), ("s64l", 128), ("c64c", 128), ("s64c", 128),
                      ("cos", 512), ("sin", 512), ("maskf", 512), ("maskb", 512),
                      ("qdf", 256), ("qdb", 256), ("kdf", 256), ("kdb", 256), ("gam", 4)):
    CONST[_name] = (_at, _at + _width)
    _at += _width
NCONST = _at
CONST_A = CONST["cos"][0]

R_CC, R_C, R_N1, R_N2, R_FIN, R_QN, R_KN, R_END = 0, 8, 16, 32, 48, 56, 58, 60
C_BMOD = R_END
C_CONV = C_BMOD + 96
NPRM = C_CONV + DEPTH * 4 * 44


def uses(*names):
    return {n: i for i, n in enumerate(names)}


C_USE = uses("sum1", "bc1", "mod0", "kbc", "mod1", "rkt0", "rkt1", "mod2", "mod3", "four0", "four1",
             "at00", "at01", "at10", "at11", "cen0f", "cen0b", "cen1f", "cen1b",
             "sctx", "sum2", "bc2")
D_USE = uses("st0", "st1", "rot0", "st2", "rot1", "st3", "rot2", "st4", "rot3", "rot4", "kct", "kcache",
             "u0", "u1", "ty0", "by0f", "by0b", "ty1", "by1f", "by1b")
NC, ND = len(C_USE), len(D_USE)
RS_USE = uses("n1", "q0", "q1", "q2", "q3", "k", "r0", "r1", "n2")
NRS = len(RS_USE)


def program(nc, x_prompt, x_sample, c, cache_k, cache_v, state_ret, c_ctx, w_mod, b_mod, norm1_w, w_in,
            q_norm_w, k_norm_w, w_out, norm2_w, w_up, conv_w, conv_b, w_down, final_norm_w,
            const_d, dft_d, y_prompt, y_sample, new_k, new_v, new_s):
    w_in_v = w_in.rearrange("l (k p) n -> l p k n", p=P)
    w_out_v = w_out.rearrange("l (k p) n -> l p k n", p=P)
    w_up_v = w_up.rearrange("l (k p) n -> l p k n", p=P)
    w_down_v = w_down.rearrange("l (k p) n -> l p k n", p=P)
    w_mod_v = w_mod.rearrange("l (k p) n -> l p k n", p=P)

    with ExitStack() as ctx:
        def sb(name, shape, dt=F32, stack=None):
            return (stack or ctx).enter_context(nc.sbuf_tensor(name, shape, dt))

        def sem(name):
            return ctx.enter_context(nc.semaphore(name))

        x = sb("x", [P, KD, TOK])
        alias = ExitStack()
        m_pre_a = sb("m_pre_a", [P, 10, D], F32, alias)
        alias.close()
        alias = ExitStack()
        o_g1 = sb("o_g1", [P, 2, TOK], F32, alias)
        alias.enter_context(nc.sbuf_tensor("act_hi_rest", [P, KD - 2, TOK], F32))
        a_dec1 = sb("a_dec1", [P, 2, TOK], F32, alias)
        alias.close()
        act_hi = sb("act_hi", [P, KD, TOK], F32R)
        act_lo = sb("act_lo", [P, KD, TOK], F32R)
        w_stage = sb("w_stage", [P, 2, 1024])
        w_hi = sb("w_hi", [P, 2, 2048], F32R)
        w_lo = sb("w_lo", [P, 2, 2048], F32R)
        const = sb("const", [P, NCONST])
        prm = sb("prm", [P, NPRM])
        silu_c = sb("silu_c", [P, KD, 32])
        mod_rows = sb("mod_rows", [P, 256])
        mod_next = sb("mod_next", [P, 2 * KD, 2])
        mod = sb("mod", [P, 48, 2])
        scale1 = sb("scale1", [P, KD, 2])
        scale2 = sb("scale2", [P, KD, 2])
        bmod_l = sb("bmod_l", [P, 48])
        n2_l = sb("n2_l", [P, KD])
        conv_l = sb("conv_l", [P, 4, 44])
        qk_w = sb("qk_w", [P, 2])
        half = sb("half", [P, 4 * NT])
        vsum = sb("vsum", [P, 4 * NT])
        rstd = sb("rstd", [P, 4 * NT])
        q_rs = sb("q_rs", [P, 4, NT, 2])
        k_out = sb("k_out", [P, DEPTH, P])
        v_out = sb("v_out", [P, DEPTH, P])
        s_out = sb("s_out", [P, DEPTH, 2, 2, HD])
        ret_s0 = sb("ret_s0", [P, 2, 2, HD])
        ret_st = sb("ret_st", [P, 2, 4, HD])

        alias = ExitStack()
        tn = sb("tn", [P, 2, TOK], F32, alias)
        hf = sb("hf", [P, 2, TOK], F32, alias)
        sq = sb("sq", [P, 2, TOK], F32, alias)
        sq_acc = sb("sq_acc", [P, TOK], F32, alias)
        alias.close()
        alias = ExitStack()
        m_next = sb("m_next", [P, KD // 2, D], F32, alias)
        alias.close()
        qT = sb("qT", [P, 4, TOK])
        v_all = sb("v_all", [P, 14, HD])
        kp = sb("kp", [P, 2, KEYS], F32R)

        phase = ExitStack()
        kT = sb("kT", [P, TOK], F32, phase)
        kc = sb("kc", [P, 2, CTX], F32, phase)
        mx = sb("mx", [P, 8], F32, phase)
        nb = sb("nb", [P, 8], F32, phase)
        rsum = sb("rsum", [P, 8], F32, phase)
        rinv = sb("rinv", [P, 8], F32, phase)
        mxc = sb("mxc", [P, 8], F32, phase)
        nbc = sb("nbc", [P, 8], F32, phase)
        rsc = sb("rsc", [P, 8], F32, phase)
        ric = sb("ric", [P, 8], F32, phase)
        ret = ExitStack()
        rqT = sb("rqT", [P, 2, TOK], F32, ret)
        rkT = sb("rkT", [P, 2, TOK], F32, ret)
        rk = sb("rk", [P, NT, 256], F32, ret)
        rv = sb("rv", [P, NT, 256], F32, ret)
        gate = sb("gate", [P, 2, 2, TOK], F32, ret)
        proj = ExitStack()
        m_stage = sb("m_stage", [P, 2, D], F32, proj)
        fx_hi = sb("fx_hi", [P, NT, 256], F32R, proj)
        fx_lo = sb("fx_lo", [P, NT, 256], F32R, proj)
        tmp = ExitStack()
        sqq = sb("sqq", [P, TOK], F32, tmp)
        rtmp = sb("rtmp", [P, LAT], F32, tmp)
        tmp.close()
        tmp = ExitStack()
        k2 = sb("k2", [P, KEYS], F32, tmp)
        k2_hi = sb("k2_hi", [P, KEYS], F32R, tmp)
        k_past = sb("k_past", [P, 2, P], F32, tmp)
        tmp.close()
        tmp = ExitStack()
        dft_y = sb("dft_y", [P, 2, 2, LAT], F32, tmp)
        dft_yc = m_stage[:, 0, 0:4 * CTX].rearrange("p (t w n) -> p t w n", t=2, w=2)
        tmp.close()
        proj.close()
        k_dec = sb("k_dec", [P, 2, NT, P], F32, ret)
        a_dec = [sb("a_dec", [P, 2, TOK], F32, ret), a_dec1]
        q_dec = sb("q_dec", [P, 2, LAT], F32, ret)
        o_sb = sb("o_sb", [P, 2, TOK], F32, ret)
        o_sq = sb("o_sq", [P, 2, TOK], F32, ret)
        o_g = [rk[:, :, :].rearrange("p b n -> p (b n)").rearrange("p (r n) -> p r n", r=2),
               o_g1]
        ret.close()
        probs = sb("probs", [P, 2, 4, KEYS], F32, phase)
        probs_t = sb("probs_t", [P, 4, LAT], F32, phase)
        q2 = sb("q2", [P, LAT], F32, phase)
        qq = sb("qq", [P, 2, LAT], F32R, phase)
        q_lo = sb("q_lo", [HD, 2, LAT], F32R, phase)
        diag = sb("diag", [P, 2, 4, P], F32, phase)
        phase.close()
        ffn = ExitStack()
        g_hi = sb("g_hi", [P, 8, TOK], F32R, ffn)
        g_lo = sb("g_lo", [P, 8, TOK], F32R, ffn)
        u_sb = sb("u_sb", [P, 2, GAP], F32, ffn)
        cv = sb("cv", [P, 2, GAP], F32, ffn)
        sg = sb("sg", [P, GAP], F32, ffn)
        gf = sb("gf", [P, TOK], F32, ffn)
        ffn.close()
        ends = ExitStack()
        rows = sb("rows", [P, NT, D], F32, ends)
        m_pre_b = sb("m_pre_b", [P, 6, D], F32, ends)
        prm_rows = sb("prm_rows", [R_END, P], F32, ends)
        bmod_rows = sb("bmod_rows", [96, P], F32, ends)
        conv_rows = sb("conv_rows", [44, DEPTH, 4, P], F32, ends)
        y_t = sb("y_t", [P, 2, TOK], F32, ends)
        ends.close()

        psum = ctx.enter_context(nc.psum_tensor("psum", [P, 8, 512], F32))
        pair = [psum[:, 2 * i:2 * i + 2, :].rearrange("p b n -> p (b n)") for i in range(4)]
        PA, PB_, PC, PD = pair
        probs_c = probs[:, 0, :, :].rearrange("p b n -> p (b n)")
        mod_ps = psum[:, 7, 0:256]
        mod_tp = PC[:, 768:1024]

        def m_pre(n):
            return m_pre_a[:, n, :] if n < 10 else m_pre_b[:, n - 10, :]

        def cst(name, lo=0, hi=None):
            a, b = CONST[name]
            return const[:, a + lo:(b if hi is None else a + hi)]

        ident = cst("ident")

        one = sem("one")
        loads = sem("loads")
        const_in = sem("const_in")
        row_in = sem("row_in")
        pre_in = [sem(f"pre_in{i}") for i in range(4)]
        next_in = sem("next_in")
        next_sums = sem("next_sums")
        next_used = sem("next_used")
        next_rows = sem("next_rows")
        next_turned = sem("next_turned")
        next_ok = sem("next_ok")
        prm_t = sem("prm_t")
        prm_ok = sem("prm_ok")
        silu_ok = sem("silu_ok")
        xt_ps = sem("xt_ps")
        xt_free = sem("xt_free")
        w_landed = [sem(f"w_landed{i}") for i in range(2)]
        w_hi_ok = sem("w_hi_ok")
        w_split = sem("w_split")
        m_landed = [sem(f"m_landed{i}") for i in range(2)]
        m_used = sem("m_used")
        m_sums = sem("m_sums")
        m_rows_ok = sem("m_rows_ok")
        job_done = sem("job_done")
        a_free = sem("a_free")
        b_free = sem("b_free")
        c_done = sem("c_done")
        c_free = sem("c_free")
        d_done = sem("d_done")
        d_free = sem("d_free")
        x_new = sem("x_new")
        sq_ok = sem("sq_ok")
        sq_used = sem("sq_used")
        tn_ok = sem("tn_ok")
        hf_ok = sem("hf_ok")
        h_hi_ok = sem("h_hi_ok")
        h_ok = sem("h_ok")
        v_ok = sem("v_ok")
        rs_ok = sem("rs_ok")
        sqq_ok = sem("sqq_ok")
        kv_in = sem("kv_in")
        s0_in = sem("s0_in")
        fx_hi_ok = sem("fx_hi_ok")
        fx_ok = sem("fx_ok")
        tok_ok = sem("tok_ok")
        rv_ok = sem("rv_ok")
        y_ok = sem("y_ok")
        four_hi = sem("four_hi")
        q_copied = sem("q_copied")
        k_normed = sem("k_normed")
        c_read = sem("c_read")
        kdec_ok = sem("kdec_ok")
        adec_ok = sem("adec_ok")
        adec_used = sem("adec_used")
        st_ok = sem("st_ok")
        o_ps = sem("o_ps")
        o_copied = sem("o_copied")
        osq_ok = sem("osq_ok")
        cg_ok = sem("cg_ok")
        ret_sum = sem("ret_sum")
        ret_hi = sem("ret_hi")
        kp_ok = sem("kp_ok")
        nbc_ok = sem("nbc_ok")
        expc_ok = sem("expc_ok")
        dgc_ok = sem("dgc_ok")
        tc_ps = sem("tc_ps")
        ptc_ok = sem("ptc_ok")
        oc_ps = sem("oc_ps")
        oc_hi = sem("oc_hi")
        oc_ok = sem("oc_ok")
        q2_ok = sem("q2_ok")
        qhi_ok = sem("qhi_ok")
        qpack = sem("qpack")
        s_done = sem("s_done")
        nb_ok = sem("nb_ok")
        exp_ok = sem("exp_ok")
        dg_ok = sem("dg_ok")
        t_done = sem("t_done")
        pt_ok = sem("pt_ok")
        pv_done = sem("pv_done")
        o_hi = sem("o_hi")
        o_ok = sem("o_ok")
        u_ok = sem("u_ok")
        cv_ok = sem("cv_ok")
        sg_ok = sem("sg_ok")
        gf_ok = sem("gf_ok")
        g_hi_ok = sem("g_hi_ok")
        g_ok = sem("g_ok")
        y_col = sem("y_col")
        y_row = sem("y_row")
        y_rows = sem("y_rows")
        stored = sem("stored")
        act_chain = sem("act_chain")
        dve_chain = sem("dve_chain")
        pool_chain = sem("pool_chain")

        block = ctx.enter_context(nc.Block())

        class Chain:

            def __init__(self, e, s):
                self.e, self.s, self.n = e, s, 0

            def link(self, ins):
                ins.then_inc(self.s, 1)
                self.n += 1
                self.e.wait_ge(self.s, self.n)

            def clear(self):
                self.e.sem_clear(self.s)
                self.n = 0

        @block.sync
        def _(sp):
            flat = lambda a, r: a.rearrange("(r n) -> r n", n=P) if r == 1 else a.rearrange("l (r n) -> (l r) n", n=P)
            sp.dma_start(prm_rows[R_CC:R_C, :], flat(c_ctx, 1)).then_inc(loads, 16)
            sp.dma_start(prm_rows[R_C:R_N1, :], flat(c, 2)).then_inc(loads, 16)
            sp.dma_start(const[:, 0:CONST_A], const_d[:, 0:CONST_A]).then_inc(loads, 16)
            sp.dma_start(prm_rows[R_N1:R_N2, :], flat(norm1_w, 2)).then_inc(loads, 16)
            sp.dma_start(prm_rows[R_N2:R_FIN, :], flat(norm2_w, 2)).then_inc(loads, 16)
            sp.dma_start(prm_rows[R_FIN:R_QN, :], flat(final_norm_w, 1)).then_inc(loads, 16)
            for half_ in range(2):
                sp.dma_start(prm_rows[R_QN:R_KN, half_ * HD:(half_ + 1) * HD], q_norm_w).then_inc(loads, 16)
                sp.dma_start(prm_rows[R_KN:R_END, half_ * HD:(half_ + 1) * HD], k_norm_w).then_inc(loads, 16)
            sp.dma_start(bmod_rows[:, :], flat(b_mod, 2)).then_inc(loads, 16)
            for l in range(DEPTH):
                sp.dma_start(conv_rows[:, l, 0:3, :], conv_w[l].rearrange("t (r n) -> r t n", n=P)).then_inc(loads, 16)
                sp.dma_start(conv_rows[:, l, 3, :], conv_b[l].rearrange("(r n) -> r n", n=P)).then_inc(loads, 16)
            sp.dma_start(rows[:, 0, :], x_prompt[0]).then_inc(row_in, 16)
            sp.dma_start(rows[:, 1:NT, :], x_sample[0].rearrange("(t p) n -> p t n", p=P)).then_inc(row_in, 16)
            for v in range(2):
                for k in range(KD):
                    sp.dma_start(m_pre(KD * v + k), w_mod_v[0, :, k, D * v:D * v + D]).then_inc(pre_in[2 * v + k // 4], 16)

            def weights(L, u, srcs):
                for h in range(2):
                    sp.wait_ge(w_split, JOBS * L + 2 * u + h + 1)
                    for dst, src in srcs(h):
                        ins = sp.dma_start(dst, src)
                        ins.then_inc(w_landed[h], 16)

            def stage(h, at, k, cols=256):
                return w_stage[:, h, cols * at:cols * (at + k)].rearrange("p (k n) -> p k n", k=k)

            def square_unit(w, L, col, k=8):
                def srcs(h):
                    n = min(4, k - 4 * h) // 2
                    return [(stage(h, n * b, n), w(L, slice(4 * h + n * b, 4 * h + n * b + n), col)) for b in range(2)]
                return srcs

            def mod_tile(L, n):
                sp.wait_ge(m_used, MT * L + n + 1)
                col = D * (V_G1 + n // KD)
                sp.dma_start(m_stage[:, n % 2, :], w_mod_v[L, :, n % KD, col:col + D]).then_inc(m_landed[n % 2], 16)

            with sp.Fori(0, DEPTH) as L:
                def unit_in(u):
                    if u < 9:
                        weights(L, u, square_unit(lambda l, ks, c0: w_in_v[l, :, ks, c0:c0 + 256], L, IN_COLS[u]))
                    elif u == U_DFTC:
                        weights(L, u, lambda h: [(w_stage[HD * b:HD * b + HD, h, 0:CTX],
                                                  dft_d[HD * b:HD * b + HD, h * CTX:(h + 1) * CTX]) for b in range(2)])
                    else:
                        weights(L, u, lambda h: [(w_stage[:, h, 512 * b:512 * b + 512],
                                                  dft_d[:, 256 + 2048 * (u - U_COS) + 1024 * h + 512 * b:][:, 0:512])
                                                 for b in range(2)])
                unit_in(0)
                with sp.If(L < 1):
                    sp.dma_start(const[:, CONST_A:NCONST], const_d[:, CONST_A:NCONST]).then_inc(const_in, 16)
                sp.wait_ge(h_ok, 16 * L + 8)
                mod_tile(L, 0)
                mod_tile(L, 1)
                sp.dma_start(k_past[:, :, :], cache_k[0, L].rearrange("(t p) g d -> p t (g d)", p=P)).then_inc(kv_in, 16)
                sp.dma_start(v_all[:, 10:14, :], cache_v[0, L].rearrange("(t p) g d -> p t (g d)", p=P)).then_inc(kv_in, 16)
                for e in range(2):
                    sp.dma_start(ret_s0[HD * e:HD * e + HD, :, :, :].rearrange("p r t v -> p (r t) v"),
                                 state_ret[0, L].rearrange("r (t e) d v -> e d (r t) v", e=2)[e]).then_inc(s0_in, 16)
                unit_in(1)
                for u in range(10):
                    unit_in(u + 2)
                    if u < 8:
                        for n in range(4 * u + 2, min(4 * u + 6, MT)):
                            mod_tile(L, n)
                with sp.Fori(0, 2) as i:
                    for s in range(2):
                        weights(L, U_OUT + 2 * i + s,
                                square_unit(lambda l, ks, c0: w_out_v[l, :, ks, bass.ds(c0, 256)], L, 512 * i + 256 * s))
                first = 0
                for n, up, down in zip(CHUNKS, U_UP, U_DOWN):
                    with sp.Fori(0, n // 2) as i:
                        for s in range(2):
                            col = 256 * i + P * (first + s)
                            for h in range(2):
                                sp.wait_ge(w_split, JOBS * L + 4 * i + 2 * (up + s) + h + 1)
                                v = w_up_v.rearrange("l p k (g n) -> l p k g n", g=2)
                                sp.dma_start(w_stage[:, h, :].rearrange("p (k g n) -> p k g n", k=4, g=2)[:, :, 0, :],
                                             v[L, :, 4 * h:4 * h + 4, 0, bass.ds(col, P)]).then_inc(w_landed[h], 16)
                                sp.dma_start(w_stage[:, h, :].rearrange("p (k g n) -> p k g n", k=4, g=2)[:, :, 1, :],
                                             v[L, :, 4 * h:4 * h + 4, 1, bass.ds(col, P)]).then_inc(w_landed[h], 16)
                    with sp.Fori(0, 2) as i:
                        for s in range(2):
                            weights(L, down + 2 * i + s,
                                    square_unit(lambda l, ks, c0: w_down_v[l, :, slice(ks.start + first, ks.stop + first), bass.ds(c0, 256)],
                                                L, 512 * i + 256 * s, k=n))
                    first += n
            sp.wait_ge(sq_used, KD * (2 * DEPTH + 1))
            sp.dma_start(new_k[0].rearrange("l p g d -> p l (g d)"), k_out[:, :, :]).then_inc(stored, 16)
            sp.dma_start(new_v[0].rearrange("l p g d -> p l (g d)"), v_out[:, :, :]).then_inc(stored, 16)
            for e in range(2):
                sp.dma_start(new_s[0].rearrange("l r (t e) d v -> e d (l r t) v", e=2)[e],
                             s_out[HD * e:HD * e + HD].rearrange("p l r t v -> p (l r t) v")).then_inc(stored, 16)
            sp.wait_ge(y_rows, KD)
            sp.dma_start(y_prompt[0], rows[:, 0, :]).then_inc(stored, 16)
            sp.dma_start(y_sample[0].rearrange("(t p) n -> p t n", p=P), rows[:, 1:NT, :]).then_inc(stored, 16)
            sp.wait_ge(stored, 16 * 6)

        @block.tensor
        def _(pe):

            def mm(out, lhs, rhs, start=True, stop=True):
                return pe.matmul(out, lhs, rhs, start=start, stop=stop, skip_group_check=True)

            def take(place, L, name):
                s, order, n = (c_free, C_USE, NC) if place == "C" else (d_free, D_USE, ND)
                pe.wait_ge(s, n * L + order[name] + 1)

            def give(place, ins):
                ins.then_inc(c_done if place == "C" else d_done, 1)

            pe.sem_inc(one, 1)
            pe.sem_inc(a_free, 1)
            pe.sem_inc(b_free, 1)
            pe.sem_inc(c_free, 1)
            pe.sem_inc(d_free, 1)
            pe.sem_inc(w_split, 2)
            pe.sem_inc(job_done, 2)
            pe.sem_inc(m_used, 2)
            pe.sem_inc(qpack, 1)
            pe.sem_inc(exp_ok, 2)
            pe.sem_inc(pt_ok, 2)
            pe.sem_inc(pv_done, 4)
            pe.sem_inc(o_ok, 2)
            pe.sem_inc(g_ok, 1)
            pe.sem_inc(s_done, 8)
            pe.sem_inc(t_done, 12)
            pe.sem_inc(cv_ok, 2)
            pe.sem_inc(gf_ok, 1)
            pe.sem_inc(sg_ok, 1)

            pe.wait_ge(loads, 16 * 15)
            for dst, src, n in [(0, prm_rows[:, :], R_END), (C_BMOD, bmod_rows[:, :], 96)] + \
                    [(C_CONV + 44 * (4 * l + t), conv_rows[:, l, t, :], 44) for l in range(DEPTH) for t in range(4)]:
                ins = pe.transpose(PC[:, dst:dst + n], src, ident[0:n, 0:n])
            ins.then_inc(prm_t, 1)
            pe.wait_ge(row_in, 32)
            for k in range(KD):
                if k >= 2:
                    pe.wait_ge(xt_free, k - 1)
                for t in range(NT):
                    ins = pe.transpose(pair[k % 2][:, P * t:P * t + P], rows[:, t, P * k:P * k + P], ident)
                ins.then_inc(xt_ps, 1)
            def mod_products(to, src, k):
                for j in range(4):
                    ins = mm(to[32 * j:32 * j + 32, :], silu_c[:, k, :], src[:, 256 * j:256 * j + 256], k == 0, k == KD - 1)
                return ins

            def turn_mod():
                for b in range(2):
                    ins = pe.transpose(mod_tp[:, P * b:P * b + P], mod_rows[:, P * b:P * b + P], ident)
                return ins

            pe.wait_ge(silu_ok, 1)
            for v in range(2):
                if v == 1:
                    pe.wait_ge(next_rows, 1)
                    turn_mod().then_inc(next_turned, 1)
                for k in range(KD):
                    if k % 4 == 0:
                        pe.wait_ge(pre_in[2 * v + k // 4], 64)
                    ins = mod_products(mod_ps, m_pre(KD * v + k), k)
                ins.then_inc(next_sums, 1)
            pe.wait_ge(xt_free, KD)
            pe.wait_ge(next_rows, 2)
            pe.wait_ge(next_ok, 1)
            turn_mod().then_inc(next_turned, 1)

            def norm(L, which, at):
                pe.wait_ge(sq_used, at)
                take("C", L, "sum" + which)
                for t in range(NT):
                    ins = mm(PC[:, 768 + t:769 + t], sq_acc[:, P * t:P * t + P], cst("ones"))
                give("C", ins)
                take("C", L, "bc" + which)
                spread(L, PC, which)

            def spread(L, place, which):
                pe.wait_ge(rs_ok, NRS * L + RS_USE["n" + which] + 1)
                for t in range(NT):
                    ins = mm(place[:, P * t:P * t + P], rstd[:, t:t + 1].to_broadcast([P, P]), ident)
                give("C", ins)

            def spread_heads(L, place, name, rs, at=0):
                pe.wait_ge(rs_ok, NRS * L + RS_USE[rs] + 1)
                for t in range(NT):
                    for e in range(2):
                        dst = PC if place == "C" else PD
                        ins = mm(dst[HD * e:HD * e + HD, P * t:P * t + P],
                                 rstd[:, at + 2 * t + e:at + 2 * t + e + 1].to_broadcast([P, HD]), ident)
                give(place, ins)

            def feature_job(L, u, cols, par, last=8, act=(act_hi, act_lo), arrive=None):
                slot = u % 2 if isinstance(u, int) else None
                for k in range(last):
                    if arrive:
                        arrive(k)
                    n = 0
                    for w, a in ((w_hi, act[0]), (w_hi, act[1]), (w_lo, act[0])):
                        for th in range(2):
                            ins = mm(pair[par][:, 512 * th:512 * th + TH], w[:, arrive_slot[0], cols(k)],
                                     a[:, k, TH * th:TH * th + TH], k == 0 and n == 0, k == last - 1 and n == 2)
                        n += 1
                ins.then_inc(job_done, 1)

            arrive_slot = [0]

            def pair_free(L, par, n):
                pe.wait_ge(a_free if par == 0 else b_free, UNITS * L + n + 1)

            def split_wait(L, halves):
                pe.wait_ge(w_split, JOBS * L + halves + 2)

            def square_cols(t):
                return lambda k: slice(256 * k + P * t, 256 * k + P * t + P)

            def token_job(u, tiles, cols, par):
                a, b = cols
                n = b - a
                for i, t in enumerate(tiles):
                    for k in range(KD):
                        m = 0
                        for w, y in ((w_hi, act_hi), (w_hi, act_lo), (w_lo, act_hi)):
                            ins = mm(pair[par][:, n * i:n * i + n], y[:, k, P * t:P * t + P],
                                     w[:, u % 2, 256 * k + a:256 * k + b], k == 0 and m == 0, k == KD - 1 and m == 2)
                            m += 1
                ins.then_inc(job_done, 1)

            def mod_tiles(L, n):
                r = n // KD
                if r and n % KD == 0:
                    pe.wait_ge(m_rows_ok, MOD_ROUNDS * L + r)
                for m in (n, n + 1):
                    pe.wait_ge(m_landed[m % 2], 16 * (MT // 2) * L + 16 * (m // 2) + 16)
                    ins = mod_products(mod_ps, m_stage[:, m % 2, :], m % KD)
                    ins.then_inc(m_used, 1)

            def mod_turned(L, r):
                pe.wait_ge(m_rows_ok, MOD_ROUNDS * L + r + 1)
                take("C", L, f"mod{r}")
                give("C", turn_mod())

            def next_half(L, v, h):
                with pe.If(L < 1):
                    pe.wait_ge(next_in, 64 * (2 * v + h + 1))
                    for k in range(4 * h, 4 * h + 4):
                        ins = mod_products(mod_ps, m_next[:, k % 4, :], k)
                    ins.then_inc(next_used, 1)
                    if h == 1:
                        pe.wait_ge(next_rows, v + 3)
                        pe.wait_ge(next_ok, v + 2)
                        pe.wait_ge(c_free, NC + 1)
                        turn_mod().then_inc(next_turned, 1)

            with pe.Fori(0, DEPTH) as L:
                pe.wait_ge(next_ok, 2 * L + 2)
                norm(L, "1", 2 * KD * L + KD)

                def stat(t):
                    pe.wait_ge(sqq_ok, 5 * L + t + 1)
                    take("D", L, f"st{t}")
                    for i in range(NT):
                        ins = mm(PD[:, 2 * i:2 * i + 2], sqq[:, P * i:P * i + P], cst("blk"))
                    give("D", ins)

                def rotate(t):
                    pe.wait_ge(q_copied if t < 4 else k_normed, (4 * L + t if t < 4 else L) + 1)
                    take("D", L, f"rot{t}")
                    src = qT[:, t, CTX:TOK] if t < 4 else kT[:, CTX:TOK]
                    give("D", mm(PD[:, 0:LAT], cst("rot"), src))

                def tile(u, t, last=8):
                    arrive_slot[0] = u % 2

                    def arrive(k):
                        if u == 0 and t == 0:
                            pe.wait_ge(h_ok, 16 * L + k + 1)
                        if t == 0 and k % 4 == 0:
                            split_wait(L, 2 * u + k // 4 + 1)
                    feature_job(L, u, square_cols(t), t, last, arrive=arrive)

                for u in range(9):
                    for t in range(2):
                        pair_free(L, t, u)
                        if u == U_KV and t == 1:
                            token_job(u, range(NT), (128, 256), 1)
                        elif u in (U_RK, U_RV, U_FX):
                            if t == 0:
                                split_wait(L, 2 * u + 2)
                            token_job(u, range(4) if t == 0 else [4], (0, 256), t)
                        else:
                            tile(u, t)
                        if u < 8:
                            mod_tiles(L, 4 * u + 2 * t)
                        j = 2 * u + t
                        if j >= 4 and j % 4 == 0:
                            mod_turned(L, j // 4 - 1)
                        if 1 <= j <= 5:
                            stat(j - 1)
                        if 2 <= j <= 5:
                            rotate(j - 2)
                        if j == 6:
                            take("C", L, "kbc")
                            spread_heads(L, "C", "kbc", "k")
                        if j == 8:
                            rotate(4)
                            take("D", L, "kct")
                            give("D", pe.transpose(PD[:, 0:P], kT[:, 0:CTX], ident))
                            pe.wait_ge(kv_in, 32 * L + 32)
                            take("D", L, "kcache")
                            for i in range(2):
                                ins = pe.transpose(PD[:, P * i:P * i + P], k_past[:, i, :], ident)
                            give("D", ins)
                        if j == 10:
                            pe.wait_ge(tok_ok, 2 * L + 2)
                            for i in range(2):
                                take("C", L, f"rkt{i}")
                                for n in range(NT):
                                    ins = pe.transpose(PC[:, P * n:P * n + P], rk[:, n, P * i:P * i + P], ident)
                                give("C", ins)

                pe.wait_ge(fx_ok, 2 * L + 2)
                for u in (U_DFTC, U_COS, U_SIN):
                    for t in range(2):
                        pair_free(L, t, u)
                        if t == 0:
                            split_wait(L, 2 * u + 2)
                        m = 0
                        for w, y in ((w_hi, fx_hi), (w_hi, fx_lo), (w_lo, fx_hi)):
                            if u == U_DFTC:
                                for h in range(2):
                                    ins = mm(pair[t][:, 512 * h:512 * h + CTX], y[:, 0, P * t:P * t + P],
                                             w[:, u % 2, 1024 * h:1024 * h + CTX], m == 0, m == 2)
                            else:
                                for k in range(4):
                                    ins = mm(pair[t][:, 0:LAT], y[:, 1 + k, P * t:P * t + P],
                                             w[:, u % 2, 512 * k:512 * k + 512], m == 0 and k == 0, m == 2 and k == 3)
                            m += 1
                        ins.then_inc(job_done, 1)
                pe.wait_ge(y_ok, 6 * L + 6)
                for t in range(2):
                    take("C", L, f"four{t}")
                    mm(PC[:, 0:LAT], cst("c64l"), dft_y[:, t, 0, :], True, False)
                    mm(PC[:, 0:LAT], cst("s64l"), dft_y[:, t, 1, :], False, True)
                    mm(PC[:, LAT:TOK], cst("c64c"), dft_yc[:, t, 0, :], True, False)
                    give("C", mm(PC[:, LAT:TOK], cst("s64c"), dft_yc[:, t, 1, :], False, True))

                def at_product(t, e):
                    take("C", L, f"at{t}{e}")
                    rows_ = slice(HD * e, HD * e + HD)
                    for n in range(NT):
                        ins = mm(PC[:, P * n:P * n + P], rkT[rows_, t, P * n:P * n + P], rqT[rows_, t, P * n:P * n + P])
                    give("C", ins)

                def within(t, e):
                    pe.wait_ge(adec_ok, 4 * L + 2 * t + e + 1)
                    if e == 1:
                        pe.wait_ge(st_ok, 2 * L + t + 1)
                    for r in range(2):
                        for n in range(NT):
                            ins = mm(pair[r][HD * e:HD * e + HD, P * n:P * n + P],
                                     rv[:, n, P * t + HD * e:P * t + HD * e + HD], a_dec[e][:, r, P * n:P * n + P],
                                     n in (0, 4), False)
                    ins.then_inc(adec_used, 1)

                def updates(t):
                    pe.wait_ge(kdec_ok, 2 * L + t + 1)
                    take("D", L, f"u{t}")
                    for r, chunks in enumerate(((0, 1, 2, 3), (0, 2, 3, 4))):
                        for i, n in enumerate(chunks):
                            ins = mm(PD[:, 512 * r + P * i:512 * r + P * i + P], k_dec[:, r, n, :],
                                     rv[:, n, P * t:P * t + P])
                    give("D", ins)

                def across(t):
                    for r in range(2):
                        for e in range(2):
                            rows_ = slice(HD * e, HD * e + HD)
                            for n in range(4):
                                ins = mm(pair[r][rows_, P * (n + 1):P * (n + 2)], ret_st[rows_, r, n, :],
                                         q_dec[rows_, r, P * n:P * n + P], False, True)
                    ins.then_inc(o_ps, 1)

                def centre(t, r):
                    pe.wait_ge(o_copied, 4 * L + 2 * t + r + 1)
                    take("C", L, f"cen{t}{'fb'[r]}")
                    mm(PC[:, 0:512], cst("center"), o_sb[:, r, 0:512])
                    give("C", mm(PC[:, 512:TOK], cst("center"), o_sb[:, r, 512:TOK]))

                def variances(t):
                    pe.wait_ge(osq_ok, 4 * L + 2 * t + 2)
                    take("D", L, f"ty{t}")
                    for r in range(2):
                        for n in range(NT):
                            at = 2 * NT * r + 2 * n
                            ins = mm(PD[:, at:at + 2], o_sq[:, r, P * n:P * n + P], cst("blk"))
                    give("D", ins)

                def spread_powers(t, r):
                    take("D", L, f"by{t}{'fb'[r]}")
                    spread_heads(L, "D", f"by{t}{'fb'[r]}", f"r{t}", 2 * NT * r)

                at_product(0, 0)
                updates(0)
                at_product(0, 1)
                pair_free(L, 0, 12)
                pair_free(L, 1, 12)
                pe.wait_ge(rv_ok, 2 * L + 2)
                within(0, 0)
                at_product(1, 0)
                within(0, 1)
                across(0)
                at_product(1, 1)
                updates(1)
                pe.wait_ge(o_copied, 4 * L + 2)
                within(1, 0)
                centre(0, 0)
                within(1, 1)
                centre(0, 1)
                across(1)
                variances(0)
                centre(1, 0)
                spread_powers(0, 0)
                centre(1, 1)
                spread_powers(0, 1)
                variances(1)

                take("C", L, "sctx")
                pe.wait_ge(kp_ok, L + 1)
                for n in range(HEADS):
                    e, t, g = n // 4, n % 4, n % 4 // 2
                    ins = mm(PC[:, P * n:P * n + P], qT[HD * e:HD * e + HD, t, 0:CTX], kc[HD * e:HD * e + HD, g, :])
                give("C", ins)
                spread_powers(1, 0)
                spread_powers(1, 1)
                pe.wait_ge(dgc_ok, L + 1)
                pe.wait_ge(o_copied, 4 * L + 4)
                for h in range(HEADS):
                    ins = mm(PA[:, P * h:P * h + P], probs_c[:, P * h:P * h + P], diag[:, h // 4, h % 4, :])
                ins.then_inc(tc_ps, 1)
                pe.wait_ge(ptc_ok, L + 1)
                for n in range(HEADS):
                    e, t, g = n // 4, n % 4, n % 4 // 2
                    ins = mm(PB_[HD * e:HD * e + HD, P * t:P * t + P], v_all[:, g, :],
                             probs_t[:, e, P * t:P * t + P])
                ins.then_inc(oc_ps, 1)

                with pe.Fori(0, 2) as i:
                    def scores(q, b):
                        n = 4 * q + b
                        g = q // 2
                        if b == 0:
                            pe.wait_ge(qpack, 8 * L + 4 * i + q + 2)
                        pe.wait_ge(exp_ok, 32 * L + 16 * i + n + 1)
                        dst = pair[2 + b % 2]
                        for lo, hi in ((0, 512), (512, KEYS)):
                            mm(dst[:, lo:hi], qq[:, q % 2, P * b:P * b + P], kp[:, g, lo:hi], True, False)
                            ins = mm(dst[:, lo:hi], q_lo[:, q % 2, P * b:P * b + P], kp[0:HD, g, lo:hi], False, True)
                        ins.then_inc(s_done, 1)

                    def turned(q, t):
                        n = 6 * q + t
                        if t == 0:
                            pe.wait_ge(dg_ok, 32 * L + 16 * i + 4 * q + 4)
                        pe.wait_ge(pt_ok, 48 * L + 24 * i + n + 1)
                        for b in range(4):
                            ins = mm(psum[:, 2 * (n % 2), P * b:P * b + P], probs[:, q % 2, b, P * t:P * t + P],
                                     diag[:, q % 2, b, :])
                        ins.then_inc(t_done, 1)

                    def values(q, t):
                        n = 6 * q + t
                        e, g = q % 2, q // 2
                        blk = 10 + 2 * t + g if t < 2 else 2 * (t - 1) + g
                        if t == 0:
                            pe.wait_ge(o_ok, 8 * L + 4 * i + q + 1)
                        pe.wait_ge(pt_ok, 48 * L + 24 * i + n + 3)
                        mm(psum[HD * e:HD * e + HD, 2 * (q % 2) + 1, :], v_all[:, blk, :], probs_t[:, n % 4, :],
                           t == 0, t == NKT - 1).then_inc(pv_done, 1)

                    pe.wait_ge(c_free, NC * L + C_USE["sctx"] + 2)
                    pe.wait_ge(d_free, ND * L + ND + 1)
                    pe.wait_ge(oc_ok, L + 1)
                    for b in range(4):
                        scores(0, b)
                    for q in range(4):
                        for t in range(NKT):
                            turned(q, t)
                            if t >= 1:
                                values(q, t - 1)
                            if q < 3 and t < 4:
                                scores(q + 1, t)
                        values(q, NKT - 1)

                def square_units(first, k, act):
                    with pe.Fori(0, 2) as i:
                        if act is None:
                            pe.wait_ge(o_ok, 8 * L + 10)
                            pe.wait_ge(ret_sum, 2 * L + 2)
                        for s in range(2):
                            u = first + s
                            arrive_slot[0] = u % 2
                            for t in range(2):
                                pe.wait_ge(a_free if t == 0 else b_free, UNITS * L + 2 * i + u + 1)

                                def arrive(kk, u=u, t=t, s=s):
                                    if act is not None and s == 0 and t == 0:
                                        act(kk)
                                    if t == 0 and kk % 4 == 0:
                                        pe.wait_ge(w_split, JOBS * L + 4 * i + 2 * u + kk // 4 + 3)
                                feature_job(L, u, square_cols(t), t, k, (act_hi, act_lo) if act is None else (g_hi, g_lo), arrive)
                square_units(U_OUT, 8, None)
                norm(L, "2", 2 * KD * L + 2 * KD)

                first = 0
                for v, n, up, down in zip(range(3), CHUNKS, U_UP, U_DOWN):
                    with pe.Fori(0, n // 2) as i:
                        for s in range(2):
                            u = up + s
                            arrive_slot[0] = u % 2
                            for t in range(2):
                                pe.wait_ge(a_free if t == 0 else b_free, UNITS * L + 2 * i + u + 1)

                                def arrive(k, u=u, t=t, s=s):
                                    if first == 0 and s == 0 and t == 0:
                                        pe.wait_ge(h_ok, 16 * L + 8 + k + 1)
                                    if t == 0 and k % 4 == 0:
                                        pe.wait_ge(w_split, JOBS * L + 4 * i + 2 * u + k // 4 + 3)
                                feature_job(L, u, square_cols(t), t, 8, arrive=arrive)
                    if v < 2:
                        next_half(L, v, 0)
                    square_units(down, n, lambda k, first=first: pe.wait_ge(g_ok, NJ * L + first + k + 2))
                    if v < 2:
                        next_half(L, v, 1)
                    first += n

            pe.wait_ge(sq_used, KD * (2 * DEPTH + 1))
            pe.wait_ge(c_free, NC * DEPTH + 1)
            for t in range(NT):
                ins = mm(PC[:, 768 + t:769 + t], sq_acc[:, P * t:P * t + P], cst("ones"))
            ins.then_inc(c_done, 1)
            pe.wait_ge(rs_ok, NRS * DEPTH + 1)
            for t in range(NT):
                ins = mm(PC[:, P * t:P * t + P], rstd[:, t:t + 1].to_broadcast([P, P]), ident)
            ins.then_inc(c_done, 1)
            for k in range(KD):
                pe.wait_ge(y_col, k + 1)
                if k >= 2:
                    pe.wait_ge(y_rows, k - 1)
                for t in range(NT):
                    ins = pe.transpose(pair[k % 2][:, P * t:P * t + P], y_t[:, k % 2, P * t:P * t + P], ident)
                ins.then_inc(y_row, 1)

        @block.scalar
        def _(act):
            chain = Chain(act, act_chain)

            def halves(par):
                return psum[:, 2 * par:2 * par + 2, 0:TH]

            def split(L, u, i=None, width=1024):
                more = 0 if i is None else i
                for h in range(2):
                    act.wait_ge(w_landed[h], 32 * UNITS * L + 32 * (u + 1) + 64 * more)
                    if h == 0:
                        act.wait_ge(job_done, JOBS * L + 2 * u + 4 * more)
                    act.activation(w_hi[:, u % 2, 1024 * h:1024 * h + width], w_stage[:, h, 0:width],
                                   ACT.Copy).then_inc(w_hi_ok, 1)

            def split_first(L):
                for h in range(2):
                    act.wait_ge(w_landed[h], 32 * UNITS * L + 32)
                    act.activation(w_hi[:, 0, 1024 * h:1024 * h + 1024], w_stage[:, h, :], ACT.Copy).then_inc(w_hi_ok, 1)

            def squares(L, m, at):
                act.wait_ge(x_new, 2 * KD * L + at + m + 1)
                act.wait_ge(sq_used, 2 * KD * L + at + m - 1)
                return act.activation

            def norm(L, first, at):
                for k in range(KD):
                    act.wait_ge(tn_ok, 2 * KD * L + at + k + 1)
                    if k >= 2:
                        act.wait_ge(h_ok, 2 * KD * L + at + k - 1)
                    sc = scale1 if first == 0 else scale2
                    act.activation(hf[:, k % 2, 0:CTX], tn[:, k % 2, 0:CTX], ACT.Identity,
                                   bias=mod[:, first + k, 0:1], scale=sc[:, k, 0:1])
                    chain.link(act.activation(hf[:, k % 2, CTX:TOK], tn[:, k % 2, CTX:TOK], ACT.Identity,
                                              bias=mod[:, first + k, 1:2], scale=sc[:, k, 1:2]))
                    act.activation(act_hi[:, k, :], hf[:, k % 2, :], ACT.Copy).then_inc(h_hi_ok, 1)

            act.wait_ge(prm_ok, 1)
            act.activation(silu_c[:, :, 0:2].rearrange("p k s -> p s k"),
                           prm[:, R_CC:R_N1].rearrange("p (s k) -> p s k", s=2), ACT.Silu).then_inc(silu_ok, 1)
            for k in range(KD):
                act.wait_ge(x_new, k + 1)
                if k >= 2:
                    act.wait_ge(sq_used, k - 1)
                act.activation(sq[:, k % 2, :], x[:, k, :], ACT.Square).then_inc(sq_ok, 1)
            for v in range(2):
                act.wait_ge(next_sums, v + 1)
                if v == 1:
                    act.wait_ge(next_turned, 1)
                act.activation(mod_rows[:, :], mod_ps, ACT.Copy).then_inc(next_rows, 1)

            with act.Fori(0, DEPTH) as L:
                chain.clear()
                split_first(L)
                norm(L, 0, 0)
                for u in range(9):
                    split(L, u + 1, width=CTX if u + 1 == U_DFTC else 1024)
                    for t in range(2):
                        j = 2 * u + t
                        act.wait_ge(job_done, JOBS * L + j + 3)
                        free = a_free if t == 0 else b_free
                        if j <= 4:
                            dst, w = (qT[:, j, :], 0) if j < 4 else (kT[:, :], 1)
                            copied = act.activation(dst.rearrange("p (h n) -> p h n", h=2), halves(t), ACT.Identity,
                                                    bias=0.0, scale=qk_w[:, w:w + 1])
                            if j < 4:
                                copied.then_inc(q_copied, 1)
                            if j >= 1:
                                act.wait_ge(d_done, ND * L + D_USE[f"st{j - 1}"] + 1)
                            chain.link(act.activation(sqq[:, :].rearrange("p (h n) -> p h n", h=2), halves(t), ACT.Square))
                            act.sem_inc(sqq_ok, 1)
                            act.sem_inc(free, 1)
                        elif j == 5:
                            act.activation(v_out[:, L, :], PB_[:, 0:P], ACT.Copy)
                            act.activation(v_all[:, 0:10, :].rearrange("p b n -> p (b n)"), PB_[:, 0:TOK],
                                           ACT.Copy).then_inc(free, 1)
                        elif u == U_RQ:
                            act.activation(rqT[:, t, :].rearrange("p (h n) -> p h n", h=2), halves(t),
                                           ACT.Copy).then_inc(free, 1)
                        elif u == U_RK:
                            dst = rk[:, 0:4, :] if t == 0 else rk[:, 4:5, :]
                            n = 1024 if t == 0 else 256
                            chain.link(act.activation(dst.rearrange("p b n -> p (b n)"), pair[t][:, 0:n],
                                                      ACT.Copy, scale=HD ** -0.5))
                            act.sem_inc(tok_ok, 1)
                            act.sem_inc(free, 1)
                        elif u == U_FX:
                            dst = fx_hi[:, 0:4, :] if t == 0 else fx_hi[:, 4:5, :]
                            n = 1024 if t == 0 else 256
                            act.activation(dst.rearrange("p b n -> p (b n)"), pair[t][:, 0:n],
                                           ACT.Copy).then_inc(fx_hi_ok, 1)
                        elif u in (U_GF, U_GB):
                            act.activation(gate[:, u - U_GF, t, :].rearrange("p (h n) -> p h n", h=2), halves(t),
                                           ACT.Silu).then_inc(free, 1)
                        if j < 16 and j % 4 == 3:
                            r = j // 4
                            act.wait_ge(m_used, MT * L + KD * r + KD + 2)
                            if r:
                                act.wait_ge(c_done, NC * L + C_USE[f"mod{r - 1}"] + 1)
                            act.activation(mod_rows[:, :], mod_ps, ACT.Copy).then_inc(m_rows_ok, 1)
                act.wait_ge(kp_ok, L + 1)
                for u in (U_DFTC, U_COS, U_SIN):
                    split(L, u + 1)
                    for t in range(2):
                        act.wait_ge(job_done, JOBS * L + 2 * u + t + 3)
                        free = a_free if t == 0 else b_free
                        if u == U_DFTC:
                            ins = act.activation(dft_yc[:, t, :, :], psum[:, 2 * t:2 * t + 2, 0:CTX], ACT.Copy)
                        else:
                            ins = act.activation(dft_y[:, t, u - U_COS, :], pair[t][:, 0:LAT], ACT.Copy)
                        chain.link(ins)
                        act.sem_inc(y_ok, 1)
                        act.sem_inc(free, 1)
                for t in range(2):
                    act.wait_ge(c_done, NC * L + C_USE[f"four{t}"] + 1)
                    act.activation(act_hi[:, 6 + t, CTX:TOK], PC[:, 0:LAT], ACT.Copy)
                    act.activation(act_hi[:, 6 + t, 0:CTX], PC[:, LAT:TOK], ACT.Copy).then_inc(four_hi, 1)

                def copies(t):
                    act.wait_ge(o_ps, 2 * L + t + 1)
                    for r in range(2):
                        act.activation(o_sb[:, r, :], pair[r][:, 0:TOK], ACT.Copy).then_inc(o_copied, 1)

                def osquares(t):
                    for r, w in enumerate("fb"):
                        act.wait_ge(c_done, NC * L + C_USE[f"cen{t}{w}"] + 1)
                        act.activation(o_sq[:, r, :], PC[:, 0:TOK], ACT.Square).then_inc(osq_ok, 1)

                def leading(t):
                    act.wait_ge(ret_hi, 2 * L + t + 1)
                    act.activation(act_hi[:, 4 + t, :], o_g[t][:, 0, :], ACT.Copy).then_inc(c_read, 1)

                copies(0)
                osquares(0)
                copies(1)
                osquares(1)
                leading(0)

                act.wait_ge(nbc_ok, L + 1)
                for h in range(HEADS):
                    ins = act.activation(probs_c[:, P * h:P * h + P], PC[:, P * h:P * h + P], ACT.Exp, bias=nbc[:, h:h + 1],
                                         scale=q_rs[:, h % 4, 0, h // 4:h // 4 + 1], accum_out=rsc[:, h:h + 1])
                ins.then_inc(expc_ok, 1)
                leading(1)
                act.wait_ge(oc_ps, L + 1)
                act.activation(act_hi[:, 0:4, 0:CTX], PB_[:, 0:512].rearrange("p (t n) -> p t n", t=4),
                               ACT.Copy).then_inc(oc_hi, 1)

                with act.Fori(0, 2) as i:
                    chain.clear()

                    def prepare(q):
                        e, t = q % 2, i + 2 * (q // 2)
                        act.wait_ge(qpack, 8 * L + 4 * i + q + 1)
                        for half_ in range(2):
                            ins = act.activation(q2[HD * half_:HD * half_ + HD, :], qT[HD * e:HD * e + HD, t, CTX:TOK], ACT.Copy)
                        chain.link(ins)
                        act.wait_ge(s_done, 32 * L + 16 * i + 4 * q + 4)
                        act.activation(qq[:, q % 2, :], q2[:, :], ACT.Copy).then_inc(qhi_ok, 1)

                    def exps(q):
                        act.wait_ge(t_done, 48 * L + 24 * i + 6 * q + 6)
                        for b in range(4):
                            act.wait_ge(nb_ok, 32 * L + 16 * i + 4 * q + b + 1)
                            at = 4 * (q % 2) + b
                            act.activation(probs[:, q % 2, b, :], pair[2 + b % 2][:, 0:KEYS], ACT.Exp, bias=nb[:, at:at + 1],
                                           scale=q_rs[:, i + 2 * (q // 2), 1 + b, q % 2:q % 2 + 1],
                                           accum_out=rsum[:, at:at + 1]).then_inc(exp_ok, 1)

                    def output(q):
                        e, t = q % 2, i + 2 * (q // 2)
                        act.wait_ge(pv_done, 48 * L + 24 * i + 6 * q + 10)
                        act.activation(act_hi[HD * e:HD * e + HD, t, CTX:TOK],
                                       psum[HD * e:HD * e + HD, 2 * (q % 2) + 1, :], ACT.Copy).then_inc(o_hi, 1)

                    prepare(0)
                    exps(0)
                    prepare(1)
                    for q in range(1, 4):
                        exps(q)
                        if q < 3:
                            prepare(q + 1)
                        output(q - 1)
                    output(3)

                def square_units(first, at, last=False):
                    def two(i, more):
                        for s in range(2):
                            if not (last and isinstance(i, int) and i == 1 and s == 1):
                                split(L, first + s + 1 + (2 * i if isinstance(i, int) else 0), None if isinstance(i, int) else i)
                            if at is not None:
                                for t in range(2):
                                    m = 4 * i + 2 * s + t
                                    act.wait_ge(x_new, 2 * KD * L + at + m + 1)
                                    act.wait_ge(sq_used, 2 * KD * L + at + m - 1)
                                    act.activation(sq[:, t, :], x[:, m, :], ACT.Square).then_inc(sq_ok, 1)
                    if last:
                        two(0, None)
                        two(1, None)
                    else:
                        with act.Fori(0, 2) as i:
                            two(i, None)

                square_units(U_OUT, KD)
                chain.clear()
                norm(L, 24, KD)
                first = 0
                for v, n, up, down in zip(range(3), CHUNKS, U_UP, U_DOWN):
                    with act.Fori(0, n // 2) as i:
                        chain.clear()
                        for s in range(2):
                            split(L, up + s + 1, i)
                            for t in range(2):
                                act.wait_ge(job_done, JOBS * L + 2 * (up + s) + t + 3 + 4 * i)
                                act.wait_ge(cv_ok, 2 * NJ * L + 4 * i + 2 * (first + s) + t + 1)
                                act.activation(u_sb[:, t, 1:1 + CTX], pair[t][:, 0:CTX], ACT.Copy)
                                act.activation(u_sb[:, t, 2 + CTX:2 + TH], pair[t][:, CTX:TH], ACT.Copy)
                                ins = act.activation(u_sb[:, t, 2 + TH:2 + TOK], pair[t][:, 512:512 + TH], ACT.Copy)
                                chain.link(ins)
                                act.sem_inc(u_ok, 1)
                                act.sem_inc(a_free if t == 0 else b_free, 1)
                            act.wait_ge(cv_ok, 2 * NJ * L + 4 * i + 2 * (first + s) + 3)
                            act.wait_ge(gf_ok, NJ * L + 2 * i + first + s + 1)
                            act.activation(sg[:, 1:2 + TOK], cv[:, 0, 1:2 + TOK], ACT.Silu).then_inc(sg_ok, 1)
                            act.wait_ge(gf_ok, NJ * L + 2 * i + first + s + 2)
                            act.activation(g_hi[:, 2 * i + s, :], gf[:, :], ACT.Copy).then_inc(g_hi_ok, 1)
                    first += n
                    square_units(down, 2 * KD if first == NJ else None, last=first == NJ)
                    if v < 2:
                        with act.If(L < 1):
                            act.wait_ge(next_used, 2 * v + 2)
                            act.activation(mod_rows[:, :], mod_ps, ACT.Copy).then_inc(next_rows, 1)

        @block.vector
        def _(dve):
            chain = Chain(dve, dve_chain)

            def tell(ins, *sems):
                chain.link(ins)
                for s in sems:
                    dve.sem_inc(s, 1)

            def split(L, u, i=None, width=1024):
                for h in range(2):
                    dve.wait_ge(w_hi_ok, JOBS * L + 2 * u + h + 1 + (0 if i is None else 4 * i))
                    cols = slice(1024 * h, 1024 * h + width)
                    dve.tensor_tensor(w_lo[:, u % 2, cols], w_stage[:, h, 0:width], w_hi[:, u % 2, cols].bitcast(F32),
                                      ALU.subtract).then_inc(w_split, 1)

            def add_squares(L, m, slot, at):
                dve.wait_ge(sq_ok, 2 * KD * L + at + m + 1)
                tell(dve.tensor_tensor(sq_acc[:, :], sq_acc[:, :], sq[:, slot, :], ALU.add), sq_used)

            def norm(L, which, at):
                dve.wait_ge(c_done, NC * L + C_USE["sum" + which] + 1)
                if which == "2":
                    dve.wait_ge(rs_ok, NRS * L + RS_USE["n2"])
                tell(dve.tensor_scalar(vsum[:, 0:NT], PC[:, 768:768 + NT], EPS, None, ALU.add), v_ok, c_free)
                dve.wait_ge(c_done, NC * L + C_USE["bc" + which] + 1)
                for k in range(KD + 1):
                    if k < KD:
                        if k >= 2:
                            dve.wait_ge(h_hi_ok, 2 * KD * L + at + k - 1)
                        ins = dve.tensor_tensor(tn[:, k % 2, :], x[:, k, :], PC[:, 0:TOK], ALU.mult)
                        if k == KD - 1:
                            tell(ins, tn_ok, c_free)
                        else:
                            ins.then_inc(tn_ok, 1)
                    if k >= 1:
                        dve.wait_ge(h_hi_ok, 2 * KD * L + at + k)
                        dve.tensor_tensor(act_lo[:, k - 1, :], hf[:, (k - 1) % 2, :], act_hi[:, k - 1, :].bitcast(F32),
                                          ALU.subtract).then_inc(h_ok, 1)

            dve.memset(silu_c[:, :, :], 0.0)
            dve.wait_ge(prm_t, 1)
            chain.link(dve.tensor_copy(prm[:, :], PC[:, 0:NPRM]))
            dve.sem_inc(prm_ok, 1)
            dve.memset(sq_acc[:, :], 0.0)
            for k in range(KD):
                dve.wait_ge(xt_ps, k + 1)
                tell(dve.tensor_copy(x[:, k, :], pair[k % 2][:, 0:TOK]), xt_free, x_new)
                if k >= 1:
                    dve.wait_ge(sq_ok, k)
                    tell(dve.tensor_tensor(sq_acc[:, :], sq_acc[:, :], sq[:, (k - 1) % 2, :], ALU.add), sq_used)
            dve.wait_ge(sq_ok, KD)
            tell(dve.tensor_tensor(sq_acc[:, :], sq_acc[:, :], sq[:, (KD - 1) % 2, :], ALU.add), sq_used)

            def by_group(v, n):
                return v.rearrange("p (t o) -> p t o", o=1).to_broadcast([P, n, 2])

            def add_bias(dst, bias):
                src = mod_tp.rearrange("p (b j q) -> p j b q", b=2, j=4)[:, :, :, 0:2]
                return dve.tensor_tensor(dst.rearrange("p (j b) s -> p j b s", j=4), src,
                                         bias.rearrange("p (j b o) -> p j b o", j=4, o=1).to_broadcast([P, 4, 2, 2]), ALU.add)

            for v in range(2):
                dve.wait_ge(next_turned, v + 1)
                tell(add_bias(mod_next[:, KD * v:KD * v + KD, :], prm[:, C_BMOD + KD * v:C_BMOD + KD * v + KD]), next_ok)

            with dve.Fori(0, DEPTH) as L:
                chain.clear()
                dve.wait_ge(next_ok, 2 * L + 2)
                dve.tensor_copy(mod[:, 0:2 * KD, :], mod_next[:, :, :])
                dve.tensor_copy(bmod_l[:, :], prm[:, bass.ds(48 * L + C_BMOD, 48)])
                dve.tensor_copy(n2_l[:, :], prm[:, bass.ds(KD * L + R_N2, KD)])
                dve.tensor_copy(conv_l[:, :, :].rearrange("p a b -> p (a b)"), prm[:, bass.ds(176 * L + C_CONV, 176)])
                dve.tensor_copy(qk_w[:, 0:1], prm[:, bass.ds(L + R_QN, 1)])
                dve.tensor_copy(qk_w[:, 1:2], prm[:, bass.ds(L + R_KN, 1)])
                chain.link(dve.tensor_copy(vsum[:, 0:KD], prm[:, bass.ds(KD * L + R_N1, KD)]))
                chain.link(dve.scalar_tensor_tensor(scale1[:, :, :], mod[:, KD:2 * KD, :], 1.0, by_group(vsum[:, 0:KD], KD),
                                                    ALU.add, ALU.mult))
                split(L, 0)
                norm(L, "1", 0)

                def rope(t, src):
                    dve.wait_ge(d_done, ND * L + D_USE[f"rot{t}"] + 1)
                    chain.link(dve.tensor_tensor(src, src, cst("cos"), ALU.mult))
                    tell(dve.tensor_tensor(rtmp[:, :], PD[:, 0:LAT], cst("sin"), ALU.mult), d_free)
                    chain.link(dve.tensor_tensor(src, src, rtmp[:, :], ALU.add))

                def powers(t):
                    dve.wait_ge(d_done, ND * L + D_USE[f"st{t}"] + 1)
                    dve.wait_ge(rs_ok, NRS * L + RS_USE[f"q{t}" if t < 4 else "k"])
                    k = float(HD) if t < 4 else 1.0
                    tell(dve.tensor_scalar(vsum[:, 0:2 * NT], PD[:, 0:2 * NT], k, k * EPS, ALU.mult, ALU.add), v_ok, d_free)

                for u in range(9):
                    split(L, u + 1, width=CTX if u + 1 == U_DFTC else 1024)
                    for t in range(2):
                        j = 2 * u + t
                        if j >= 4 and j % 4 == 0:
                            r = j // 4 - 1
                            dve.wait_ge(c_done, NC * L + C_USE[f"mod{r}"] + 1)
                            at = KD * (V_G1 + r)
                            tell(add_bias(mod[:, at:at + KD, :], bmod_l[:, at:at + KD]), c_free)
                        if 1 <= j <= 5:
                            powers(j - 1)
                        if j == 2:
                            dve.wait_ge(const_in, 16)
                        if 2 <= j <= 5:
                            rope(j - 2, qT[:, j - 2, CTX:TOK])
                        if j == 6:
                            dve.wait_ge(c_done, NC * L + C_USE["kbc"] + 1)
                            tell(dve.tensor_tensor(kT[:, :], kT[:, :], PC[:, 0:TOK], ALU.mult), c_free, k_normed)
                        if j == 8:
                            for g in range(2):
                                for half_ in range(2):
                                    dve.tensor_copy(kc[HD * half_:HD * half_ + HD, g, :], kT[HD * g:HD * g + HD, 0:CTX])
                            rope(4, kT[:, CTX:TOK])
                            dve.wait_ge(d_done, ND * L + D_USE["kct"] + 1)
                            tell(dve.tensor_copy(k_out[:, L, :], PD[:, 0:P]), d_free)
                            dve.wait_ge(d_done, ND * L + D_USE["kcache"] + 1)
                            for g in range(2):
                                rows_ = slice(HD * g, HD * g + HD)
                                for half_ in range(2):
                                    to = slice(HD * half_, HD * half_ + HD)
                                    dve.tensor_copy(k2[to, 0:PAST], PD[rows_, 0:PAST])
                                    ins = dve.tensor_copy(k2[to, PAST:KEYS], kT[rows_, CTX:TOK])
                                tell(ins, *([d_free] if g else []))
                                dve.tensor_copy(kp[0:HD, g, :], k2[0:HD, :])
                                chain.link(dve.tensor_copy(k2_hi[:, :], k2[:, :]))
                                chain.link(dve.tensor_tensor(kp[HD:P, g, :], k2[HD:P, :], k2_hi[HD:P, :].bitcast(F32), ALU.subtract))
                            dve.sem_inc(kp_ok, 1)
                        if u == U_RV:
                            dve.wait_ge(job_done, JOBS * L + j + 3)
                            dst, n = (rv[:, 0:4, :], 1024) if t == 0 else (rv[:, 4:5, :], 256)
                            tell(dve.tensor_copy(dst.rearrange("p b n -> p (b n)"), pair[t][:, 0:n]), rv_ok,
                                 a_free if t == 0 else b_free)
                            dve.wait_ge(c_done, NC * L + C_USE[f"rkt{t}"] + 1)
                            dve.tensor_copy(rkT[:, t, :], PC[:, 0:TOK]).then_inc(c_free, 1)
                        if u == U_FX:
                            dve.wait_ge(fx_hi_ok, 2 * L + t + 1)
                            dst, src, n = (fx_lo[:, 0:4, :], fx_hi[:, 0:4, :], 1024) if t == 0 else (fx_lo[:, 4:5, :], fx_hi[:, 4:5, :], 256)
                            tell(dve.tensor_tensor(dst.rearrange("p b n -> p (b n)"), pair[t][:, 0:n],
                                                   src.rearrange("p b n -> p (b n)").bitcast(F32), ALU.subtract), fx_ok,
                                 a_free if t == 0 else b_free)
                chain.link(dve.scalar_tensor_tensor(scale2[:, :, :], mod[:, 32:40, :], 1.0, by_group(n2_l[:, :], KD), ALU.add, ALU.mult))
                for u in (U_DFTC, U_COS, U_SIN):
                    split(L, u + 1)
                for t in range(2):
                    dve.wait_ge(four_hi, 2 * L + t + 1)
                    dve.tensor_tensor(act_lo[:, 6 + t, CTX:TOK], PC[:, 0:LAT], act_hi[:, 6 + t, CTX:TOK].bitcast(F32), ALU.subtract)
                    dve.tensor_tensor(act_lo[:, 6 + t, 0:CTX], PC[:, LAT:TOK], act_hi[:, 6 + t, 0:CTX].bitcast(F32),
                                      ALU.subtract).then_inc(c_free, 1)

                def keys_decayed(t):
                    if t == 1:
                        dve.wait_ge(d_done, ND * L + D_USE["u0"] + 1)
                    for r, name in enumerate(("kdf", "kdb")):
                        w = cst(name, P * t, P * t + P).rearrange("p (o n) -> p o n", o=1).to_broadcast([P, NT, P])
                        ins = dve.tensor_tensor(k_dec[:, r, :, :], rk[:, :, P * t:P * t + P], w, ALU.mult)
                    tell(ins, kdec_ok)

                def queries_decayed(t):
                    if t == 1:
                        dve.wait_ge(o_ps, 2 * L + 1)
                    for r, name in enumerate(("qdf", "qdb")):
                        w = cst(name, P * t, P * t + P).rearrange("p (o n) -> p o n", o=1).to_broadcast([P, 4, P])
                        ins = dve.tensor_tensor(q_dec[:, r, :].rearrange("p (c n) -> p c n", c=4),
                                                rqT[:, t, CTX:TOK].rearrange("p (c n) -> p c n", c=4), w, ALU.mult)
                    chain.link(ins)

                def masked(t, e):
                    dve.wait_ge(c_done, NC * L + C_USE[f"at{t}{e}"] + 1)
                    if t:
                        dve.wait_ge(adec_used, 4 * L + e + 1)
                    for r, name in enumerate(("maskf", "maskb")):
                        h = 2 * t + e
                        w = cst(name, P * h, P * h + P).rearrange("p (o n) -> p o n", o=1).to_broadcast([P, NT, P])
                        ins = dve.tensor_tensor(a_dec[e][:, r, :].rearrange("p (c n) -> p c n", c=NT),
                                                PC[:, 0:TOK].rearrange("p (c n) -> p c n", c=NT), w, ALU.mult)
                    tell(ins, adec_ok, c_free)

                def states(t):
                    dve.wait_ge(d_done, ND * L + D_USE[f"u{t}"] + 1)
                    if t == 1:
                        dve.wait_ge(o_ps, 2 * L + 1)
                    for r in range(2):
                        for e in range(2):
                            rows_ = slice(HD * e, HD * e + HD)
                            dve.tensor_copy(s_out[rows_, L, r, t, :], PD[rows_, 512 * r + HD * e:512 * r + HD * e + HD])
                    first = dve.tensor_copy(ret_st[:, 0, 0, :], ret_s0[:, 0, t, :])
                    chain.link(dve.tensor_copy(ret_st[:, 1, 3, :], ret_s0[:, 1, t, :]))
                    for n in range(3):
                        for r, to, frm, up in ((0, n + 1, n, n + 1), (1, 2 - n, 3 - n, 3 - n)):
                            for e in range(2):
                                rows_ = slice(HD * e, HD * e + HD)
                                at = 512 * r + P * up + HD * e
                                g = CONST["gam"][0] + 2 * r + t
                                ins = dve.scalar_tensor_tensor(ret_st[rows_, r, to, :], ret_st[rows_, r, frm, :],
                                                               const[rows_, g:g + 1], PD[rows_, at:at + HD], ALU.mult, ALU.add)
                        chain.link(ins)
                    dve.sem_inc(st_ok, 1)
                    dve.sem_inc(d_free, 1)

                def gated(t, r):
                    dve.wait_ge(osq_ok, 4 * L + 2 * t + r + 1)
                    tell(dve.tensor_tensor(o_g[t][:, r, :], PC[:, 0:TOK], gate[:, r, t, :], ALU.mult), c_free)

                def variances(t):
                    dve.wait_ge(d_done, ND * L + D_USE[f"ty{t}"] + 1)
                    dve.wait_ge(rs_ok, NRS * L + RS_USE[f"r{t}"])
                    tell(dve.tensor_scalar(vsum[:, :], PD[:, 0:4 * NT], EPS, None, ALU.add), v_ok, d_free)

                def normalised(t, r):
                    dve.wait_ge(d_done, ND * L + D_USE[f"by{t}{'fb'[r]}"] + 1)
                    tell(dve.tensor_tensor(o_g[t][:, r, :], o_g[t][:, r, :], PD[:, 0:TOK], ALU.mult), d_free)

                def directions(t):
                    tell(dve.tensor_tensor(o_g[t][:, 0, :], o_g[t][:, 0, :], o_g[t][:, 1, :], ALU.add), ret_hi)

                def rest_of_sum(t):
                    dve.wait_ge(c_read, 2 * L + t + 1)
                    tell(dve.tensor_tensor(act_lo[:, 4 + t, :], o_g[t][:, 0, :], act_hi[:, 4 + t, :].bitcast(F32), ALU.subtract), ret_sum)

                dve.wait_ge(s0_in, 32 * (L + 1))
                keys_decayed(0)
                masked(0, 0)
                queries_decayed(0)
                masked(0, 1)
                states(0)
                keys_decayed(1)
                masked(1, 0)
                masked(1, 1)
                queries_decayed(1)
                states(1)
                gated(0, 0)
                gated(0, 1)
                variances(0)
                gated(1, 0)
                normalised(0, 0)
                gated(1, 1)
                normalised(0, 1)
                directions(0)
                variances(1)
                rest_of_sum(0)

                dve.wait_ge(c_done, NC * L + C_USE["sctx"] + 1)
                chain.link(dve.reduce_max(mxc[:, :], PC[:, 0:1024].rearrange("p (h n) -> p h n", h=HEADS), AX.X))
                dve.scalar_tensor_tensor(nbc[:, :].rearrange("p (e t) -> p e t", e=2), mxc[:, :].rearrange("p (e t) -> p e t", e=2),
                                         -1.0, q_rs[:, :, 0, :].rearrange("p t e -> p e t"), ALU.mult, ALU.mult).then_inc(nbc_ok, 1)
                normalised(1, 0)
                normalised(1, 1)
                directions(1)
                dve.wait_ge(expc_ok, L + 1)
                dve.sem_inc(c_free, 1)
                chain.link(dve.reciprocal(ric[:, :], rsc[:, :]))
                for h in range(HEADS):
                    ins = dve.tensor_scalar(diag[:, h // 4, h % 4, :], ident, ric[:, h:h + 1], None, ALU.mult)
                ins.then_inc(dgc_ok, 1)
                rest_of_sum(1)
                dve.wait_ge(tc_ps, L + 1)
                dve.tensor_copy(probs_t[:, 0:2, :].rearrange("p b n -> p (b n)"), PA).then_inc(ptc_ok, 1)
                dve.wait_ge(oc_hi, L + 1)
                dve.tensor_tensor(act_lo[:, 0:4, 0:CTX], PB_[:, 0:512].rearrange("p (t n) -> p t n", t=4),
                                  act_hi[:, 0:4, 0:CTX].bitcast(F32), ALU.subtract).then_inc(oc_ok, 1)

                with dve.Fori(0, 2) as i:
                    chain.clear()

                    def rest(q):
                        dve.wait_ge(qhi_ok, 8 * L + 4 * i + q + 1)
                        dve.tensor_tensor(q_lo[:, q % 2, :], q2[0:HD, :], qq[0:HD, q % 2, :].bitcast(F32),
                                          ALU.subtract).then_inc(qpack, 1)

                    def maximum(q, b):
                        dve.wait_ge(s_done, 32 * L + 16 * i + 4 * q + b + 9)
                        at = 4 * (q % 2) + b
                        chain.link(dve.reduce_max(mx[:, at:at + 1], pair[2 + b % 2][:, 0:KEYS], AX.X))
                        dve.scalar_tensor_tensor(nb[:, at:at + 1], mx[:, at:at + 1], -1.0,
                                                 q_rs[:, i + 2 * (q // 2), 1 + b, q % 2:q % 2 + 1], ALU.mult, ALU.mult).then_inc(nb_ok, 1)

                    def diagonals(q):
                        dve.wait_ge(t_done, 48 * L + 24 * i + 6 * q + 6)
                        a = 4 * (q % 2)
                        dve.wait_ge(exp_ok, 32 * L + 16 * i + 4 * q + 6)
                        chain.link(dve.reciprocal(rinv[:, a:a + 4], rsum[:, a:a + 4]))
                        for b in range(4):
                            dve.tensor_scalar(diag[:, q % 2, b, :], ident, rinv[:, a + b:a + b + 1], None, ALU.mult).then_inc(dg_ok, 1)

                    def turned(q, t):
                        n = 6 * q + t
                        dve.wait_ge(t_done, 48 * L + 24 * i + n + 13)
                        dve.wait_ge(pv_done, 48 * L + 24 * i + n + 1)
                        dve.tensor_copy(probs_t[:, n % 4, :], psum[:, 2 * (n % 2), :]).then_inc(pt_ok, 1)

                    def output(q):
                        e, t = q % 2, i + 2 * (q // 2)
                        dve.wait_ge(o_hi, 8 * L + 4 * i + q + 1)
                        rows_ = slice(HD * e, HD * e + HD)
                        dve.tensor_tensor(act_lo[rows_, t, CTX:TOK], psum[rows_, 2 * (q % 2) + 1, :],
                                          act_hi[rows_, t, CTX:TOK].bitcast(F32), ALU.subtract).then_inc(o_ok, 1)

                    rest(0)
                    for b in range(4):
                        maximum(0, b)
                    for q in range(4):
                        diagonals(q)
                        if q < 3:
                            rest(q + 1)
                        for t in range(NKT):
                            turned(q, t)
                            if q < 3 and t < 4:
                                maximum(q + 1, t)
                            if q >= 1 and t == 2:
                                output(q - 1)
                    output(3)

                chain.clear()
                dve.memset(sq_acc[:, :], 0.0)
                for t in range(2):
                    for at in (0, CTX + 1, GAP - 1):
                        ins = dve.memset(u_sb[:, t, at:at + 1], 0.0)
                chain.link(ins)

                def square_units(first, gains, at, last=False):
                    def two(i):
                        static = isinstance(i, int)
                        for s in range(2):
                            if not (last and i == 1 and s == 1):
                                split(L, first + s + 1 + (2 * i if static else 0), None if static else i)
                            for t in range(2):
                                m = 4 * i + 2 * s + t
                                dve.wait_ge(job_done, JOBS * L + 2 * (first + s) + t + 3 + 4 * i)
                                for lo, hi, src in ((0, CTX, pair[t][:, 0:CTX]), (CTX, TH, pair[t][:, CTX:TH]),
                                                    (TH, TOK, pair[t][:, 512:512 + TH])):
                                    g = 0 if lo == 0 else 1
                                    ins = dve.scalar_tensor_tensor(x[:, m, lo:hi], src, mod[:, gains + m, g:g + 1],
                                                                   x[:, m, lo:hi], ALU.mult, ALU.add)
                                tell(ins, a_free if t == 0 else b_free, *([x_new] if at is not None else []))
                                if at is not None:
                                    add_squares(L, m, t, at)
                    if last:
                        two(0)
                        two(1)
                    else:
                        with dve.Fori(0, 2) as i:
                            chain.clear()
                            two(i)
                    chain.clear()

                square_units(U_OUT, 16, KD)
                norm(L, "2", KD)

                first = 0
                for v, n, up, down in zip(range(3), CHUNKS, U_UP, U_DOWN):
                    with dve.Fori(0, n // 2) as i:
                        chain.clear()
                        for s in range(2):
                            split(L, up + s + 1, i)
                            j = first + s
                            for t in range(2):
                                dve.wait_ge(u_ok, 2 * NJ * L + 4 * i + 2 * j + t + 1)
                                if t == 0:
                                    dve.wait_ge(sg_ok, NJ * L + 2 * i + j + 1)
                                tile = 2 * i + j + 22 * t
                                c1 = slice(1, 2 + TOK)
                                chain.link(dve.tensor_scalar(cv[:, t, c1], u_sb[:, t, c1], conv_l[:, 1, bass.ds(tile, 1)],
                                                             conv_l[:, 3, bass.ds(tile, 1)], ALU.mult, ALU.add))
                                chain.link(dve.scalar_tensor_tensor(cv[:, t, c1], u_sb[:, t, 0:1 + TOK], conv_l[:, 0, bass.ds(tile, 1)],
                                                                    cv[:, t, c1], ALU.mult, ALU.add))
                                tell(dve.scalar_tensor_tensor(cv[:, t, c1], u_sb[:, t, 2:3 + TOK], conv_l[:, 2, bass.ds(tile, 1)],
                                                              cv[:, t, c1], ALU.mult, ALU.add), cv_ok)
                            dve.wait_ge(sg_ok, NJ * L + 2 * i + j + 2)
                            dve.tensor_tensor(gf[:, 0:CTX], sg[:, 1:1 + CTX], cv[:, 1, 1:1 + CTX], ALU.mult)
                            dve.tensor_tensor(gf[:, CTX:TOK], sg[:, 2 + CTX:2 + TOK], cv[:, 1, 2 + CTX:2 + TOK], ALU.mult).then_inc(gf_ok, 1)
                            dve.wait_ge(g_hi_ok, NJ * L + 2 * i + j + 1)
                            dve.tensor_tensor(g_lo[:, 2 * i + s, :], gf[:, :], g_hi[:, 2 * i + s, :].bitcast(F32),
                                              ALU.subtract).then_inc(g_ok, 1)
                    first += n
                    chain.clear()
                    if first == NJ:
                        chain.link(dve.memset(sq_acc[:, :], 0.0))
                    square_units(down, 40, 2 * KD if first == NJ else None, last=first == NJ)
                    if v < 2:
                        with dve.If(L < 1):
                            dve.wait_ge(next_turned, v + 3)
                            add_bias(mod_next[:, KD * v:KD * v + KD, :],
                                     prm[:, C_BMOD + 48 + KD * v:C_BMOD + 48 + KD * v + KD]).then_inc(next_ok, 1)

            chain.clear()
            dve.wait_ge(c_done, NC * DEPTH + 1)
            tell(dve.tensor_scalar(vsum[:, 0:NT], PC[:, 768:768 + NT], EPS, None, ALU.add), v_ok)
            dve.wait_ge(c_done, NC * DEPTH + 2)
            for k in range(KD + 1):
                if k < KD:
                    if k >= 2:
                        dve.wait_ge(y_row, k - 1)
                    dve.scalar_tensor_tensor(y_t[:, k % 2, :], x[:, k, :], prm[:, R_FIN + k:R_FIN + k + 1], PC[:, 0:TOK],
                                             ALU.mult, ALU.mult).then_inc(y_col, 1)
                if k >= 1:
                    dve.wait_ge(y_row, k)
                    dve.tensor_copy(rows[:, :, P * (k - 1):P * k], pair[(k - 1) % 2][:, 0:TOK].rearrange("p (t n) -> p t n", t=NT))\
                       .then_inc(y_rows, 1)

        @block.gpsimd
        def _(pool):
            pool.memset(half[:, :], -0.5).then_inc(pool_chain, 1)
            pool.wait_ge(pool_chain, 1)
            with pool.Fori(0, DEPTH) as L:
                for name, n in RS_USE.items():
                    pool.wait_ge(v_ok, NRS * L + n + 1)
                    w = {"n": NT, "r": 4 * NT}.get(name[0], 2 * NT)
                    if name[0] == "q":
                        dst = q_rs[:, int(name[1]), :, :].rearrange("p t e -> p (t e)")
                    else:
                        dst = rstd[:, 0:w]
                    pool.tensor_tensor(dst, vsum[:, 0:w], half[:, 0:w], ALU.pow).then_inc(rs_ok, 1)
                with pool.If(L < 1):
                    for n in range(4):
                        if n == 0:
                            pool.wait_ge(h_ok, 2 * KD)
                        else:
                            pool.wait_ge(next_used, n)
                        for k in range(4):
                            at = 4 * (n % 2) + k
                            pool.dma_start(m_next[:, k, :], w_mod_v[1, :, at, D * (n // 2):D * (n // 2) + D]).then_inc(next_in, 16)
            pool.wait_ge(v_ok, NRS * DEPTH + 1)
            pool.tensor_tensor(rstd[:, 0:NT], vsum[:, 0:NT], half[:, 0:NT], ALU.pow).then_inc(rs_ok, 1)


def constants(np):
    f32 = np.float32
    out = np.zeros((P, NCONST), np.float64)

    def put(name, v):
        a, b = CONST[name]
        out[:, a:b] = v

    i = np.arange(P)
    put("ident", np.eye(P))
    put("ones", np.full((P, 1), 1.0 / D))
    put("blk", (i[:, None] // HD == np.arange(2)[None]) / HD)
    same = (i[:, None] // HD == i[None] // HD)
    put("center", np.eye(P) - same / HD)
    rot = np.zeros((P, P))
    for m in range(P):
        base, r = m // 32 * 32, m % 32
        if r < 16:
            rot[base + r + 16, m] = -1.0
        else:
            rot[base + r - 16, m] = 1.0
    put("rot", rot)
    ang = 2 * np.pi * (np.outer(i % HD, i % HD) % HD) / HD
    for name, n in (("l", LAT), ("c", CTX)):
        put("c64" + name, same * np.cos(ang) / np.sqrt(n * HD))
        put("s64" + name, same * -np.sin(ang) / np.sqrt(n * HD))
    tok = np.arange(LAT)
    freqs = (f32(10000.0) ** (-np.arange(16, dtype=f32) / f32(16))).astype(f32)
    pos = np.stack([(tok // 64).astype(f32), (tok % 64).astype(f32)])
    d = i % HD
    a = (pos[d // 32] * freqs[d % 16][:, None]).astype(f32).astype(np.float64)
    put("cos", np.cos(a))
    put("sin", np.sin(a))
    j, q = i[:, None], i[None]
    for r, (w, base) in enumerate((("f", 5.0), ("b", 5.5))):
        lg = np.log1p(-np.exp2(-(f32(base) + np.arange(4, dtype=f32)))).astype(f32).astype(np.float64)
        dist = (q - j) if r == 0 else (j - q)
        put("mask" + w, np.concatenate([np.where(dist >= 0, np.exp(np.maximum(dist, 0) * lg[h]), 0.0) for h in range(4)], 1))
        place = i if r == 0 else P - 1 - i
        put("qd" + w, np.concatenate([np.exp((place + 1.0)[None] * lg[2 * t + i // HD][:, None]) for t in range(2)], 1))
        put("kd" + w, np.exp((P - 1.0 - place)[:, None] * lg[np.arange(256) // HD][None]))
        for t in range(2):
            out[:, CONST["gam"][0] + 2 * r + t] = np.exp(P * lg[2 * t + i // HD])
    dft = np.zeros((P, 256 + 4096), np.float64)
    a = 2 * np.pi * (np.outer(i, i) % CTX) / CTX
    dft[:, 0:128], dft[:, 128:256] = np.cos(a), np.sin(a)
    a = 2 * np.pi * (np.outer(tok, tok) % LAT) / LAT
    for n, v in enumerate((np.cos(a), np.sin(a))):
        dft[:, 256 + 2048 * n:256 + 2048 * (n + 1)] = v.reshape(4, P, LAT).transpose(1, 0, 2).reshape(P, 2048)
    return out.astype(f32), dft.astype(f32)


_INS = ["x_prompt", "x_sample", "c", "cache_attn_k", "cache_attn_v", "state_ret", "c_ctx", "w_mod", "b_mod", "norm1_w",
        "w_in", "q_norm_w", "k_norm_w", "w_out", "norm2_w", "w_up", "conv_w", "conv_b", "w_down", "final_norm_w"]
_OUTS = [(1, CTX, D), (1, LAT, D), (1, DEPTH, CTX, 2, HD), (1, DEPTH, CTX, 2, HD), (1, DEPTH, 2, 4, HD, HD)]


def kernel(**inputs):
    import numpy as _np
    import concourse.bacc as _bacc
    from concourse import mybir as _mybir
    from concourse.bass_utils import run_bass_kernel_spmd as _run

    nc = _bacc.Bacc("TRN2", target_bir_lowering=False, num_devices=1)
    arrays, args = {}, []
    const, dft = constants(_np)
    for name, a in [(n, inputs[n]) for n in _INS] + [("const", const), ("dft", dft)]:
        a = _np.ascontiguousarray(a)
        arrays[f"in_{name}_dram"] = a
        args.append(nc.dram_tensor(f"in_{name}_dram", a.shape, _mybir.dt.from_np(a.dtype), kind="ExternalInput").ap())
    for i, shape in enumerate(_OUTS):
        args.append(nc.dram_tensor(f"out_{i}_dram", shape, _mybir.dt.float32, kind="ExternalOutput").ap())
    program(nc, *args)
    r = _run(nc, [arrays], core_ids=[0])
    return tuple(r.results[0][f"out_{i}_dram"] for i in range(len(_OUTS)))
```

```python
from contextlib import ExitStack

import concourse.bass as bass
from concourse import mybir

F32 = mybir.dt.float32
F32R = mybir.dt.float32r
ALU = mybir.AluOpType
ACT = mybir.ActivationFunctionType
AX = mybir.AxisListType

P = 128
D = 1024
KD = D // P
CTX = 128
LAT = 512
TOK = CTX + LAT
NT = TOK // P
TH = TOK // 2
DEPTH = 2
HEADS = 8
HD = 64
PAST = 256
KEYS = PAST + LAT
NKT = KEYS // P
FF = 2816
NJ = FF // P
EPS = 1e-6
GAP = TOK + 3
CHUNKS = (8, 8, 6)

IN_COLS = (0, 256, 512, 768, 1024, 1280, 2048, 1536, 1792)
U_Q0, U_Q1, U_KV, U_RQ, U_RK, U_RV, U_FX, U_GF, U_GB, U_DFTC, U_COS, U_SIN = range(12)
U_OUT = 12
U_UP = (16, 28, 40)
U_DOWN = (24, 36, 46)
UNITS = 50
JOBS = 2 * UNITS
MOD_ROUNDS = 4
MT = KD * MOD_ROUNDS
V_SH1, V_SC1, V_G1, V_SH2, V_SC2, V_G2 = range(6)

CONST = {}
_at = 0
for _name, _width in (("ident", 128), ("ones", 1), ("blk", 2), ("center", 128), ("rot", 128),
                      ("c64l", 128), ("s64l", 128), ("c64c", 128), ("s64c", 128),
                      ("cos", 512), ("sin", 512), ("maskf", 512), ("maskb", 512),
                      ("qdf", 256), ("qdb", 256), ("kdf", 256), ("kdb", 256), ("gam", 4)):
    CONST[_name] = (_at, _at + _width)
    _at += _width
NCONST = _at
CONST_A = CONST["cos"][0]

R_CC, R_C, R_N1, R_N2, R_FIN, R_QN, R_KN, R_END = 0, 8, 16, 32, 48, 56, 58, 60
C_BMOD = R_END
C_CONV = C_BMOD + 96
NPRM = C_CONV + DEPTH * 4 * 44


def uses(*names):
    return {n: i for i, n in enumerate(names)}


C_USE = uses("sum1", "bc1", "mod0", "kbc", "mod1", "rkt0", "rkt1", "mod2", "mod3", "four0", "four1",
             "at00", "at01", "at10", "at11", "cen0f", "cen0b", "cen1f", "cen1b",
             "sctx", "sum2", "bc2")
D_USE = uses("st0", "st1", "rot0", "st2", "rot1", "st3", "rot2", "st4", "rot3", "rot4", "kct", "kcache",
             "u0", "u1", "ty0", "by0f", "by0b", "ty1", "by1f", "by1b")
NC, ND = len(C_USE), len(D_USE)
RS_USE = uses("n1", "q0", "q1", "q2", "q3", "k", "r0", "r1", "n2")
NRS = len(RS_USE)


def program(nc, x_prompt, x_sample, c, cache_k, cache_v, state_ret, c_ctx, w_mod, b_mod, norm1_w, w_in,
            q_norm_w, k_norm_w, w_out, norm2_w, w_up, conv_w, conv_b, w_down, final_norm_w,
            const_d, dft_d, y_prompt, y_sample, new_k, new_v, new_s):
    w_in_v = w_in.rearrange("l (k p) n -> l p k n", p=P)
    w_out_v = w_out.rearrange("l (k p) n -> l p k n", p=P)
    w_up_v = w_up.rearrange("l (k p) n -> l p k n", p=P)
    w_down_v = w_down.rearrange("l (k p) n -> l p k n", p=P)
    w_mod_v = w_mod.rearrange("l (k p) n -> l p k n", p=P)

    with ExitStack() as ctx:
        def sb(name, shape, dt=F32, stack=None):
            return (stack or ctx).enter_context(nc.sbuf_tensor(name, shape, dt))

        def sem(name):
            return ctx.enter_context(nc.semaphore(name))

        x = sb("x", [P, KD, TOK])
        alias = ExitStack()
        m_pre_a = sb("m_pre_a", [P, 10, D], F32, alias)
        alias.close()
        alias = ExitStack()
        o_g1 = sb("o_g1", [P, 2, TOK], F32, alias)
        alias.enter_context(nc.sbuf_tensor("act_hi_rest", [P, KD - 2, TOK], F32))
        a_dec1 = sb("a_dec1", [P, 2, TOK], F32, alias)
        alias.close()
        act_hi = sb("act_hi", [P, KD, TOK], F32R)
        act_lo = sb("act_lo", [P, KD, TOK], F32R)
        w_stage = sb("w_stage", [P, 2, 1024])
        w_hi = sb("w_hi", [P, 2, 2048], F32R)
        w_lo = sb("w_lo", [P, 2, 2048], F32R)
        const = sb("const", [P, NCONST])
        prm = sb("prm", [P, NPRM])
        silu_c = sb("silu_c", [P, KD, 32])
        mod_rows = sb("mod_rows", [P, 256])
        mod_next = sb("mod_next", [P, 2 * KD, 2])
        mod = sb("mod", [P, 48, 2])
        scale1 = sb("scale1", [P, KD, 2])
        scale2 = sb("scale2", [P, KD, 2])
        bmod_l = sb("bmod_l", [P, 48])
        n1_l = sb("n1_l", [P, KD])
        n2_l = sb("n2_l", [P, KD])
        conv_l = sb("conv_l", [P, 4, 44])
        qk_w = sb("qk_w", [P, 2])
        half = sb("half", [P, 4 * NT])
        vsum = sb("vsum", [P, 4 * NT])
        rstd = sb("rstd", [P, 4 * NT])
        q_rs = sb("q_rs", [P, 4, NT, 2])
        k_out = sb("k_out", [P, DEPTH, P])
        v_out = sb("v_out", [P, DEPTH, P])
        s_out = sb("s_out", [P, DEPTH, 2, 2, HD])
        ret_s0 = sb("ret_s0", [P, 2, 2, HD])
        ret_st = sb("ret_st", [P, 2, 4, HD])

        alias = ExitStack()
        tn = sb("tn", [P, 2, TOK], F32, alias)
        hf = sb("hf", [P, 2, TOK], F32, alias)
        sq = sb("sq", [P, 2, TOK], F32, alias)
        sq_acc = sb("sq_acc", [P, TOK], F32, alias)
        alias.close()
        alias = ExitStack()
        m_next = sb("m_next", [P, KD // 2, D], F32, alias)
        alias.close()
        qT = sb("qT", [P, 4, TOK])
        v_all = sb("v_all", [P, 14, HD])
        kp = sb("kp", [P, 2, KEYS], F32R)

        phase = ExitStack()
        kT = sb("kT", [P, TOK], F32, phase)
        kc = sb("kc", [P, 2, CTX], F32, phase)
        mx = sb("mx", [P, 8], F32, phase)
        nb = sb("nb", [P, 8], F32, phase)
        rsum = sb("rsum", [P, 8], F32, phase)
        rinv = sb("rinv", [P, 8], F32, phase)
        mxc = sb("mxc", [P, 8], F32, phase)
        nbc = sb("nbc", [P, 8], F32, phase)
        rsc = sb("rsc", [P, 8], F32, phase)
        ric = sb("ric", [P, 8], F32, phase)
        ret = ExitStack()
        rqT = sb("rqT", [P, 2, TOK], F32, ret)
        rkT = sb("rkT", [P, 2, TOK], F32, ret)
        rk = sb("rk", [P, NT, 256], F32, ret)
        rv = sb("rv", [P, NT, 256], F32, ret)
        gate = sb("gate", [P, 2, 2, TOK], F32, ret)
        proj = ExitStack()
        m_stage = sb("m_stage", [P, 2, D], F32, proj)
        fx_hi = sb("fx_hi", [P, NT, 256], F32R, proj)
        fx_lo = sb("fx_lo", [P, NT, 256], F32R, proj)
        tmp = ExitStack()
        sqq = sb("sqq", [P, 2, TOK], F32, tmp)
        rtmp = sb("rtmp", [P, LAT], F32, tmp)
        tmp.close()
        tmp = ExitStack()
        k2 = sb("k2", [P, KEYS], F32, tmp)
        k2_hi = sb("k2_hi", [P, KEYS], F32R, tmp)
        sb("k_past_gap", [P, 2 * P], F32, tmp)
        k_past = sb("k_past", [P, 2, P], F32, tmp)
        tmp.close()
        tmp = ExitStack()
        dft_y = sb("dft_y", [P, 2, 2, LAT], F32, tmp)
        dft_yc = m_stage[:, 0, 0:4 * CTX].rearrange("p (t w n) -> p t w n", t=2, w=2)
        tmp.close()
        proj.close()
        k_dec = sb("k_dec", [P, 2, NT, P], F32, ret)
        a_dec = [sb("a_dec", [P, 2, TOK], F32, ret), a_dec1]
        q_dec = sb("q_dec", [P, 2, LAT], F32, ret)
        o_sb = sb("o_sb", [P, 2, TOK], F32, ret)
        o_sq = sb("o_sq", [P, 2, TOK], F32, ret)
        o_g = [rk[:, :, :].rearrange("p b n -> p (b n)").rearrange("p (r n) -> p r n", r=2),
               o_g1]
        ret.close()
        probs = sb("probs", [P, 2, 4, KEYS], F32, phase)
        probs_t = sb("probs_t", [P, 9, LAT], F32, phase)
        q2 = sb("q2", [P, LAT], F32, phase)
        qq = sb("qq", [P, 2, LAT], F32R, phase)
        q_lo = sb("q_lo", [HD, 2, LAT], F32R, phase)
        phase.close()
        ffn = ExitStack()
        g_hi = sb("g_hi", [P, 8, TOK], F32R, ffn)
        g_lo = sb("g_lo", [P, 8, TOK], F32R, ffn)
        u_sb = sb("u_sb", [P, 2, GAP], F32, ffn)
        cv = sb("cv", [P, 2, GAP], F32, ffn)
        sg = sb("sg", [P, GAP], F32, ffn)
        gf = sb("gf", [P, TOK], F32, ffn)
        ffn.close()
        ends = ExitStack()
        rows = sb("rows", [P, NT, D], F32, ends)
        m_pre_b = sb("m_pre_b", [P, 6, D], F32, ends)
        prm_rows = sb("prm_rows", [R_END, P], F32, ends)
        bmod_rows = sb("bmod_rows", [96, P], F32, ends)
        conv_rows = sb("conv_rows", [44, DEPTH, 4, P], F32, ends)
        y_t = sb("y_t", [P, 2, TOK], F32, ends)
        ends.close()

        psum = ctx.enter_context(nc.psum_tensor("psum", [P, 8, 512], F32))
        pair = [psum[:, 2 * i:2 * i + 2, :].rearrange("p b n -> p (b n)") for i in range(4)]
        PA, PB_, PC, PD = pair
        probs_c = probs[:, 0, :, :].rearrange("p b n -> p (b n)")
        mod_ps = psum[:, 7, 0:256]
        mod_tp = PC[:, 768:1024]

        def m_pre(n):
            return m_pre_a[:, n, :] if n < 10 else m_pre_b[:, n - 10, :]

        def cst(name, lo=0, hi=None):
            a, b = CONST[name]
            return const[:, a + lo:(b if hi is None else a + hi)]

        ident = cst("ident")

        one = sem("one")
        loads = sem("loads")
        const_in = sem("const_in")
        row_in = sem("row_in")
        pre_in = [sem(f"pre_in{i}") for i in range(4)]
        next_in = sem("next_in")
        next_sums = sem("next_sums")
        next_used = sem("next_used")
        next_rows = sem("next_rows")
        next_turned = sem("next_turned")
        next_ok = sem("next_ok")
        prm_t = sem("prm_t")
        prm_ok = sem("prm_ok")
        silu_ok = sem("silu_ok")
        xt_ps = sem("xt_ps")
        xt_free = sem("xt_free")
        w_landed = [sem(f"w_landed{i}") for i in range(2)]
        w_hi_ok = sem("w_hi_ok")
        w_split = sem("w_split")
        m_landed = [sem(f"m_landed{i}") for i in range(2)]
        m_used = sem("m_used")
        m_rows_ok = sem("m_rows_ok")
        job_done = sem("job_done")
        a_free = sem("a_free")
        b_free = sem("b_free")
        c_done = sem("c_done")
        c_free = sem("c_free")
        d_done = sem("d_done")
        d_free = sem("d_free")
        x_new = sem("x_new")
        sq_ok = sem("sq_ok")
        sq_used = sem("sq_used")
        tn_ok = sem("tn_ok")
        h_hi_ok = sem("h_hi_ok")
        h_ok = sem("h_ok")
        v_ok = sem("v_ok")
        rs_ok = sem("rs_ok")
        sqq_ok = sem("sqq_ok")
        kv_in = sem("kv_in")
        s0_in = sem("s0_in")
        fx_hi_ok = sem("fx_hi_ok")
        fx_ok = sem("fx_ok")
        tok_ok = sem("tok_ok")
        rv_ok = sem("rv_ok")
        y_ok = sem("y_ok")
        four_hi = sem("four_hi")
        q_copied = sem("q_copied")
        k_normed = sem("k_normed")
        c_read = sem("c_read")
        kdec_ok = sem("kdec_ok")
        adec_ok = sem("adec_ok")
        adec_used = sem("adec_used")
        st_ok = sem("st_ok")
        o_ps = sem("o_ps")
        o_copied = sem("o_copied")
        osq_ok = sem("osq_ok")
        ret_sum = sem("ret_sum")
        ret_hi = sem("ret_hi")
        kp_ok = sem("kp_ok")
        nbc_ok = sem("nbc_ok")
        expc_ok = sem("expc_ok")
        scaled_c = sem("scaled_c")
        tc_ps = sem("tc_ps")
        ptc_ok = sem("ptc_ok")
        oc_ps = sem("oc_ps")
        oc_hi = sem("oc_hi")
        oc_ok = sem("oc_ok")
        q2_turn = sem("q2_turn")
        q2_ok = sem("q2_ok")
        qhi_ok = sem("qhi_ok")
        qpack = sem("qpack")
        s_done = sem("s_done")
        nb_ok = sem("nb_ok")
        exp_ok = sem("exp_ok")
        ri_ok = sem("ri_ok")
        scaled = sem("scaled")
        scaled_act = sem("scaled_act")
        t_done = sem("t_done")
        pt_ok = sem("pt_ok")
        pt_act_ok = sem("pt_act_ok")
        pv_done = sem("pv_done")
        o_hi = sem("o_hi")
        o_ok = sem("o_ok")
        u_ok = sem("u_ok")
        cv_ok = sem("cv_ok")
        sg_ok = sem("sg_ok")
        gf_ok = sem("gf_ok")
        g_hi_ok = sem("g_hi_ok")
        g_ok = sem("g_ok")
        y_col = sem("y_col")
        y_row = sem("y_row")
        y_rows = sem("y_rows")
        stored = sem("stored")
        act_chain = sem("act_chain")
        dve_chain = sem("dve_chain")
        pool_chain = sem("pool_chain")

        block = ctx.enter_context(nc.Block())

        def slot_t(q, t):
            return t if q % 2 == 0 else 6 + t % 3

        def wait_slot_t(e, L, i, q, t):
            back = t if q % 2 == 0 else t + 3
            e.wait_ge(pv_done, 24 * L + 12 * i + 6 * (q // 2) + back + 1)

        class Chain:

            def __init__(self, e, s):
                self.e, self.s, self.n = e, s, 0

            def link(self, ins):
                ins.then_inc(self.s, 1)
                self.n += 1
                self.e.wait_ge(self.s, self.n)

            def clear(self):
                self.e.sem_clear(self.s)
                self.n = 0

        @block.sync
        def _(sp):
            flat = lambda a, r: a.rearrange("(r n) -> r n", n=P) if r == 1 else a.rearrange("l (r n) -> (l r) n", n=P)
            sp.dma_start(prm_rows[R_CC:R_C, :], flat(c_ctx, 1)).then_inc(loads, 16)
            sp.dma_start(prm_rows[R_C:R_N1, :], flat(c, 2)).then_inc(loads, 16)
            sp.dma_start(const[:, 0:CONST_A], const_d[:, 0:CONST_A]).then_inc(loads, 16)
            sp.dma_start(prm_rows[R_N1:R_N2, :], flat(norm1_w, 2)).then_inc(loads, 16)
            sp.dma_start(prm_rows[R_N2:R_FIN, :], flat(norm2_w, 2)).then_inc(loads, 16)
            sp.dma_start(prm_rows[R_FIN:R_QN, :], flat(final_norm_w, 1)).then_inc(loads, 16)
            for half_ in range(2):
                sp.dma_start(prm_rows[R_QN:R_KN, half_ * HD:(half_ + 1) * HD], q_norm_w).then_inc(loads, 16)
                sp.dma_start(prm_rows[R_KN:R_END, half_ * HD:(half_ + 1) * HD], k_norm_w).then_inc(loads, 16)
            sp.dma_start(bmod_rows[:, :], flat(b_mod, 2)).then_inc(loads, 16)
            for l in range(DEPTH):
                sp.dma_start(conv_rows[:, l, 0:3, :], conv_w[l].rearrange("t (r n) -> r t n", n=P)).then_inc(loads, 16)
                sp.dma_start(conv_rows[:, l, 3, :], conv_b[l].rearrange("(r n) -> r n", n=P)).then_inc(loads, 16)
            sp.dma_start(rows[:, 0, :], x_prompt[0]).then_inc(row_in, 16)
            sp.dma_start(rows[:, 1:NT, :], x_sample[0].rearrange("(t p) n -> p t n", p=P)).then_inc(row_in, 16)
            for v in range(2):
                for k in range(KD):
                    sp.dma_start(m_pre(KD * v + k), w_mod_v[0, :, k, D * v:D * v + D]).then_inc(pre_in[2 * v + k // 4], 16)

            def weights(L, u, srcs):
                for h in range(2):
                    sp.wait_ge(w_split, JOBS * L + 2 * u + h + 1)
                    for dst, src in srcs(h):
                        ins = sp.dma_start(dst, src)
                        ins.then_inc(w_landed[h], 16)

            def stage(h, at, k, cols=256):
                return w_stage[:, h, cols * at:cols * (at + k)].rearrange("p (k n) -> p k n", k=k)

            def square_unit(w, L, col, k=8):
                def srcs(h):
                    n = min(4, k - 4 * h) // 2
                    return [(stage(h, n * b, n), w(L, slice(4 * h + n * b, 4 * h + n * b + n), col)) for b in range(2)]
                return srcs

            def mod_tile(L, n):
                sp.wait_ge(m_used, MT * L + n + 1)
                col = D * (V_G1 + n // KD)
                sp.dma_start(m_stage[:, n % 2, :], w_mod_v[L, :, n % KD, col:col + D]).then_inc(m_landed[n % 2], 16)

            with sp.Fori(0, DEPTH) as L:
                def unit_in(u):
                    if u < 9:
                        weights(L, u, square_unit(lambda l, ks, c0: w_in_v[l, :, ks, c0:c0 + 256], L, IN_COLS[u]))
                    elif u == U_DFTC:
                        weights(L, u, lambda h: [(w_stage[HD * b:HD * b + HD, h, 0:CTX],
                                                  dft_d[HD * b:HD * b + HD, h * CTX:(h + 1) * CTX]) for b in range(2)])
                    else:
                        weights(L, u, lambda h: [(w_stage[:, h, 512 * b:512 * b + 512],
                                                  dft_d[:, 256 + 2048 * (u - U_COS) + 1024 * h + 512 * b:][:, 0:512])
                                                 for b in range(2)])
                unit_in(0)
                with sp.If(L < 1):
                    sp.dma_start(const[:, CONST_A:NCONST], const_d[:, CONST_A:NCONST]).then_inc(const_in, 16)
                unit_in(1)
                sp.wait_ge(h_ok, 16 * L + 1)
                mod_tile(L, 0)
                mod_tile(L, 1)
                sp.wait_ge(h_ok, 16 * L + 8)
                sp.dma_start(k_past[:, :, :], cache_k[0, L].rearrange("(t p) g d -> p t (g d)", p=P)).then_inc(kv_in, 16)
                sp.dma_start(v_all[:, 10:14, :], cache_v[0, L].rearrange("(t p) g d -> p t (g d)", p=P)).then_inc(kv_in, 16)
                for e in range(2):
                    sp.dma_start(ret_s0[HD * e:HD * e + HD, :, :, :].rearrange("p r t v -> p (r t) v"),
                                 state_ret[0, L].rearrange("r (t e) d v -> e d (r t) v", e=2)[e]).then_inc(s0_in, 16)
                for u in range(10):
                    unit_in(u + 2)
                    if u < 8:
                        for n in range(4 * u + 2, min(4 * u + 6, MT)):
                            mod_tile(L, n)
                with sp.Fori(0, 2) as i:
                    for s in range(2):
                        weights(L, U_OUT + 2 * i + s,
                                square_unit(lambda l, ks, c0: w_out_v[l, :, ks, bass.ds(c0, 256)], L, 512 * i + 256 * s))
                first = 0
                for n, up, down in zip(CHUNKS, U_UP, U_DOWN):
                    with sp.Fori(0, n // 2) as i:
                        for s in range(2):
                            col = 256 * i + P * (first + s)
                            for h in range(2):
                                sp.wait_ge(w_split, JOBS * L + 4 * i + 2 * (up + s) + h + 1)
                                v = w_up_v.rearrange("l p k (g n) -> l p k g n", g=2)
                                sp.dma_start(w_stage[:, h, :].rearrange("p (k g n) -> p k g n", k=4, g=2)[:, :, 0, :],
                                             v[L, :, 4 * h:4 * h + 4, 0, bass.ds(col, P)]).then_inc(w_landed[h], 16)
                                sp.dma_start(w_stage[:, h, :].rearrange("p (k g n) -> p k g n", k=4, g=2)[:, :, 1, :],
                                             v[L, :, 4 * h:4 * h + 4, 1, bass.ds(col, P)]).then_inc(w_landed[h], 16)
                    with sp.Fori(0, 2) as i:
                        for s in range(2):
                            weights(L, down + 2 * i + s,
                                    square_unit(lambda l, ks, c0: w_down_v[l, :, slice(ks.start + first, ks.stop + first), bass.ds(c0, 256)],
                                                L, 512 * i + 256 * s, k=n))
                    first += n
            sp.wait_ge(sq_used, KD * (2 * DEPTH + 1))
            sp.dma_start(new_k[0].rearrange("l p g d -> p l (g d)"), k_out[:, :, :]).then_inc(stored, 16)
            sp.dma_start(new_v[0].rearrange("l p g d -> p l (g d)"), v_out[:, :, :]).then_inc(stored, 16)
            for e in range(2):
                sp.dma_start(new_s[0].rearrange("l r (t e) d v -> e d (l r t) v", e=2)[e],
                             s_out[HD * e:HD * e + HD].rearrange("p l r t v -> p (l r t) v")).then_inc(stored, 16)
            for n in range(KD // 2):
                cols = slice(256 * n, 256 * n + 256)
                sp.wait_ge(y_rows, 2 * n + 2)
                sp.dma_start(y_prompt[0, :, cols], rows[:, 0, cols]).then_inc(stored, 16)
                sp.dma_start(y_sample[0].rearrange("(t p) n -> p t n", p=P)[:, :, cols], rows[:, 1:NT, cols]).then_inc(stored, 16)
            sp.wait_ge(stored, 16 * (4 + KD))

        @block.tensor
        def _(pe):

            def mm(out, lhs, rhs, start=True, stop=True):
                return pe.matmul(out, lhs, rhs, start=start, stop=stop, skip_group_check=True)

            def take(place, L, name):
                s, order, n = (c_free, C_USE, NC) if place == "C" else (d_free, D_USE, ND)
                pe.wait_ge(s, n * L + order[name] + 1)

            def give(place, ins):
                ins.then_inc(c_done if place == "C" else d_done, 1)

            pe.sem_inc(one, 1)
            pe.sem_inc(a_free, 1)
            pe.sem_inc(b_free, 1)
            pe.sem_inc(c_free, 1)
            pe.sem_inc(d_free, 1)
            pe.sem_inc(w_split, 2)
            pe.sem_inc(job_done, 2)
            pe.sem_inc(m_used, 2)
            pe.sem_inc(qpack, 1)
            pe.sem_inc(exp_ok, 2)
            pe.sem_inc(pv_done, 6)
            pe.sem_inc(o_ok, 2)
            pe.sem_inc(g_ok, 1)
            pe.sem_inc(s_done, 8)
            pe.sem_inc(t_done, 12)
            pe.sem_inc(cv_ok, 2)
            pe.sem_inc(gf_ok, 1)
            pe.sem_inc(sg_ok, 1)

            pe.wait_ge(loads, 16 * 15)
            for dst, src, n in [(0, prm_rows[:, :], R_END), (C_BMOD, bmod_rows[:, :], 96)] + \
                    [(C_CONV + 44 * (4 * l + t), conv_rows[:, l, t, :], 44) for l in range(DEPTH) for t in range(4)]:
                ins = pe.transpose(PC[:, dst:dst + n], src, ident[0:n, 0:n])
            ins.then_inc(prm_t, 1)
            pe.wait_ge(row_in, 32)
            for k in range(KD):
                if k >= 2:
                    pe.wait_ge(xt_free, k - 1)
                for t in range(NT):
                    ins = pe.transpose(pair[k % 2][:, P * t:P * t + P], rows[:, t, P * k:P * k + P], ident)
                ins.then_inc(xt_ps, 1)
            def mod_products(to, src, k):
                for j in range(4):
                    ins = mm(to[32 * j:32 * j + 32, :], silu_c[:, k, :], src[:, 256 * j:256 * j + 256], k == 0, k == KD - 1)
                return ins

            def turn_mod():
                for b in range(2):
                    ins = pe.transpose(mod_tp[:, P * b:P * b + P], mod_rows[:, P * b:P * b + P], ident)
                return ins

            pe.wait_ge(silu_ok, 1)
            for v in range(2):
                if v == 1:
                    pe.wait_ge(next_rows, 1)
                    turn_mod().then_inc(next_turned, 1)
                for k in range(KD):
                    if k % 4 == 0:
                        pe.wait_ge(pre_in[2 * v + k // 4], 64)
                    ins = mod_products(mod_ps, m_pre(KD * v + k), k)
                ins.then_inc(next_sums, 1)
            pe.wait_ge(xt_free, KD)
            pe.wait_ge(next_rows, 2)
            pe.wait_ge(next_ok, 1)
            turn_mod().then_inc(next_turned, 1)

            def norm(L, which, at):
                pe.wait_ge(sq_used, at)
                take("C", L, "sum" + which)
                for t in range(NT):
                    ins = mm(PC[:, 768 + t:769 + t], sq_acc[:, P * t:P * t + P], cst("ones"))
                give("C", ins)
                take("C", L, "bc" + which)
                spread(L, PC, which)

            def spread(L, place, which):
                pe.wait_ge(rs_ok, NRS * L + RS_USE["n" + which] + 1)
                for t in range(NT):
                    ins = mm(place[:, P * t:P * t + P], rstd[:, t:t + 1].to_broadcast([P, P]), ident)
                give("C", ins)

            def spread_heads(L, place, name, rs, at=0):
                pe.wait_ge(rs_ok, NRS * L + RS_USE[rs] + 1)
                for t in range(NT):
                    for e in range(2):
                        dst = PC if place == "C" else PD
                        ins = mm(dst[HD * e:HD * e + HD, P * t:P * t + P],
                                 rstd[:, at + 2 * t + e:at + 2 * t + e + 1].to_broadcast([P, HD]), ident)
                give(place, ins)

            def feature_job(L, u, cols, par, last=8, act=(act_hi, act_lo), arrive=None):
                slot = u % 2 if isinstance(u, int) else None
                for k in range(last):
                    if arrive:
                        arrive(k)
                    n = 0
                    for w, a in ((w_hi, act[0]), (w_hi, act[1]), (w_lo, act[0])):
                        for th in range(2):
                            ins = mm(pair[par][:, 512 * th:512 * th + TH], w[:, arrive_slot[0], cols(k)],
                                     a[:, k, TH * th:TH * th + TH], k == 0 and n == 0, k == last - 1 and n == 2)
                        n += 1
                ins.then_inc(job_done, 1)

            arrive_slot = [0]

            def two_feature_jobs(arrive):
                for k in range(KD):
                    arrive(k)
                    for t in range(2):
                        for n, (w, a) in enumerate(((w_hi, act_hi), (w_hi, act_lo), (w_lo, act_hi))):
                            for th in range(2):
                                ins = mm(pair[t][:, 512 * th:512 * th + TH], w[:, 0, 256 * k + P * t:256 * k + P * t + P],
                                         a[:, k, TH * th:TH * th + TH], k == 0 and n == 0, k == KD - 1 and n == 2)
                        if k == KD - 1:
                            ins.then_inc(job_done, 1)

            def pair_free(L, par, n):
                pe.wait_ge(a_free if par == 0 else b_free, UNITS * L + n + 1)

            def split_wait(L, halves):
                pe.wait_ge(w_split, JOBS * L + halves + 2)

            def square_cols(t):
                return lambda k: slice(256 * k + P * t, 256 * k + P * t + P)

            def token_job(u, tiles, cols, par):
                a, b = cols
                n = b - a
                for i, t in enumerate(tiles):
                    for k in range(KD):
                        m = 0
                        for w, y in ((w_hi, act_hi), (w_hi, act_lo), (w_lo, act_hi)):
                            ins = mm(pair[par][:, n * i:n * i + n], y[:, k, P * t:P * t + P],
                                     w[:, u % 2, 256 * k + a:256 * k + b], k == 0 and m == 0, k == KD - 1 and m == 2)
                            m += 1
                ins.then_inc(job_done, 1)

            def mod_tiles(L, n):
                r = n // KD
                if r and n % KD == 0:
                    pe.wait_ge(m_rows_ok, MOD_ROUNDS * L + r)
                for m in (n, n + 1):
                    pe.wait_ge(m_landed[m % 2], 16 * (MT // 2) * L + 16 * (m // 2) + 16)
                    ins = mod_products(mod_ps, m_stage[:, m % 2, :], m % KD)
                    ins.then_inc(m_used, 1)

            def mod_turned(L, r):
                pe.wait_ge(m_rows_ok, MOD_ROUNDS * L + r + 1)
                take("C", L, f"mod{r}")
                give("C", turn_mod())

            def next_half(L, v, h):
                with pe.If(L < 1):
                    pe.wait_ge(next_in, 64 * (2 * v + h + 1))
                    for k in range(4 * h, 4 * h + 4):
                        ins = mod_products(mod_ps, m_next[:, k % 4, :], k)
                    ins.then_inc(next_used, 1)
                    if h == 1:
                        pe.wait_ge(next_rows, v + 3)
                        pe.wait_ge(next_ok, v + 2)
                        pe.wait_ge(c_free, NC + 1)
                        turn_mod().then_inc(next_turned, 1)

            with pe.Fori(0, DEPTH) as L:
                pe.wait_ge(next_ok, 2 * L + 2)
                norm(L, "1", 2 * KD * L + KD)

                def stat(t):
                    pe.wait_ge(sqq_ok, 5 * L + t + 1)
                    take("D", L, f"st{t}")
                    for i in range(NT):
                        ins = mm(PD[:, 2 * i:2 * i + 2], sqq[:, t % 2, P * i:P * i + P], cst("blk"))
                    give("D", ins)

                def rotate(t):
                    pe.wait_ge(q_copied if t < 4 else k_normed, (4 * L + t if t < 4 else L) + 1)
                    take("D", L, f"rot{t}")
                    src = qT[:, t, CTX:TOK] if t < 4 else kT[:, CTX:TOK]
                    give("D", mm(PD[:, 0:LAT], cst("rot"), src))

                def tile(u, t, last=8):
                    arrive_slot[0] = u % 2

                    def arrive(k):
                        if t == 0 and k % 4 == 0:
                            split_wait(L, 2 * u + k // 4 + 1)
                    feature_job(L, u, square_cols(t), t, last, arrive=arrive)

                def arrive_first(k):
                    pe.wait_ge(h_ok, 16 * L + k + 1)
                    if k % 4 == 0:
                        split_wait(L, k // 4 + 1)

                for u in range(9):
                    for t in range(2):
                        if u == 0:
                            if t == 0:
                                pair_free(L, 0, 0)
                                pair_free(L, 1, 0)
                                two_feature_jobs(arrive_first)
                        else:
                            pair_free(L, t, u)
                        if u == 0:
                            pass
                        elif u == U_KV and t == 1:
                            token_job(u, range(NT), (128, 256), 1)
                        elif u in (U_RK, U_RV, U_FX):
                            if t == 0:
                                split_wait(L, 2 * u + 2)
                            token_job(u, range(4) if t == 0 else [4], (0, 256), t)
                        else:
                            tile(u, t)
                        if 1 <= 2 * u + t <= MT // 2:
                            mod_tiles(L, 2 * (2 * u + t - 1))
                        j = 2 * u + t
                        if j >= 5 and j % 4 == 1:
                            mod_turned(L, j // 4 - 1)
                        if 2 <= j <= 6:
                            stat(j - 2)
                        if 3 <= j <= 6:
                            rotate(j - 3)
                        if j == 7:
                            take("C", L, "kbc")
                            spread_heads(L, "C", "kbc", "k")
                        if j == 8:
                            rotate(4)
                            take("D", L, "kct")
                            give("D", pe.transpose(PD[:, 0:P], kT[:, 0:CTX], ident))
                            pe.wait_ge(kv_in, 32 * L + 32)
                            take("D", L, "kcache")
                            for i in range(2):
                                ins = pe.transpose(PD[:, P * i:P * i + P], k_past[:, i, :], ident)
                            give("D", ins)
                        if j == 10:
                            pe.wait_ge(tok_ok, 2 * L + 2)
                            for i in range(2):
                                take("C", L, f"rkt{i}")
                                for n in range(NT):
                                    ins = pe.transpose(PC[:, P * n:P * n + P], rk[:, n, P * i:P * i + P], ident)
                                give("C", ins)

                pe.wait_ge(fx_ok, 2 * L + 2)
                for u in (U_DFTC, U_COS, U_SIN):
                    for t in range(2):
                        pair_free(L, t, u)
                        if t == 0:
                            split_wait(L, 2 * u + 2)
                        m = 0
                        for w, y in ((w_hi, fx_hi), (w_hi, fx_lo), (w_lo, fx_hi)):
                            if u == U_DFTC:
                                for h in range(2):
                                    ins = mm(pair[t][:, 512 * h:512 * h + CTX], y[:, 0, P * t:P * t + P],
                                             w[:, u % 2, 1024 * h:1024 * h + CTX], m == 0, m == 2)
                            else:
                                for k in range(4):
                                    ins = mm(pair[t][:, 0:LAT], y[:, 1 + k, P * t:P * t + P],
                                             w[:, u % 2, 512 * k:512 * k + 512], m == 0 and k == 0, m == 2 and k == 3)
                            m += 1
                        ins.then_inc(job_done, 1)
                pe.wait_ge(y_ok, 6 * L + 6)
                for t in range(2):
                    take("C", L, f"four{t}")
                    mm(PC[:, 0:LAT], cst("c64l"), dft_y[:, t, 0, :], True, False)
                    mm(PC[:, 0:LAT], cst("s64l"), dft_y[:, t, 1, :], False, True)
                    mm(PC[:, LAT:TOK], cst("c64c"), dft_yc[:, t, 0, :], True, False)
                    give("C", mm(PC[:, LAT:TOK], cst("s64c"), dft_yc[:, t, 1, :], False, True))

                def at_product(t, e):
                    take("C", L, f"at{t}{e}")
                    rows_ = slice(HD * e, HD * e + HD)
                    for n in range(NT):
                        ins = mm(PC[:, P * n:P * n + P], rkT[rows_, t, P * n:P * n + P], rqT[rows_, t, P * n:P * n + P])
                    give("C", ins)

                def within(t, e):
                    pe.wait_ge(adec_ok, 4 * L + 2 * t + e + 1)
                    if e == 1:
                        pe.wait_ge(st_ok, 2 * L + t + 1)
                    for r in range(2):
                        for n in range(NT):
                            ins = mm(pair[r][HD * e:HD * e + HD, P * n:P * n + P],
                                     rv[:, n, P * t + HD * e:P * t + HD * e + HD], a_dec[e][:, r, P * n:P * n + P],
                                     n in (0, 4), False)
                    ins.then_inc(adec_used, 1)

                def updates(t):
                    pe.wait_ge(kdec_ok, 2 * L + t + 1)
                    take("D", L, f"u{t}")
                    for r, chunks in enumerate(((0, 1, 2, 3), (0, 2, 3, 4))):
                        for i, n in enumerate(chunks):
                            ins = mm(PD[:, 512 * r + P * i:512 * r + P * i + P], k_dec[:, r, n, :],
                                     rv[:, n, P * t:P * t + P])
                    give("D", ins)

                def across(t):
                    for r in range(2):
                        for e in range(2):
                            rows_ = slice(HD * e, HD * e + HD)
                            for n in range(4):
                                ins = mm(pair[r][rows_, P * (n + 1):P * (n + 2)], ret_st[rows_, r, n, :],
                                         q_dec[rows_, r, P * n:P * n + P], False, True)
                    ins.then_inc(o_ps, 1)

                def centre(t, r):
                    pe.wait_ge(o_copied, 4 * L + 2 * t + r + 1)
                    take("C", L, f"cen{t}{'fb'[r]}")
                    mm(PC[:, 0:512], cst("center"), o_sb[:, r, 0:512])
                    give("C", mm(PC[:, 512:TOK], cst("center"), o_sb[:, r, 512:TOK]))

                def variances(t):
                    pe.wait_ge(osq_ok, 4 * L + 2 * t + 2)
                    take("D", L, f"ty{t}")
                    for r in range(2):
                        for n in range(NT):
                            at = 2 * NT * r + 2 * n
                            ins = mm(PD[:, at:at + 2], o_sq[:, r, P * n:P * n + P], cst("blk"))
                    give("D", ins)

                def spread_powers(t, r):
                    take("D", L, f"by{t}{'fb'[r]}")
                    spread_heads(L, "D", f"by{t}{'fb'[r]}", f"r{t}", 2 * NT * r)

                at_product(0, 0)
                updates(0)
                at_product(0, 1)
                pair_free(L, 0, 12)
                pair_free(L, 1, 12)
                pe.wait_ge(rv_ok, 2 * L + 2)
                within(0, 0)
                at_product(1, 0)
                within(0, 1)
                across(0)
                at_product(1, 1)
                updates(1)
                pe.wait_ge(o_copied, 4 * L + 2)
                within(1, 0)
                centre(0, 0)
                within(1, 1)
                centre(0, 1)
                across(1)
                variances(0)
                centre(1, 0)
                spread_powers(0, 0)
                centre(1, 1)
                spread_powers(0, 1)
                variances(1)

                take("C", L, "sctx")
                pe.wait_ge(kp_ok, L + 1)
                for n in range(HEADS):
                    e, t, g = n // 4, n % 4, n % 4 // 2
                    ins = mm(PC[:, P * n:P * n + P], qT[HD * e:HD * e + HD, t, 0:CTX], kc[HD * e:HD * e + HD, g, :])
                give("C", ins)
                spread_powers(1, 0)
                spread_powers(1, 1)
                pe.wait_ge(scaled_c, L + 1)
                pe.wait_ge(o_copied, 4 * L + 4)
                for h in range(HEADS):
                    ins = pe.transpose(PA[:, P * h:P * h + P], probs_c[:, P * h:P * h + P], ident)
                ins.then_inc(tc_ps, 1)
                pe.wait_ge(ptc_ok, L + 1)
                for n in range(HEADS):
                    e, t, g = n // 4, n % 4, n % 4 // 2
                    ins = mm(PB_[HD * e:HD * e + HD, P * t:P * t + P], v_all[:, g, :],
                             probs_t[:, e, P * t:P * t + P])
                ins.then_inc(oc_ps, 1)

                with pe.Fori(0, 2) as i:
                    def scores(q, b):
                        n = 4 * q + b
                        g = q // 2
                        if b == 0:
                            pe.wait_ge(qpack, 8 * L + 4 * i + q + 2)
                        pe.wait_ge(exp_ok, 32 * L + 16 * i + n + 1)
                        dst = pair[2 + b % 2]
                        for lo, hi in ((0, 512), (512, KEYS)):
                            mm(dst[:, lo:hi], qq[:, q % 2, P * b:P * b + P], kp[:, g, lo:hi], True, False)
                            ins = mm(dst[:, lo:hi], q_lo[:, q % 2, P * b:P * b + P], kp[0:HD, g, lo:hi], False, True)
                        ins.then_inc(s_done, 1)

                    def copied(q, t):
                        pe.wait_ge(pt_act_ok if t % 2 else pt_ok, 24 * L + 12 * i + 3 * q + t // 2 + 1)

                    def turned(q, t):
                        n = 6 * q + t
                        if t == 0:
                            pe.wait_ge(scaled, 16 * L + 8 * i + 2 * q + 2)
                            pe.wait_ge(scaled_act, 16 * L + 8 * i + 2 * q + 2)
                        if n >= 2:
                            copied((n - 2) // 6, (n - 2) % 6)
                        for b in range(4):
                            ins = pe.transpose(psum[:, 2 * (n % 2), P * b:P * b + P], probs[:, q % 2, b, P * t:P * t + P], ident)
                        ins.then_inc(t_done, 1)

                    def values(p, t):
                        blk = 10 + 2 * t + p if t < 2 else 2 * (t - 1) + p
                        if t == 0:
                            pe.wait_ge(o_ok, 4 * L + 2 * i + p + 1)
                        copied(2 * p + 1, t)
                        for e in range(2):
                            ins = mm(psum[HD * e:HD * e + HD, 2 * p + 1, :], v_all[:, blk, :], probs_t[:, slot_t(e, t), :],
                                     t == 0, t == NKT - 1)
                        ins.then_inc(pv_done, 1)

                    pe.wait_ge(c_free, NC * L + C_USE["sctx"] + 2)
                    pe.wait_ge(d_free, ND * L + ND + 1)
                    pe.wait_ge(oc_ok, L + 1)
                    for b in range(4):
                        scores(0, b)
                    for q in range(4):
                        for t in range(NKT):
                            if q < 3 and t == 0:
                                scores(q + 1, 0)
                                scores(q + 1, 1)
                            turned(q, t)
                            if q % 2 and t >= 1:
                                values(q // 2, t - 1)
                            if q == 2 and t == 0:
                                values(0, NKT - 1)
                            if q < 3 and t < 2:
                                scores(q + 1, t + 2)
                    values(1, NKT - 1)

                def square_units(first, k, act):
                    with pe.Fori(0, 2) as i:
                        if act is None:
                            pe.wait_ge(o_ok, 4 * L + 6)
                            pe.wait_ge(ret_sum, 2 * L + 2)
                        for s in range(2):
                            u = first + s
                            arrive_slot[0] = u % 2
                            for t in range(2):
                                pe.wait_ge(a_free if t == 0 else b_free, UNITS * L + 2 * i + u + 1)

                                def arrive(kk, u=u, t=t, s=s):
                                    if act is not None and s == 0 and t == 0:
                                        act(kk)
                                    if t == 0 and kk % 4 == 0:
                                        pe.wait_ge(w_split, JOBS * L + 4 * i + 2 * u + kk // 4 + 3)
                                feature_job(L, u, square_cols(t), t, k, (act_hi, act_lo) if act is None else (g_hi, g_lo), arrive)
                square_units(U_OUT, 8, None)
                norm(L, "2", 2 * KD * L + 2 * KD)

                first = 0
                for v, n, up, down in zip(range(3), CHUNKS, U_UP, U_DOWN):
                    def up_units(i):
                        for s in range(2):
                            u = up + s
                            arrive_slot[0] = u % 2
                            for t in range(2):
                                pe.wait_ge(a_free if t == 0 else b_free, UNITS * L + 2 * i + u + 1)

                                def arrive(k, u=u, t=t):
                                    if t == 0 and k % 4 == 0:
                                        pe.wait_ge(w_split, JOBS * L + 4 * i + 2 * u + k // 4 + 3)
                                if v == 0 and isinstance(i, int) and s == 0:
                                    continue
                                feature_job(L, u, square_cols(t), t, 8, arrive=arrive)
                            if v == 0 and isinstance(i, int) and s == 0:
                                def arrive_up(k):
                                    pe.wait_ge(h_ok, 16 * L + 8 + k + 1)
                                    if k % 4 == 0:
                                        split_wait(L, 2 * U_UP[0] + k // 4 + 1)
                                two_feature_jobs(arrive_up)

                    if v == 0:
                        up_units(0)
                    with pe.Fori(1 if v == 0 else 0, n // 2) as i:
                        up_units(i)
                    if v < 2:
                        next_half(L, v, 0)
                    square_units(down, n, lambda k, first=first: pe.wait_ge(g_ok, NJ * L + first + k + 2))
                    if v < 2:
                        next_half(L, v, 1)
                    first += n

            pe.wait_ge(sq_used, KD * (2 * DEPTH + 1))
            pe.wait_ge(c_free, NC * DEPTH + 1)
            for t in range(NT):
                ins = mm(PC[:, 768 + t:769 + t], sq_acc[:, P * t:P * t + P], cst("ones"))
            ins.then_inc(c_done, 1)
            pe.wait_ge(rs_ok, NRS * DEPTH + 1)
            for t in range(NT):
                ins = mm(PC[:, P * t:P * t + P], rstd[:, t:t + 1].to_broadcast([P, P]), ident)
            ins.then_inc(c_done, 1)
            for k in range(KD):
                pe.wait_ge(y_col, k + 1)
                if k >= 2:
                    pe.wait_ge(y_rows, k - 1)
                for t in range(NT):
                    ins = pe.transpose(pair[k % 2][:, P * t:P * t + P], y_t[:, k % 2, P * t:P * t + P], ident)
                ins.then_inc(y_row, 1)

        @block.scalar
        def _(act):
            chain = Chain(act, act_chain)

            def halves(par):
                return psum[:, 2 * par:2 * par + 2, 0:TH]

            def split(L, u, i=None, width=1024):
                more = 0 if i is None else i
                for h in range(2):
                    act.wait_ge(w_landed[h], 32 * UNITS * L + 32 * (u + 1) + 64 * more)
                    if h == 0:
                        act.wait_ge(job_done, JOBS * L + 2 * u + 4 * more)
                    act.activation(w_hi[:, u % 2, 1024 * h:1024 * h + width], w_stage[:, h, 0:width],
                                   ACT.Copy).then_inc(w_hi_ok, 1)

            def split_first(L):
                for h in range(2):
                    act.wait_ge(w_landed[h], 32 * UNITS * L + 32)
                    act.activation(w_hi[:, 0, 1024 * h:1024 * h + 1024], w_stage[:, h, :], ACT.Copy).then_inc(w_hi_ok, 1)

            def norm(L, first, at):
                for k in range(KD):
                    act.wait_ge(tn_ok, 2 * KD * L + at + k + 1)
                    if k >= 2:
                        act.wait_ge(h_ok, 2 * KD * L + at + k - 1)
                    sc = scale1 if first == 0 else scale2
                    act.activation(hf[:, k % 2, 0:CTX], tn[:, k % 2, 0:CTX], ACT.Identity,
                                   bias=mod[:, first + k, 0:1], scale=sc[:, k, 0:1])
                    chain.link(act.activation(hf[:, k % 2, CTX:TOK], tn[:, k % 2, CTX:TOK], ACT.Identity,
                                              bias=mod[:, first + k, 1:2], scale=sc[:, k, 1:2]))
                    act.activation(act_hi[:, k, :], hf[:, k % 2, :], ACT.Copy).then_inc(h_hi_ok, 1)

            act.wait_ge(prm_ok, 1)
            act.activation(silu_c[:, :, 0:2].rearrange("p k s -> p s k"),
                           prm[:, R_CC:R_N1].rearrange("p (s k) -> p s k", s=2), ACT.Silu).then_inc(silu_ok, 1)
            for k in range(KD):
                act.wait_ge(x_new, k + 1)
                if k >= 2:
                    act.wait_ge(sq_used, k - 1)
                act.activation(sq[:, k % 2, :], x[:, k, :], ACT.Square).then_inc(sq_ok, 1)
            for v in range(2):
                act.wait_ge(next_sums, v + 1)
                if v == 1:
                    act.wait_ge(next_turned, 1)
                act.activation(mod_rows[:, :], mod_ps, ACT.Copy).then_inc(next_rows, 1)

            with act.Fori(0, DEPTH) as L:
                chain.clear()
                split_first(L)
                norm(L, 0, 0)
                for u in range(9):
                    split(L, u + 1, width=CTX if u + 1 == U_DFTC else 1024)
                    for t in range(2):
                        j = 2 * u + t
                        act.wait_ge(job_done, JOBS * L + j + 3)
                        free = a_free if t == 0 else b_free
                        if j <= 4:
                            dst, w = (qT[:, j, :], 0) if j < 4 else (kT[:, :], 1)
                            copied = act.activation(dst.rearrange("p (h n) -> p h n", h=2), halves(t), ACT.Identity,
                                                    bias=0.0, scale=qk_w[:, w:w + 1])
                            if j < 4:
                                copied.then_inc(q_copied, 1)
                            if j >= 2:
                                act.wait_ge(d_done, ND * L + D_USE[f"st{j - 2}"] + 1)
                            chain.link(act.activation(sqq[:, j % 2, :].rearrange("p (h n) -> p h n", h=2), halves(t), ACT.Square))
                            act.sem_inc(sqq_ok, 1)
                            act.sem_inc(free, 1)
                        elif j == 5:
                            act.activation(v_out[:, L, :], PB_[:, 0:P], ACT.Copy)
                            act.activation(v_all[:, 0:10, :].rearrange("p b n -> p (b n)"), PB_[:, 0:TOK],
                                           ACT.Copy).then_inc(free, 1)
                        elif u == U_RQ:
                            act.activation(rqT[:, t, :].rearrange("p (h n) -> p h n", h=2), halves(t),
                                           ACT.Copy).then_inc(free, 1)
                        elif u == U_RK:
                            dst = rk[:, 0:4, :] if t == 0 else rk[:, 4:5, :]
                            n = 1024 if t == 0 else 256
                            chain.link(act.activation(dst.rearrange("p b n -> p (b n)"), pair[t][:, 0:n],
                                                      ACT.Copy, scale=HD ** -0.5))
                            act.sem_inc(tok_ok, 1)
                            act.sem_inc(free, 1)
                        elif u == U_FX:
                            dst = fx_hi[:, 0:4, :] if t == 0 else fx_hi[:, 4:5, :]
                            n = 1024 if t == 0 else 256
                            act.activation(dst.rearrange("p b n -> p (b n)"), pair[t][:, 0:n],
                                           ACT.Copy).then_inc(fx_hi_ok, 1)
                        elif u in (U_GF, U_GB):
                            act.activation(gate[:, u - U_GF, t, :].rearrange("p (h n) -> p h n", h=2), halves(t),
                                           ACT.Silu).then_inc(free, 1)
                        if j >= 4 and j % 4 == 0:
                            r = j // 4 - 1
                            act.wait_ge(m_used, MT * L + KD * r + KD + 2)
                            if r:
                                act.wait_ge(c_done, NC * L + C_USE[f"mod{r - 1}"] + 1)
                            act.activation(mod_rows[:, :], mod_ps, ACT.Copy).then_inc(m_rows_ok, 1)
                act.wait_ge(kp_ok, L + 1)
                for u in (U_DFTC, U_COS, U_SIN):
                    split(L, u + 1)
                    for t in range(2):
                        act.wait_ge(job_done, JOBS * L + 2 * u + t + 3)
                        free = a_free if t == 0 else b_free
                        if u == U_DFTC:
                            ins = act.activation(dft_yc[:, t, :, :], psum[:, 2 * t:2 * t + 2, 0:CTX], ACT.Copy)
                        else:
                            ins = act.activation(dft_y[:, t, u - U_COS, :], pair[t][:, 0:LAT], ACT.Copy)
                        chain.link(ins)
                        act.sem_inc(y_ok, 1)
                        act.sem_inc(free, 1)
                for t in range(2):
                    act.wait_ge(c_done, NC * L + C_USE[f"four{t}"] + 1)
                    act.activation(act_hi[:, 6 + t, CTX:TOK], PC[:, 0:LAT], ACT.Copy)
                    act.activation(act_hi[:, 6 + t, 0:CTX], PC[:, LAT:TOK], ACT.Copy).then_inc(four_hi, 1)

                def copies(t):
                    act.wait_ge(o_ps, 2 * L + t + 1)
                    for r in range(2):
                        act.activation(o_sb[:, r, :], pair[r][:, 0:TOK], ACT.Copy).then_inc(o_copied, 1)

                def osquares(t):
                    for r, w in enumerate("fb"):
                        act.wait_ge(c_done, NC * L + C_USE[f"cen{t}{w}"] + 1)
                        act.activation(o_sq[:, r, :], PC[:, 0:TOK], ACT.Square).then_inc(osq_ok, 1)

                def leading(t):
                    act.wait_ge(ret_hi, 2 * L + t + 1)
                    act.activation(act_hi[:, 4 + t, :], o_g[t][:, 0, :], ACT.Copy).then_inc(c_read, 1)

                copies(0)
                osquares(0)
                copies(1)
                osquares(1)
                leading(0)

                act.wait_ge(nbc_ok, L + 1)
                for h in range(HEADS):
                    ins = act.activation(probs_c[:, P * h:P * h + P], PC[:, P * h:P * h + P], ACT.Exp, bias=nbc[:, h:h + 1],
                                         scale=q_rs[:, h % 4, 0, h // 4:h // 4 + 1], accum_out=rsc[:, h:h + 1])
                ins.then_inc(expc_ok, 1)
                leading(1)
                act.wait_ge(oc_ps, L + 1)
                act.activation(act_hi[:, 0:4, 0:CTX], PB_[:, 0:512].rearrange("p (t n) -> p t n", t=4),
                               ACT.Copy).then_inc(oc_hi, 1)

                with act.Fori(0, 2) as i:
                    chain.clear()

                    def leading_q(q):
                        act.wait_ge(q2_ok, 8 * L + 4 * i + q + 1)
                        act.wait_ge(s_done, 32 * L + 16 * i + 4 * q + 4)
                        act.activation(qq[:, q % 2, :], q2[:, :], ACT.Copy).then_inc(qhi_ok, 1)

                    def normalise(q, b):
                        act.wait_ge(ri_ok, 16 * L + 8 * i + 2 * q + b // 2 + 1)
                        at = 4 * (q % 2) + b
                        act.activation(probs[:, q % 2, b, :], probs[:, q % 2, b, :], ACT.Copy,
                                       scale=rinv[:, at:at + 1]).then_inc(scaled_act, 1)

                    def exps(q, b):
                        if b == 0:
                            act.wait_ge(t_done, 48 * L + 24 * i + 6 * q + 6)
                        act.wait_ge(nb_ok, 32 * L + 16 * i + 4 * q + b + 1)
                        at = 4 * (q % 2) + b
                        act.activation(probs[:, q % 2, b, :], pair[2 + b % 2][:, 0:KEYS], ACT.Exp, bias=nb[:, at:at + 1],
                                       scale=q_rs[:, i + 2 * (q // 2), 1 + b, q % 2:q % 2 + 1],
                                       accum_out=rsum[:, at:at + 1]).then_inc(exp_ok, 1)

                    def turned(q, t):
                        n = 6 * q + t
                        act.wait_ge(t_done, 48 * L + 24 * i + n + 13)
                        wait_slot_t(act, L, i, q, t)
                        act.activation(probs_t[:, slot_t(q, t), :], psum[:, 2 * (n % 2), :], ACT.Copy).then_inc(pt_act_ok, 1)

                    def output(p):
                        act.wait_ge(pv_done, 24 * L + 12 * i + 6 * p + 12)
                        act.activation(act_hi[:, i + 2 * p, CTX:TOK], psum[:, 2 * p + 1, :], ACT.Copy).then_inc(o_hi, 1)

                    leading_q(0)
                    exps(0, 0)
                    exps(0, 1)
                    normalise(0, 0)
                    leading_q(1)
                    exps(0, 2)
                    exps(0, 3)
                    normalise(0, 2)
                    for q in range(4):
                        if q < 3:
                            exps(q + 1, 0)
                            exps(q + 1, 1)
                            normalise(q + 1, 0)
                        turned(q, 1)
                        if q < 2:
                            leading_q(q + 2)
                        if q < 3:
                            exps(q + 1, 2)
                            exps(q + 1, 3)
                        turned(q, 3)
                        if q < 3:
                            normalise(q + 1, 2)
                        turned(q, 5)
                        if q == 2:
                            output(0)
                    output(1)

                def square_units(first, at, last=False):
                    def two(i, more):
                        for s in range(2):
                            if not (last and isinstance(i, int) and i == 1 and s == 1):
                                split(L, first + s + 1 + (2 * i if isinstance(i, int) else 0), None if isinstance(i, int) else i)
                            if at is not None:
                                for t in range(2):
                                    m = 4 * i + 2 * s + t
                                    act.wait_ge(x_new, 2 * KD * L + at + m + 1)
                                    act.wait_ge(sq_used, 2 * KD * L + at + m - 1)
                                    act.activation(sq[:, t, :], x[:, m, :], ACT.Square).then_inc(sq_ok, 1)
                    if last:
                        two(0, None)
                        two(1, None)
                    else:
                        with act.Fori(0, 2) as i:
                            two(i, None)

                square_units(U_OUT, KD)
                chain.clear()
                norm(L, 24, KD)
                first = 0
                for v, n, up, down in zip(range(3), CHUNKS, U_UP, U_DOWN):
                    with act.Fori(0, n // 2) as i:
                        chain.clear()
                        for s in range(2):
                            split(L, up + s + 1, i)
                            for t in range(2):
                                act.wait_ge(job_done, JOBS * L + 2 * (up + s) + t + 3 + 4 * i)
                                act.wait_ge(cv_ok, 2 * NJ * L + 4 * i + 2 * (first + s) + t + 1)
                                act.activation(u_sb[:, t, 1:1 + CTX], pair[t][:, 0:CTX], ACT.Copy)
                                act.activation(u_sb[:, t, 2 + CTX:2 + TH], pair[t][:, CTX:TH], ACT.Copy)
                                ins = act.activation(u_sb[:, t, 2 + TH:2 + TOK], pair[t][:, 512:512 + TH], ACT.Copy)
                                chain.link(ins)
                                act.sem_inc(u_ok, 1)
                                act.sem_inc(a_free if t == 0 else b_free, 1)
                            act.wait_ge(cv_ok, 2 * NJ * L + 4 * i + 2 * (first + s) + 3)
                            act.wait_ge(gf_ok, NJ * L + 2 * i + first + s + 1)
                            act.activation(sg[:, 1:2 + TOK], cv[:, 0, 1:2 + TOK], ACT.Silu).then_inc(sg_ok, 1)
                            act.wait_ge(gf_ok, NJ * L + 2 * i + first + s + 2)
                            act.activation(g_hi[:, 2 * i + s, :], gf[:, :], ACT.Copy).then_inc(g_hi_ok, 1)
                    first += n
                    square_units(down, 2 * KD if first == NJ else None, last=first == NJ)
                    if v < 2:
                        with act.If(L < 1):
                            act.wait_ge(next_used, 2 * v + 2)
                            act.activation(mod_rows[:, :], mod_ps, ACT.Copy).then_inc(next_rows, 1)

        @block.vector
        def _(dve):
            chain = Chain(dve, dve_chain)

            def tell(ins, *sems):
                chain.link(ins)
                for s in sems:
                    dve.sem_inc(s, 1)

            def split(L, u, i=None, width=1024):
                for h in range(2):
                    dve.wait_ge(w_hi_ok, JOBS * L + 2 * u + h + 1 + (0 if i is None else 4 * i))
                    cols = slice(1024 * h, 1024 * h + width)
                    dve.tensor_tensor(w_lo[:, u % 2, cols], w_stage[:, h, 0:width], w_hi[:, u % 2, cols].bitcast(F32),
                                      ALU.subtract).then_inc(w_split, 1)

            def add_squares(L, m, slot, at):
                dve.wait_ge(sq_ok, 2 * KD * L + at + m + 1)
                tell(dve.tensor_tensor(sq_acc[:, :], sq_acc[:, :], sq[:, slot, :], ALU.add), sq_used)

            def norm_powers(L, which):
                dve.wait_ge(c_done, NC * L + C_USE["sum" + which] + 1)
                if which == "2":
                    dve.wait_ge(rs_ok, NRS * L + RS_USE["n2"])
                tell(dve.tensor_scalar(vsum[:, 0:NT], PC[:, 768:768 + NT], EPS, None, ALU.add), v_ok, c_free)

            def norm(L, which, at):
                dve.wait_ge(c_done, NC * L + C_USE["bc" + which] + 1)
                for k in range(KD + 1):
                    if k < KD:
                        if k >= 2:
                            dve.wait_ge(h_hi_ok, 2 * KD * L + at + k - 1)
                        ins = dve.tensor_tensor(tn[:, k % 2, :], x[:, k, :], PC[:, 0:TOK], ALU.mult)
                        if k == KD - 1:
                            tell(ins, tn_ok, c_free)
                        else:
                            ins.then_inc(tn_ok, 1)
                    if k >= 1:
                        dve.wait_ge(h_hi_ok, 2 * KD * L + at + k)
                        dve.tensor_tensor(act_lo[:, k - 1, :], hf[:, (k - 1) % 2, :], act_hi[:, k - 1, :].bitcast(F32),
                                          ALU.subtract).then_inc(h_ok, 1)

            dve.memset(silu_c[:, :, :], 0.0)
            dve.wait_ge(prm_t, 1)
            chain.link(dve.tensor_copy(prm[:, :], PC[:, 0:NPRM]))
            dve.sem_inc(prm_ok, 1)
            dve.memset(sq_acc[:, :], 0.0)
            for k in range(KD):
                dve.wait_ge(xt_ps, k + 1)
                tell(dve.tensor_copy(x[:, k, :], pair[k % 2][:, 0:TOK]), xt_free, x_new)
                if k >= 1:
                    dve.wait_ge(sq_ok, k)
                    tell(dve.tensor_tensor(sq_acc[:, :], sq_acc[:, :], sq[:, (k - 1) % 2, :], ALU.add), sq_used)
            dve.wait_ge(sq_ok, KD)
            tell(dve.tensor_tensor(sq_acc[:, :], sq_acc[:, :], sq[:, (KD - 1) % 2, :], ALU.add), sq_used)

            def by_group(v, n):
                return v.rearrange("p (t o) -> p t o", o=1).to_broadcast([P, n, 2])

            def add_bias(dst, bias):
                src = mod_tp.rearrange("p (b j q) -> p j b q", b=2, j=4)[:, :, :, 0:2]
                return dve.tensor_tensor(dst.rearrange("p (j b) s -> p j b s", j=4), src,
                                         bias.rearrange("p (j b o) -> p j b o", j=4, o=1).to_broadcast([P, 4, 2, 2]), ALU.add)

            for v in range(2):
                dve.wait_ge(next_turned, v + 1)
                tell(add_bias(mod_next[:, KD * v:KD * v + KD, :], prm[:, C_BMOD + KD * v:C_BMOD + KD * v + KD]), next_ok)

            with dve.Fori(0, DEPTH) as L:
                chain.clear()
                norm_powers(L, "1")
                dve.wait_ge(next_ok, 2 * L + 2)
                dve.tensor_copy(mod[:, 0:2 * KD, :], mod_next[:, :, :])
                dve.tensor_copy(bmod_l[:, :], prm[:, bass.ds(48 * L + C_BMOD, 48)])
                dve.tensor_copy(n2_l[:, :], prm[:, bass.ds(KD * L + R_N2, KD)])
                dve.tensor_copy(conv_l[:, :, :].rearrange("p a b -> p (a b)"), prm[:, bass.ds(176 * L + C_CONV, 176)])
                dve.tensor_copy(qk_w[:, 0:1], prm[:, bass.ds(L + R_QN, 1)])
                dve.tensor_copy(qk_w[:, 1:2], prm[:, bass.ds(L + R_KN, 1)])
                chain.link(dve.tensor_copy(n1_l[:, :], prm[:, bass.ds(KD * L + R_N1, KD)]))
                chain.link(dve.scalar_tensor_tensor(scale1[:, :, :], mod[:, KD:2 * KD, :], 1.0, by_group(n1_l[:, :], KD),
                                                    ALU.add, ALU.mult))
                split(L, 0)
                norm(L, "1", 0)

                def rope(t, src):
                    dve.wait_ge(d_done, ND * L + D_USE[f"rot{t}"] + 1)
                    chain.link(dve.tensor_tensor(src, src, cst("cos"), ALU.mult))
                    tell(dve.tensor_tensor(rtmp[:, :], PD[:, 0:LAT], cst("sin"), ALU.mult), d_free)
                    chain.link(dve.tensor_tensor(src, src, rtmp[:, :], ALU.add))

                def powers(t):
                    dve.wait_ge(d_done, ND * L + D_USE[f"st{t}"] + 1)
                    dve.wait_ge(rs_ok, NRS * L + RS_USE[f"q{t}" if t < 4 else "k"])
                    k = float(HD) if t < 4 else 1.0
                    tell(dve.tensor_scalar(vsum[:, 0:2 * NT], PD[:, 0:2 * NT], k, k * EPS, ALU.mult, ALU.add), v_ok, d_free)

                for u in range(9):
                    split(L, u + 1, width=CTX if u + 1 == U_DFTC else 1024)
                    for t in range(2):
                        j = 2 * u + t
                        if j >= 5 and j % 4 == 1:
                            r = j // 4 - 1
                            dve.wait_ge(c_done, NC * L + C_USE[f"mod{r}"] + 1)
                            at = KD * (V_G1 + r)
                            tell(add_bias(mod[:, at:at + KD, :], bmod_l[:, at:at + KD]), c_free)
                        if 2 <= j <= 6:
                            powers(j - 2)
                        if j == 3:
                            dve.wait_ge(const_in, 16)
                        if 3 <= j <= 6:
                            rope(j - 3, qT[:, j - 3, CTX:TOK])
                        if j == 7:
                            dve.wait_ge(c_done, NC * L + C_USE["kbc"] + 1)
                            tell(dve.tensor_tensor(kT[:, :], kT[:, :], PC[:, 0:TOK], ALU.mult), c_free, k_normed)
                        if j == 8:
                            for g in range(2):
                                for half_ in range(2):
                                    dve.tensor_copy(kc[HD * half_:HD * half_ + HD, g, :], kT[HD * g:HD * g + HD, 0:CTX])
                            rope(4, kT[:, CTX:TOK])
                            dve.wait_ge(d_done, ND * L + D_USE["kct"] + 1)
                            tell(dve.tensor_copy(k_out[:, L, :], PD[:, 0:P]), d_free)
                            dve.wait_ge(d_done, ND * L + D_USE["kcache"] + 1)
                            for g in range(2):
                                rows_ = slice(HD * g, HD * g + HD)
                                for half_ in range(2):
                                    to = slice(HD * half_, HD * half_ + HD)
                                    dve.tensor_copy(k2[to, 0:PAST], PD[rows_, 0:PAST])
                                    ins = dve.tensor_copy(k2[to, PAST:KEYS], kT[rows_, CTX:TOK])
                                tell(ins, *([d_free] if g else []))
                                dve.tensor_copy(kp[0:HD, g, :], k2[0:HD, :])
                                chain.link(dve.tensor_copy(k2_hi[:, :], k2[:, :]))
                                chain.link(dve.tensor_tensor(kp[HD:P, g, :], k2[HD:P, :], k2_hi[HD:P, :].bitcast(F32), ALU.subtract))
                            dve.sem_inc(kp_ok, 1)
                        if u == U_RV:
                            dve.wait_ge(job_done, JOBS * L + j + 3)
                            dst, n = (rv[:, 0:4, :], 1024) if t == 0 else (rv[:, 4:5, :], 256)
                            tell(dve.tensor_copy(dst.rearrange("p b n -> p (b n)"), pair[t][:, 0:n]), rv_ok,
                                 a_free if t == 0 else b_free)
                            dve.wait_ge(c_done, NC * L + C_USE[f"rkt{t}"] + 1)
                            dve.tensor_copy(rkT[:, t, :], PC[:, 0:TOK]).then_inc(c_free, 1)
                        if u == U_FX:
                            dve.wait_ge(fx_hi_ok, 2 * L + t + 1)
                            dst, src, n = (fx_lo[:, 0:4, :], fx_hi[:, 0:4, :], 1024) if t == 0 else (fx_lo[:, 4:5, :], fx_hi[:, 4:5, :], 256)
                            tell(dve.tensor_tensor(dst.rearrange("p b n -> p (b n)"), pair[t][:, 0:n],
                                                   src.rearrange("p b n -> p (b n)").bitcast(F32), ALU.subtract), fx_ok,
                                 a_free if t == 0 else b_free)
                chain.link(dve.scalar_tensor_tensor(scale2[:, :, :], mod[:, 32:40, :], 1.0, by_group(n2_l[:, :], KD), ALU.add, ALU.mult))
                for u in (U_DFTC, U_COS, U_SIN):
                    split(L, u + 1)
                for t in range(2):
                    dve.wait_ge(four_hi, 2 * L + t + 1)
                    dve.tensor_tensor(act_lo[:, 6 + t, CTX:TOK], PC[:, 0:LAT], act_hi[:, 6 + t, CTX:TOK].bitcast(F32), ALU.subtract)
                    dve.tensor_tensor(act_lo[:, 6 + t, 0:CTX], PC[:, LAT:TOK], act_hi[:, 6 + t, 0:CTX].bitcast(F32),
                                      ALU.subtract).then_inc(c_free, 1)

                def keys_decayed(t):
                    if t == 1:
                        dve.wait_ge(d_done, ND * L + D_USE["u0"] + 1)
                    for r, name in enumerate(("kdf", "kdb")):
                        w = cst(name, P * t, P * t + P).rearrange("p (o n) -> p o n", o=1).to_broadcast([P, NT, P])
                        ins = dve.tensor_tensor(k_dec[:, r, :, :], rk[:, :, P * t:P * t + P], w, ALU.mult)
                    tell(ins, kdec_ok)

                def queries_decayed(t):
                    if t == 1:
                        dve.wait_ge(o_ps, 2 * L + 1)
                    for r, name in enumerate(("qdf", "qdb")):
                        w = cst(name, P * t, P * t + P).rearrange("p (o n) -> p o n", o=1).to_broadcast([P, 4, P])
                        ins = dve.tensor_tensor(q_dec[:, r, :].rearrange("p (c n) -> p c n", c=4),
                                                rqT[:, t, CTX:TOK].rearrange("p (c n) -> p c n", c=4), w, ALU.mult)
                    chain.link(ins)

                def masked(t, e):
                    dve.wait_ge(c_done, NC * L + C_USE[f"at{t}{e}"] + 1)
                    if t:
                        dve.wait_ge(adec_used, 4 * L + e + 1)
                    for r, name in enumerate(("maskf", "maskb")):
                        h = 2 * t + e
                        w = cst(name, P * h, P * h + P).rearrange("p (o n) -> p o n", o=1).to_broadcast([P, NT, P])
                        ins = dve.tensor_tensor(a_dec[e][:, r, :].rearrange("p (c n) -> p c n", c=NT),
                                                PC[:, 0:TOK].rearrange("p (c n) -> p c n", c=NT), w, ALU.mult)
                    tell(ins, adec_ok, c_free)

                def states(t):
                    dve.wait_ge(d_done, ND * L + D_USE[f"u{t}"] + 1)
                    if t == 1:
                        dve.wait_ge(o_ps, 2 * L + 1)
                    for r in range(2):
                        for e in range(2):
                            rows_ = slice(HD * e, HD * e + HD)
                            dve.tensor_copy(s_out[rows_, L, r, t, :], PD[rows_, 512 * r + HD * e:512 * r + HD * e + HD])
                    first = dve.tensor_copy(ret_st[:, 0, 0, :], ret_s0[:, 0, t, :])
                    chain.link(dve.tensor_copy(ret_st[:, 1, 3, :], ret_s0[:, 1, t, :]))
                    for n in range(3):
                        for r, to, frm, up in ((0, n + 1, n, n + 1), (1, 2 - n, 3 - n, 3 - n)):
                            for e in range(2):
                                rows_ = slice(HD * e, HD * e + HD)
                                at = 512 * r + P * up + HD * e
                                g = CONST["gam"][0] + 2 * r + t
                                ins = dve.scalar_tensor_tensor(ret_st[rows_, r, to, :], ret_st[rows_, r, frm, :],
                                                               const[rows_, g:g + 1], PD[rows_, at:at + HD], ALU.mult, ALU.add)
                        chain.link(ins)
                    dve.sem_inc(st_ok, 1)
                    dve.sem_inc(d_free, 1)

                def gated(t, r):
                    dve.wait_ge(osq_ok, 4 * L + 2 * t + r + 1)
                    tell(dve.tensor_tensor(o_g[t][:, r, :], PC[:, 0:TOK], gate[:, r, t, :], ALU.mult), c_free)

                def variances(t):
                    dve.wait_ge(d_done, ND * L + D_USE[f"ty{t}"] + 1)
                    dve.wait_ge(rs_ok, NRS * L + RS_USE[f"r{t}"])
                    tell(dve.tensor_scalar(vsum[:, :], PD[:, 0:4 * NT], EPS, None, ALU.add), v_ok, d_free)

                def normalised(t, r):
                    dve.wait_ge(d_done, ND * L + D_USE[f"by{t}{'fb'[r]}"] + 1)
                    tell(dve.tensor_tensor(o_g[t][:, r, :], o_g[t][:, r, :], PD[:, 0:TOK], ALU.mult), d_free)

                def directions(t):
                    tell(dve.tensor_tensor(o_g[t][:, 0, :], o_g[t][:, 0, :], o_g[t][:, 1, :], ALU.add), ret_hi)

                def rest_of_sum(t):
                    dve.wait_ge(c_read, 2 * L + t + 1)
                    tell(dve.tensor_tensor(act_lo[:, 4 + t, :], o_g[t][:, 0, :], act_hi[:, 4 + t, :].bitcast(F32), ALU.subtract), ret_sum)

                dve.wait_ge(s0_in, 32 * (L + 1))
                keys_decayed(0)
                masked(0, 0)
                queries_decayed(0)
                masked(0, 1)
                states(0)
                keys_decayed(1)
                masked(1, 0)
                masked(1, 1)
                queries_decayed(1)
                states(1)
                gated(0, 0)
                gated(0, 1)
                variances(0)
                gated(1, 0)
                normalised(0, 0)
                gated(1, 1)
                normalised(0, 1)
                directions(0)
                variances(1)
                rest_of_sum(0)

                dve.wait_ge(c_done, NC * L + C_USE["sctx"] + 1)
                chain.link(dve.reduce_max(mxc[:, :], PC[:, 0:1024].rearrange("p (h n) -> p h n", h=HEADS), AX.X))
                dve.scalar_tensor_tensor(nbc[:, :].rearrange("p (e t) -> p e t", e=2), mxc[:, :].rearrange("p (e t) -> p e t", e=2),
                                         -1.0, q_rs[:, :, 0, :].rearrange("p t e -> p e t"), ALU.mult, ALU.mult).then_inc(nbc_ok, 1)
                normalised(1, 0)
                normalised(1, 1)
                directions(1)
                dve.wait_ge(expc_ok, L + 1)
                dve.sem_inc(c_free, 1)
                chain.link(dve.reciprocal(ric[:, :], rsc[:, :]))
                by_head = probs_c[:, 0:HEADS * P].rearrange("p (h n) -> p h n", h=HEADS)
                dve.tensor_tensor(by_head, by_head, ric[:, :].rearrange("p (h o) -> p h o", o=1).to_broadcast([P, HEADS, P]),
                                  ALU.mult).then_inc(scaled_c, 1)
                rest_of_sum(1)
                dve.wait_ge(tc_ps, L + 1)
                dve.tensor_copy(probs_t[:, 0:2, :].rearrange("p b n -> p (b n)"), PA).then_inc(ptc_ok, 1)
                dve.wait_ge(oc_hi, L + 1)
                dve.tensor_tensor(act_lo[:, 0:4, 0:CTX], PB_[:, 0:512].rearrange("p (t n) -> p t n", t=4),
                                  act_hi[:, 0:4, 0:CTX].bitcast(F32), ALU.subtract).then_inc(oc_ok, 1)

                with dve.Fori(0, 2) as i:
                    chain.clear()

                    def rest(q):
                        dve.wait_ge(qhi_ok, 8 * L + 4 * i + q + 1)
                        dve.tensor_tensor(q_lo[:, q % 2, :], q2[0:HD, :], qq[0:HD, q % 2, :].bitcast(F32),
                                          ALU.subtract).then_inc(qpack, 1)

                    def maximum(q, b):
                        dve.wait_ge(s_done, 32 * L + 16 * i + 4 * q + b + 9)
                        at = 4 * (q % 2) + b
                        chain.link(dve.reduce_max(mx[:, at:at + 1], pair[2 + b % 2][:, 0:KEYS], AX.X))
                        dve.scalar_tensor_tensor(nb[:, at:at + 1], mx[:, at:at + 1], -1.0,
                                                 q_rs[:, i + 2 * (q // 2), 1 + b, q % 2:q % 2 + 1], ALU.mult, ALU.mult).then_inc(nb_ok, 1)

                    def inverse(q, b):
                        at = 4 * (q % 2) + b
                        dve.wait_ge(exp_ok, 32 * L + 16 * i + 4 * q + b + 3)
                        ins = dve.reciprocal(rinv[:, at:at + 1], rsum[:, at:at + 1])
                        if b % 2 == 0:
                            ins.then_inc(ri_ok, 1)
                        else:
                            chain.link(ins)
                            dve.tensor_scalar(probs[:, q % 2, b, :], probs[:, q % 2, b, :], rinv[:, at:at + 1], None,
                                              ALU.mult).then_inc(scaled, 1)

                    def turned(q, t):
                        n = 6 * q + t
                        dve.wait_ge(t_done, 48 * L + 24 * i + n + 13)
                        wait_slot_t(dve, L, i, q, t)
                        dve.tensor_copy(probs_t[:, slot_t(q, t), :], psum[:, 2 * (n % 2), :]).then_inc(pt_ok, 1)

                    def output(p):
                        dve.wait_ge(o_hi, 4 * L + 2 * i + p + 1)
                        t = i + 2 * p
                        dve.tensor_tensor(act_lo[:, t, CTX:TOK], psum[:, 2 * p + 1, :],
                                          act_hi[:, t, CTX:TOK].bitcast(F32), ALU.subtract).then_inc(o_ok, 1)

                    rest(0)
                    maximum(0, 0)
                    maximum(0, 1)
                    inverse(0, 0)
                    maximum(0, 2)
                    inverse(0, 1)
                    rest(1)
                    maximum(0, 3)
                    inverse(0, 2)
                    inverse(0, 3)
                    for q in range(4):
                        if q < 3:
                            maximum(q + 1, 0)
                            maximum(q + 1, 1)
                            inverse(q + 1, 0)
                        turned(q, 0)
                        if q < 3:
                            maximum(q + 1, 2)
                            inverse(q + 1, 1)
                            maximum(q + 1, 3)
                        turned(q, 2)
                        if q < 2:
                            rest(q + 2)
                        if q < 3:
                            inverse(q + 1, 2)
                        turned(q, 4)
                        if q < 3:
                            inverse(q + 1, 3)
                        if q == 2:
                            output(0)
                    output(1)

                chain.clear()
                dve.memset(sq_acc[:, :], 0.0)
                for t in range(2):
                    for at in (0, CTX + 1, GAP - 1):
                        ins = dve.memset(u_sb[:, t, at:at + 1], 0.0)
                chain.link(ins)

                def square_units(first, gains, at, last=False):
                    def two(i):
                        static = isinstance(i, int)
                        for s in range(2):
                            if not (last and i == 1 and s == 1):
                                split(L, first + s + 1 + (2 * i if static else 0), None if static else i)
                            for t in range(2):
                                m = 4 * i + 2 * s + t
                                dve.wait_ge(job_done, JOBS * L + 2 * (first + s) + t + 3 + 4 * i)
                                for lo, hi, src in ((0, CTX, pair[t][:, 0:CTX]), (CTX, TH, pair[t][:, CTX:TH]),
                                                    (TH, TOK, pair[t][:, 512:512 + TH])):
                                    g = 0 if lo == 0 else 1
                                    ins = dve.scalar_tensor_tensor(x[:, m, lo:hi], src, mod[:, gains + m, g:g + 1],
                                                                   x[:, m, lo:hi], ALU.mult, ALU.add)
                                tell(ins, a_free if t == 0 else b_free, *([x_new] if at is not None else []))
                                if at is not None:
                                    add_squares(L, m, t, at)
                    if last:
                        two(0)
                        two(1)
                    else:
                        with dve.Fori(0, 2) as i:
                            chain.clear()
                            two(i)
                    chain.clear()

                square_units(U_OUT, 16, KD)
                norm_powers(L, "2")
                norm(L, "2", KD)

                first = 0
                for v, n, up, down in zip(range(3), CHUNKS, U_UP, U_DOWN):
                    with dve.Fori(0, n // 2) as i:
                        chain.clear()
                        for s in range(2):
                            split(L, up + s + 1, i)
                            j = first + s
                            for t in range(2):
                                dve.wait_ge(u_ok, 2 * NJ * L + 4 * i + 2 * j + t + 1)
                                if t == 0:
                                    dve.wait_ge(sg_ok, NJ * L + 2 * i + j + 1)
                                tile = 2 * i + j + 22 * t
                                c1 = slice(1, 2 + TOK)
                                chain.link(dve.tensor_scalar(cv[:, t, c1], u_sb[:, t, c1], conv_l[:, 1, bass.ds(tile, 1)],
                                                             conv_l[:, 3, bass.ds(tile, 1)], ALU.mult, ALU.add))
                                chain.link(dve.scalar_tensor_tensor(cv[:, t, c1], u_sb[:, t, 0:1 + TOK], conv_l[:, 0, bass.ds(tile, 1)],
                                                                    cv[:, t, c1], ALU.mult, ALU.add))
                                tell(dve.scalar_tensor_tensor(cv[:, t, c1], u_sb[:, t, 2:3 + TOK], conv_l[:, 2, bass.ds(tile, 1)],
                                                              cv[:, t, c1], ALU.mult, ALU.add), cv_ok)
                            dve.wait_ge(sg_ok, NJ * L + 2 * i + j + 2)
                            dve.tensor_tensor(gf[:, 0:CTX], sg[:, 1:1 + CTX], cv[:, 1, 1:1 + CTX], ALU.mult)
                            dve.tensor_tensor(gf[:, CTX:TOK], sg[:, 2 + CTX:2 + TOK], cv[:, 1, 2 + CTX:2 + TOK], ALU.mult).then_inc(gf_ok, 1)
                            dve.wait_ge(g_hi_ok, NJ * L + 2 * i + j + 1)
                            dve.tensor_tensor(g_lo[:, 2 * i + s, :], gf[:, :], g_hi[:, 2 * i + s, :].bitcast(F32),
                                              ALU.subtract).then_inc(g_ok, 1)
                    first += n
                    chain.clear()
                    if first == NJ:
                        chain.link(dve.memset(sq_acc[:, :], 0.0))
                    square_units(down, 40, 2 * KD if first == NJ else None, last=first == NJ)
                    if v < 2:
                        with dve.If(L < 1):
                            dve.wait_ge(next_turned, v + 3)
                            add_bias(mod_next[:, KD * v:KD * v + KD, :],
                                     prm[:, C_BMOD + 48 + KD * v:C_BMOD + 48 + KD * v + KD]).then_inc(next_ok, 1)

            chain.clear()
            dve.wait_ge(c_done, NC * DEPTH + 1)
            tell(dve.tensor_scalar(vsum[:, 0:NT], PC[:, 768:768 + NT], EPS, None, ALU.add), v_ok)
            dve.wait_ge(c_done, NC * DEPTH + 2)
            for k in range(KD + 1):
                if k < KD:
                    if k >= 2:
                        dve.wait_ge(y_row, k - 1)
                    dve.scalar_tensor_tensor(y_t[:, k % 2, :], x[:, k, :], prm[:, R_FIN + k:R_FIN + k + 1], PC[:, 0:TOK],
                                             ALU.mult, ALU.mult).then_inc(y_col, 1)
                if k >= 1:
                    dve.wait_ge(y_row, k)
                    dve.tensor_copy(rows[:, :, P * (k - 1):P * k], pair[(k - 1) % 2][:, 0:TOK].rearrange("p (t n) -> p t n", t=NT))\
                       .then_inc(y_rows, 1)

        @block.gpsimd
        def _(pool):
            pool.memset(half[:, :], -0.5).then_inc(pool_chain, 1)
            pool.wait_ge(pool_chain, 1)
            with pool.Fori(0, DEPTH) as L:
                for name, n in RS_USE.items():
                    if name == "n2":
                        with pool.Fori(0, 2) as i:
                            for q in range(4):
                                if q == 0:
                                    pool.wait_ge(rs_ok, NRS * L + RS_USE["r1"] + 1)
                                pool.wait_ge(qpack, 8 * L + 4 * i + q + 1)
                                pool.sem_inc(q2_turn, 1)
                                e, t = q % 2, i + 2 * (q // 2)
                                for half_ in range(2):
                                    ins = pool.tensor_copy(q2[HD * half_:HD * half_ + HD, :], qT[HD * e:HD * e + HD, t, CTX:TOK])
                                ins.then_inc(q2_ok, 1)
                    pool.wait_ge(v_ok, NRS * L + n + 1)
                    w = {"n": NT, "r": 4 * NT}.get(name[0], 2 * NT)
                    if name[0] == "q":
                        dst = q_rs[:, int(name[1]), :, :].rearrange("p t e -> p (t e)")
                    else:
                        dst = rstd[:, 0:w]
                    pool.tensor_tensor(dst, vsum[:, 0:w], half[:, 0:w], ALU.pow).then_inc(rs_ok, 1)
                with pool.If(L < 1):
                    for n in range(4):
                        if n == 0:
                            pool.wait_ge(h_ok, 2 * KD)
                        else:
                            pool.wait_ge(next_used, n)
                        for k in range(4):
                            at = 4 * (n % 2) + k
                            pool.dma_start(m_next[:, k, :], w_mod_v[1, :, at, D * (n // 2):D * (n // 2) + D]).then_inc(next_in, 16)
            pool.wait_ge(v_ok, NRS * DEPTH + 1)
            pool.tensor_tensor(rstd[:, 0:NT], vsum[:, 0:NT], half[:, 0:NT], ALU.pow).then_inc(rs_ok, 1)


def constants(np):
    f32 = np.float32
    out = np.zeros((P, NCONST), np.float64)

    def put(name, v):
        a, b = CONST[name]
        out[:, a:b] = v

    i = np.arange(P)
    put("ident", np.eye(P))
    put("ones", np.full((P, 1), 1.0 / D))
    put("blk", (i[:, None] // HD == np.arange(2)[None]) / HD)
    same = (i[:, None] // HD == i[None] // HD)
    put("center", np.eye(P) - same / HD)
    rot = np.zeros((P, P))
    for m in range(P):
        base, r = m // 32 * 32, m % 32
        if r < 16:
            rot[base + r + 16, m] = -1.0
        else:
            rot[base + r - 16, m] = 1.0
    put("rot", rot)
    ang = 2 * np.pi * (np.outer(i % HD, i % HD) % HD) / HD
    for name, n in (("l", LAT), ("c", CTX)):
        put("c64" + name, same * np.cos(ang) / np.sqrt(n * HD))
        put("s64" + name, same * -np.sin(ang) / np.sqrt(n * HD))
    tok = np.arange(LAT)
    freqs = (f32(10000.0) ** (-np.arange(16, dtype=f32) / f32(16))).astype(f32)
    pos = np.stack([(tok // 64).astype(f32), (tok % 64).astype(f32)])
    d = i % HD
    a = (pos[d // 32] * freqs[d % 16][:, None]).astype(f32).astype(np.float64)
    put("cos", np.cos(a))
    put("sin", np.sin(a))
    j, q = i[:, None], i[None]
    for r, (w, base) in enumerate((("f", 5.0), ("b", 5.5))):
        lg = np.log1p(-np.exp2(-(f32(base) + np.arange(4, dtype=f32)))).astype(f32).astype(np.float64)
        dist = (q - j) if r == 0 else (j - q)
        put("mask" + w, np.concatenate([np.where(dist >= 0, np.exp(np.maximum(dist, 0) * lg[h]), 0.0) for h in range(4)], 1))
        place = i if r == 0 else P - 1 - i
        put("qd" + w, np.concatenate([np.exp((place + 1.0)[None] * lg[2 * t + i // HD][:, None]) for t in range(2)], 1))
        put("kd" + w, np.exp((P - 1.0 - place)[:, None] * lg[np.arange(256) // HD][None]))
        for t in range(2):
            out[:, CONST["gam"][0] + 2 * r + t] = np.exp(P * lg[2 * t + i // HD])
    dft = np.zeros((P, 256 + 4096), np.float64)
    a = 2 * np.pi * (np.outer(i, i) % CTX) / CTX
    dft[:, 0:128], dft[:, 128:256] = np.cos(a), np.sin(a)
    a = 2 * np.pi * (np.outer(tok, tok) % LAT) / LAT
    for n, v in enumerate((np.cos(a), np.sin(a))):
        dft[:, 256 + 2048 * n:256 + 2048 * (n + 1)] = v.reshape(4, P, LAT).transpose(1, 0, 2).reshape(P, 2048)
    return out.astype(f32), dft.astype(f32)


_INS = ["x_prompt", "x_sample", "c", "cache_attn_k", "cache_attn_v", "state_ret", "c_ctx", "w_mod", "b_mod", "norm1_w",
        "w_in", "q_norm_w", "k_norm_w", "w_out", "norm2_w", "w_up", "conv_w", "conv_b", "w_down", "final_norm_w"]
_OUTS = [(1, CTX, D), (1, LAT, D), (1, DEPTH, CTX, 2, HD), (1, DEPTH, CTX, 2, HD), (1, DEPTH, 2, 4, HD, HD)]


def kernel(**inputs):
    import numpy as _np
    import concourse.bacc as _bacc
    from concourse import mybir as _mybir
    from concourse.bass_utils import run_bass_kernel_spmd as _run

    nc = _bacc.Bacc("TRN2", target_bir_lowering=False, num_devices=1)
    arrays, args = {}, []
    const, dft = constants(_np)
    for name, a in [(n, inputs[n]) for n in _INS] + [("const", const), ("dft", dft)]:
        a = _np.ascontiguousarray(a)
        arrays[f"in_{name}_dram"] = a
        args.append(nc.dram_tensor(f"in_{name}_dram", a.shape, _mybir.dt.from_np(a.dtype), kind="ExternalInput").ap())
    for i, shape in enumerate(_OUTS):
        args.append(nc.dram_tensor(f"out_{i}_dram", shape, _mybir.dt.float32, kind="ExternalOutput").ap())
    program(nc, *args)
    r = _run(nc, [arrays], core_ids=[0])
    return tuple(r.results[0][f"out_{i}_dram"] for i in range(len(_OUTS)))
```
